# Optimizing a Trainium2 kernel written in Bass

```python
import jax, jax.numpy as jnp
from jax import lax
import numpy as np

D_MODEL = 1024
BATCH = 1
SEQ = 1024
DEPTH = 2

GRID_W = 64
CTX_LEN = 256
N_MIXERS = 3
Q_BLOCK = 128
ROPE_THETA = 10000.0
NORM_EPS = 1e-6

GQA_HEAD_DIM = 128
GQA_HEADS = D_MODEL // GQA_HEAD_DIM
GQA_KV_HEADS = GQA_HEADS // 4
GQA_GROUP = GQA_HEADS // GQA_KV_HEADS
GQA_WIDTH = GQA_HEADS * GQA_HEAD_DIM
GQA_KV_WIDTH = GQA_KV_HEADS * GQA_HEAD_DIM
GQA_PROJ = 2 * GQA_WIDTH + 2 * GQA_KV_WIDTH

NA_HEAD_DIM = 64
NA_HEADS = D_MODEL // NA_HEAD_DIM
NA_WIDTH = NA_HEADS * NA_HEAD_DIM
NA_KH = 8
NA_KW = 16
NA_PROJ = 4 * NA_WIDTH

MLA_HEADS = 8
MLA_Q_LORA = 512
MLA_KV_LORA = 256
MLA_NOPE = 128
MLA_ROPE = 64
MLA_V = 128
MLA_WIDTH = MLA_HEADS * MLA_V
MLA_PROJ = MLA_Q_LORA + MLA_KV_LORA + MLA_ROPE + MLA_WIDTH

kernel_name = 'hybrid_gqa_natten_mla_prefix_dit'

def rms_norm(x, g):
    xf = x.astype(jnp.float32)
    y = xf * lax.rsqrt(jnp.mean(xf * xf, axis=-1, keepdims=True) + NORM_EPS)
    return (y * g.astype(jnp.float32)).astype(x.dtype)

def axial_rope_tables(n_tok, rot_dim):
    n_freq = rot_dim // 4
    inv = ROPE_THETA ** (-jnp.arange(n_freq, dtype=jnp.float32) / n_freq)
    t = jnp.arange(n_tok)
    row = (t // GRID_W).astype(jnp.float32)
    col = (t % GRID_W).astype(jnp.float32)
    ang_r = row[:, None] * inv
    ang_c = col[:, None] * inv
    ang = jnp.concatenate([ang_r, ang_r, ang_c, ang_c], axis=-1)
    return jnp.cos(ang), jnp.sin(ang)

def apply_axial_rope(x, cos, sin):
    n_freq = x.shape[-1] // 4
    bshape = (cos.shape[0],) + (1,) * (x.ndim - 3) + (cos.shape[1],)
    xs = x.reshape(x.shape[:-1] + (2, 2, n_freq))
    rot = jnp.concatenate([-xs[..., 1:2, :], xs[..., 0:1, :]], axis=-2).reshape(x.shape)
    return x * cos.reshape(bshape).astype(x.dtype) + rot * sin.reshape(bshape).astype(x.dtype)

def blocked_attention(q, k, v, scale):
    b, n_q = q.shape[:2]
    nb = n_q // Q_BLOCK
    qb = jnp.moveaxis(q.reshape((b, nb, Q_BLOCK) + q.shape[2:]), 1, 0)

    def one_block(q_blk):
        s = jnp.einsum('bqkgd,bnkd->bkgqn', q_blk, k, preferred_element_type=jnp.float32) * scale
        p = jax.nn.softmax(s, axis=-1).astype(v.dtype)
        return jnp.einsum('bkgqn,bnkd->bqkgd', p, v)

    o = lax.map(one_block, qb)
    return jnp.moveaxis(o, 0, 1).reshape((b, n_q) + o.shape[3:])

def gqa_axial_mixer(h_lat, h_ctx, w_in, q_g, k_g, w_out, cos, sin, need_ctx):
    def project(h):
        b, n = h.shape[:2]
        q, k, v, g = jnp.split(h @ w_in, [GQA_WIDTH, GQA_WIDTH + GQA_KV_WIDTH, GQA_WIDTH + 2 * GQA_KV_WIDTH], axis=-1)
        q = rms_norm(q.reshape(b, n, GQA_KV_HEADS, GQA_GROUP, GQA_HEAD_DIM), q_g)
        k = rms_norm(k.reshape(b, n, GQA_KV_HEADS, GQA_HEAD_DIM), k_g)
        v = v.reshape(b, n, GQA_KV_HEADS, GQA_HEAD_DIM)
        return q, k, v, g

    q_l, k_l, v_l, g_l = project(h_lat)
    q_c, k_c, v_c, g_c = project(h_ctx)
    q_l = apply_axial_rope(q_l, cos, sin)
    k_l = apply_axial_rope(k_l, cos, sin)
    scale = GQA_HEAD_DIM ** -0.5
    o_l = blocked_attention(q_l, jnp.concatenate([k_c, k_l], axis=1), jnp.concatenate([v_c, v_l], axis=1), scale)
    y_l = (o_l.reshape(h_lat.shape[:2] + (GQA_WIDTH,)) * jax.nn.silu(g_l)) @ w_out
    if not need_ctx:
        return y_l, None
    o_c = blocked_attention(q_c, k_c, v_c, scale)
    y_c = (o_c.reshape(h_ctx.shape[:2] + (GQA_WIDTH,)) * jax.nn.silu(g_c)) @ w_out
    return y_l, y_c

def neighbourhood_mixer(h_lat, h_ctx, w_in, rpb, w_out, need_ctx):
    b, n = h_lat.shape[:2]
    rows = n // GRID_W
    kh = min(NA_KH, rows)
    kw = NA_KW

    def project(h):
        q, k, v, g = jnp.split(h @ w_in, [NA_WIDTH, 2 * NA_WIDTH, 3 * NA_WIDTH], axis=-1)
        sh = h.shape[:2] + (NA_HEADS, NA_HEAD_DIM)
        return q.reshape(sh), k.reshape(sh), v.reshape(sh), g

    q_l, k_l, v_l, g_l = project(h_lat)
    q_c, k_c, v_c, g_c = project(h_ctx)
    grid = (b, rows, GRID_W, NA_HEADS, NA_HEAD_DIM)
    qg, kg, vg = q_l.reshape(grid), k_l.reshape(grid), v_l.reshape(grid)
    scale = NA_HEAD_DIM ** -0.5
    row_start = jnp.clip(jnp.arange(rows) - kh // 2, 0, rows - kh)
    col_idx = jnp.clip(jnp.arange(GRID_W) - kw // 2, 0, GRID_W - kw)[:, None] + jnp.arange(kw)
    col_off = col_idx - jnp.arange(GRID_W)[:, None] + (NA_KW - 1)

    def row_block(r):
        rs = row_start[r]
        q_r = lax.dynamic_index_in_dim(qg, r, axis=1, keepdims=False)
        k_win = lax.dynamic_slice_in_dim(kg, rs, kh, axis=1)[:, :, col_idx]
        v_win = lax.dynamic_slice_in_dim(vg, rs, kh, axis=1)[:, :, col_idx]
        row_off = rs + jnp.arange(kh) - r + (NA_KH - 1)
        bias = rpb[:, row_off[None, :, None], col_off[:, None, :]]
        s_loc = jnp.einsum('bqhd,biqjhd->bhqij', q_r, k_win, preferred_element_type=jnp.float32) * scale + bias
        s_ctx = jnp.einsum('bqhd,bchd->bhqc', q_r, k_c, preferred_element_type=jnp.float32) * scale
        s = jnp.concatenate([s_loc.reshape(b, NA_HEADS, GRID_W, kh * kw), s_ctx], axis=-1)
        p = jax.nn.softmax(s, axis=-1).astype(v_l.dtype)
        p_loc = p[..., :kh * kw].reshape(b, NA_HEADS, GRID_W, kh, kw)
        p_ctx = p[..., kh * kw:]
        return jnp.einsum('bhqij,biqjhd->bqhd', p_loc, v_win) + jnp.einsum('bhqc,bchd->bqhd', p_ctx, v_c)

    o = lax.map(row_block, jnp.arange(rows))
    o = jnp.moveaxis(o, 0, 1).reshape(b, n, NA_WIDTH)
    y_l = (o * jax.nn.silu(g_l)) @ w_out
    if not need_ctx:
        return y_l, None
    o_c = blocked_attention(q_c[:, :, :, None, :], k_c, v_c, scale)
    y_c = (o_c.reshape(h_ctx.shape[:2] + (NA_WIDTH,)) * jax.nn.silu(g_c)) @ w_out
    return y_l, y_c

def mla_mixer(h_lat, h_ctx, w_in, q_g, kv_g, w_uq, w_ukv, w_out, cos, sin, need_ctx):
    def project(h, use_rope):
        b, n = h.shape[:2]
        c_q, c_kv, k_r, g = jnp.split(h @ w_in, [MLA_Q_LORA, MLA_Q_LORA + MLA_KV_LORA, MLA_Q_LORA + MLA_KV_LORA + MLA_ROPE], axis=-1)
        q = (rms_norm(c_q, q_g) @ w_uq).reshape(b, n, MLA_HEADS, MLA_NOPE + MLA_ROPE)
        kv = (rms_norm(c_kv, kv_g) @ w_ukv).reshape(b, n, MLA_HEADS, MLA_NOPE + MLA_V)
        q_nope, q_rope = q[..., :MLA_NOPE], q[..., MLA_NOPE:]
        k_nope, v = kv[..., :MLA_NOPE], kv[..., MLA_NOPE:]
        k_r = k_r[:, :, None, :]
        if use_rope:
            q_rope = apply_axial_rope(q_rope, cos, sin)
            k_r = apply_axial_rope(k_r, cos, sin)
        q = jnp.concatenate([q_nope, q_rope], axis=-1)
        k = jnp.concatenate([k_nope, jnp.broadcast_to(k_r, (b, n, MLA_HEADS, MLA_ROPE))], axis=-1)
        return q, k, v, g

    q_l, k_l, v_l, g_l = project(h_lat, True)
    q_c, k_c, v_c, g_c = project(h_ctx, False)
    scale = (MLA_NOPE + MLA_ROPE) ** -0.5
    o_l = blocked_attention(q_l[:, :, :, None, :], jnp.concatenate([k_c, k_l], axis=1), jnp.concatenate([v_c, v_l], axis=1), scale)
    y_l = (o_l.reshape(h_lat.shape[:2] + (MLA_WIDTH,)) * jax.nn.silu(g_l)) @ w_out
    if not need_ctx:
        return y_l, None
    o_c = blocked_attention(q_c[:, :, :, None, :], k_c, v_c, scale)
    y_c = (o_c.reshape(h_ctx.shape[:2] + (MLA_WIDTH,)) * jax.nn.silu(g_c)) @ w_out
    return y_l, y_c

def setup_inputs(seed: int = 0) -> dict:
    key = jax.random.key(seed)
    ks = jax.random.split(key, 24)
    f32 = jnp.float32
    D = D_MODEL
    n_a = len(range(0, DEPTH, N_MIXERS))
    n_b = len(range(1, DEPTH, N_MIXERS))
    n_c = len(range(2, DEPTH, N_MIXERS))

    def dense(k, shape):
        return jax.random.normal(k, shape, f32) * shape[-2] ** -0.5

    def gain(k, shape):
        return 1.0 + 0.05 * jax.random.normal(k, shape, f32)

    return {
        'x': jax.random.normal(ks[0], (BATCH, SEQ, D), f32),
        'c': jax.random.normal(ks[1], (BATCH, D), f32),
        'ctx': jax.random.normal(ks[2], (BATCH, CTX_LEN, D), f32),
        'c_ctx': jax.random.normal(ks[3], (D,), f32),
        'mod_w': 0.5 * dense(ks[4], (DEPTH, D, 3 * D)),
        'mod_b': 0.01 * jax.random.normal(ks[5], (DEPTH, 3 * D), f32),
        'norm_g': gain(ks[6], (DEPTH, D)),
        'final_g': gain(ks[7], (D,)),
        'ga_w_in': dense(ks[8], (n_a, D, GQA_PROJ)),
        'ga_q_g': gain(ks[9], (n_a, GQA_HEAD_DIM)),
        'ga_k_g': gain(ks[10], (n_a, GQA_HEAD_DIM)),
        'ga_w_out': dense(ks[11], (n_a, GQA_WIDTH, D)),
        'na_w_in': dense(ks[12], (n_b, D, NA_PROJ)),
        'na_rpb': 0.1 * jax.random.normal(ks[13], (n_b, NA_HEADS, 2 * NA_KH - 1, 2 * NA_KW - 1), f32),
        'na_w_out': dense(ks[14], (n_b, NA_WIDTH, D)),
        'mla_w_in': dense(ks[15], (n_c, D, MLA_PROJ)),
        'mla_q_g': gain(ks[16], (n_c, MLA_Q_LORA)),
        'mla_kv_g': gain(ks[17], (n_c, MLA_KV_LORA)),
        'mla_w_uq': dense(ks[18], (n_c, MLA_Q_LORA, MLA_HEADS * (MLA_NOPE + MLA_ROPE))),
        'mla_w_ukv': dense(ks[19], (n_c, MLA_KV_LORA, MLA_HEADS * (MLA_NOPE + MLA_V))),
        'mla_w_out': dense(ks[20], (n_c, MLA_WIDTH, D)),
    }

def reference(x, c, ctx, c_ctx, mod_w, mod_b, norm_g, final_g,
              ga_w_in, ga_q_g, ga_k_g, ga_w_out,
              na_w_in, na_rpb, na_w_out,
              mla_w_in, mla_q_g, mla_kv_g, mla_w_uq, mla_w_ukv, mla_w_out):
    n_lat = x.shape[1]
    cos_a, sin_a = axial_rope_tables(n_lat, GQA_HEAD_DIM)
    cos_m, sin_m = axial_rope_tables(n_lat, MLA_ROPE)
    xc = ctx
    for i in range(DEPTH):
        kind, j = i % N_MIXERS, i // N_MIXERS
        need_ctx = i < DEPTH - 1
        shift, scale, gate = jnp.split(jax.nn.silu(c) @ mod_w[i] + mod_b[i], 3, axis=-1)
        shift_c, scale_c, gate_c = jnp.split(jax.nn.silu(c_ctx) @ mod_w[i] + mod_b[i], 3, axis=-1)
        h = rms_norm(x, norm_g[i]) * (1.0 + scale[:, None]) + shift[:, None]
        hc = rms_norm(xc, norm_g[i]) * (1.0 + scale_c) + shift_c
        if kind == 0:
            y, yc = gqa_axial_mixer(h, hc, ga_w_in[j], ga_q_g[j], ga_k_g[j], ga_w_out[j], cos_a, sin_a, need_ctx)
        elif kind == 1:
            y, yc = neighbourhood_mixer(h, hc, na_w_in[j], na_rpb[j], na_w_out[j], need_ctx)
        else:
            y, yc = mla_mixer(h, hc, mla_w_in[j], mla_q_g[j], mla_kv_g[j], mla_w_uq[j], mla_w_ukv[j], mla_w_out[j], cos_m, sin_m, need_ctx)
        x = x + gate[:, None] * y
        if need_ctx:
            xc = xc + gate_c * yc
    return rms_norm(x, final_g)


_drawn_inputs = setup_inputs


def setup_inputs(seed=0):
    import zlib

    import numpy as np

    out = dict(_drawn_inputs(seed))
    spreads = {}
    factors = {'ctx': 3.382, 'mod_b': 8.0, 'norm_g': 8.0, 'ga_q_g': 8.0, 'ga_k_g': 8.0, 'na_rpb': 8.0}
    for name, (base, spread) in spreads.items():
        noise = np.random.default_rng([zlib.crc32(name.encode()), seed]).standard_normal(out[name].shape)
        drawn = base * np.exp(spread * noise) if base else spread * noise
        out[name] = __import__('jax').numpy.asarray(drawn.astype(out[name].dtype))
    for name, factor in factors.items():
        out[name] = (out[name] * factor).astype(out[name].dtype)
    return out
```

```python
from contextlib import ExitStack, contextmanager

import numpy as np

import concourse.bass as bass
from concourse import mybir

ALU = mybir.AluOpType
ACT = mybir.ActivationFunctionType
F32 = mybir.dt.float32
F32R = mybir.dt.float32r
AX = mybir.AxisListType.X

P = 128
D = 1024
KT = D // P
NCTX, NLAT = 256, 1024
T = NCTX + NLAT
TT = T // P
CT = NCTX // P
GRID_W = 64
EPS = 1e-6
THETA = 10000.0

HD = 128
QH, KVH = 8, 2
GROUP = QH // KVH
NH, ND = 16, 64
KH, KW = 8, 16
ROWS = NLAT // GRID_W
MASKED = -1e30
BIAS_ROWS, BIAS_W = 2 * KH - 1, 2 * GRID_W - 1
SKEW_W = BIAS_W + GRID_W - 1
END_SLOTS = range(1, 15)
MID_SLOTS = range(3, 12)

ALL_CHUNKS = [(0, NCTX), (NCTX, 512), (NCTX + 512, 512)]
LAT_CHUNKS = [(NCTX, 512), (NCTX + 512, 512)]


def rope_tables():
    nf = HD // 4
    inv = (np.float32(THETA) ** (-np.arange(nf, dtype=np.float32) / np.float32(nf))).astype(np.float32)
    t = np.arange(NLAT)
    row, col = (t // GRID_W).astype(np.float32), (t % GRID_W).astype(np.float32)
    ar, ac = row[:, None] * inv, col[:, None] * inv
    ang = np.concatenate([ar, ar, ac, ac], axis=-1).T
    cos, sin = np.ones((HD, T), np.float32), np.zeros((HD, T), np.float32)
    sign = np.where((np.arange(HD) // nf) % 2 == 0, -1.0, 1.0).astype(np.float32)[:, None]
    cos[:, NCTX:], sin[:, NCTX:] = np.cos(ang), np.sin(ang) * sign
    return cos, sin


def window_masks():
    q = np.arange(P) % GRID_W
    start = np.clip(q - KW // 2, 0, GRID_W - KW)[:, None]
    k = np.arange(GRID_W)[None]
    cols = np.where((k >= start) & (k < start + KW), 0.0, MASKED).astype(np.float32)
    mid = np.repeat(cols[:, None], len(MID_SLOTS), axis=1)
    mid[P // 2:, 0] = MASKED
    mid[:P // 2, -1] = MASKED
    return cols, mid


AREA_H = (0, 80)
AREA_X = (80, 120)
AREA_MID = (120, 160)
AREA_W = (160, 199)
AREA_QKV = (80, 170)
AREA_STAGE = (184, 199)
AREA_CONST = (199, 207)


class Core:

    BASE = 17 * 1024

    def __init__(self, nc, stack):
        self.nc, self.stack, self.top = nc, stack, stack
        self.free = []
        self.sems, self.old_sems = [], []

    def sb(self, name, shape, dt=F32):
        size = int(np.prod(shape[1:])) * 4
        size = (size + 63) // 64 * 64
        for r in self.free:
            if r[0] + size <= r[1]:
                at = r[0]
                r[0] += size
                return self.nc.alloc_sbuf_tensor_at(name, shape, dt, offset=at)
        raise ValueError(f"{name}: {size} bytes in {self.free}")

    def ps(self, name, shape):
        return self.stack.enter_context(self.nc.psum_tensor(name, shape, F32))

    def sem(self, name):
        self.sems.append(self.nc.alloc_semaphore(name=name))
        return self.sems[-1]

    @contextmanager
    def block(self):
        with self.nc.Block() as block:
            old = self.old_sems

            @block.gpsimd
            def _(pool):
                for sem in old:
                    pool.sem_clear(sem)
            yield block
        for sem in old:
            self.nc.release_semaphore(sem)
        self.old_sems, self.sems = self.sems, []

    @contextmanager
    def scope(self, *ranges):
        keep = self.stack, self.free
        self.free = [[self.BASE + int(a * 1024), self.BASE + int(b * 1024)] for a, b in ranges]
        with ExitStack() as inner:
            self.stack = inner
            yield
        self.stack, self.free = keep



def load_and_modulate(c, io, consts, xt, mod, cols):
    nc = c.nc
    ident, ones = consts["ident"], consts["ones"]
    with c.scope(AREA_H, AREA_MID):
        xin = c.sb("xin", [P, TT, D])
        wmod = c.sb("wmod", [P, 3, 3 * D])
        vec = c.sb("vec_rows", [P, P])
        vec2 = c.sb("vec_rows2", [P, P])
        cs = c.sb("silu_cols", [P, 16])
        mrow = c.sb("mod_rows", [2, 2, 3 * D])
        tps = c.ps("tps", [P, 2, 512])
        mps = c.ps("mps", [P, 6, 512])
        cst, cst0 = c.sem("const_ready"), c.sem("const_zeroed")
        s_vec, s_x, s_w = c.sem("vec_loaded"), c.sem("x_loaded"), [c.sem(f"wmod_loaded{i}") for i in range(3)]
        silu, turned, taken, csd = c.sem("silu_done"), c.sem("turned"), c.sem("turn_taken"), c.sem("cs_done")
        mm, rows, colst, colsd = c.sem("mod_mm"), c.sem("mod_rows_done"), c.sem("mod_turned"), c.sem("mod_cols_done")
        msem, stored = c.sem("mod_step"), c.sem("xt_stored")
        vt, vd = c.sem("vec_turned"), c.sem("vec_taken")

        with c.block() as block:
            @block.gpsimd
            def _(pool):
                pool.memset(ones[:, :], 1.0).then_inc(cst, 1)
                pool.memset(ident[:, :], 0.0).then_inc(cst0, 1)
                pool.memset(consts["eps"][:, :], EPS).then_inc(cst, 1)
                pool.memset(consts["sel"][:, :], 0.0).then_inc(cst0, 1)
                pool.memset(consts["spread"][:, :, :], 1.0).then_inc(cst0, 1)
                pool.wait_ge(cst0, 3)
                pool.affine_select(out=ident[:, :], in_=ident[:, :], compare_op=ALU.not_equal, fill=1.0,
                                   base=0, pattern=[[-1, P]], channel_multiplier=1).then_inc(cst, 1)
                pool.memset(consts["sel"][:, QH + KVH - 1:QH + KVH], 1.0).then_inc(cst, 1)
                pool.affine_select(out=consts["spread"][:, :, :], in_=consts["spread"][:, :, :],
                                   compare_op=ALU.is_equal, fill=0.0, base=0,
                                   pattern=[[-1, QH + KVH], [0, P]], channel_multiplier=1).then_inc(cst, 1)

            @block.sync
            def _(sp):
                row = lambda a, n: a.rearrange("(r p) -> r p", p=P) if n else a
                sp.dma_start(vec[0:8, :], io["c"].rearrange("a (r p) -> (a r) p", p=P)).then_inc(s_vec, 16)
                sp.dma_start(vec[8:16, :], io["c_ctx"].rearrange("(r p) -> r p", p=P)).then_inc(s_vec, 16)
                sp.dma_start(vec2[0:48, :], io["mod_b"].rearrange("l (r p) -> (l r) p", p=P)).then_inc(s_vec, 16)
                sp.dma_start(vec2[48:64, :], io["norm_g"].rearrange("l (r p) -> (l r) p", p=P)).then_inc(s_vec, 16)
                sp.dma_start(vec2[64:65, :], io["ga_q_g"]).then_inc(s_vec, 16)
                sp.dma_start(vec2[65:66, :], io["ga_k_g"]).then_inc(s_vec, 16)
                for t in range(TT):
                    src = io["ctx"][0, t * P:(t + 1) * P] if t < CT else io["x"][0, (t - CT) * P:(t - CT + 1) * P]
                    sp.dma_start(xin[:, t, :], src).then_inc(s_x, 16)
                for n in range(2 * KT):
                    l, k = n // KT, n % KT
                    if n >= 3:
                        sp.wait_ge(mm, n - 2)
                    sp.dma_start(wmod[:, n % 3, :], io["mod_w"][l, k * P:(k + 1) * P, :]).then_inc(s_w[n % 3], 16)
                sp.wait_ge(taken, 2 * TT)
                sp.dma_start(io["xt"], xt[:, :, :]).then_inc(stored, 16)
                sp.wait_ge(stored, 16)

            @block.tensor
            def _(pe):
                pe.wait_ge(cst, 5)
                pe.wait_ge(silu, 1)
                pe.transpose(mps[:, 0, 0:16], vec[0:16, :], ident[0:16, 0:16]).then_inc(vt, 1)
                pe.transpose(mps[:, 1, 0:66], vec2[0:66, :], ident[0:66, 0:66]).then_inc(vt, 1)
                for t in range(TT):
                    pe.wait_ge(s_x, 16 * TT)
                    for b in range(2):
                        n = 2 * t + b
                        if n >= 2:
                            pe.wait_ge(taken, n - 1)
                        for k in range(4):
                            last = pe.transpose(tps[:, b, k * P:(k + 1) * P],
                                                xin[:, t, (4 * b + k) * P:(4 * b + k + 1) * P], ident[:, :])
                        last.then_inc(turned, 1)
                pe.wait_ge(csd, 2)
                for l in range(2):
                    for k in range(KT):
                        n = l * KT + k
                        pe.wait_ge(s_w[n % 3], 16 * (n // 3 + 1))
                        if l and k == 0:
                            pe.wait_ge(rows, 1)
                        for j in range(6):
                            last = pe.matmul(mps[0:2, j, :], cs[:, k:16:KT], wmod[:, n % 3, j * 512:(j + 1) * 512],
                                             start=(k == 0), stop=(k == KT - 1))
                        last.then_inc(mm, 1)
                    pe.wait_ge(rows, l + 1)
                    pe.wait_ge(taken, 2 * TT)
                    if l:
                        pe.wait_ge(colsd, 1)
                    for j in range(24):
                        last = pe.transpose(tps[:, 0, 2 * j:2 * j + 2], mrow[:, l, j * P:(j + 1) * P],
                                            ident[0:2, 0:2])
                    last.then_inc(colst, 1)

            @block.scalar
            def _(act):
                act.wait_ge(s_vec, 16 * 6)
                act.activation(vec[0:16, :], vec[0:16, :], ACT.Silu).then_inc(silu, 1)
                for t in range(TT):
                    act.wait_ge(turned, 2 * t + 1)
                    if t:
                        act.wait_ge(taken, 2 * t)
                    act.copy(xt[:, 0:4, t * P:(t + 1) * P],
                             tps[:, 0, :].rearrange("p (k q) -> p k q", k=4)).then_inc(taken, 1)

            @block.vector
            def _(dve):
                dve.wait_ge(vt, 2)
                dve.tensor_copy(cs[:, :], mps[:, 0, 0:16]).then_inc(csd, 1)
                dve.tensor_copy(cols[:, :], mps[:, 1, 0:66]).then_inc(csd, 1)
                for t in range(TT):
                    dve.wait_ge(turned, 2 * t + 2)
                    dve.wait_ge(taken, 2 * t + 1)
                    dve.tensor_copy(xt[:, 4:8, t * P:(t + 1) * P],
                                    tps[:, 1, :].rearrange("p (k q) -> p k q", k=4)).then_inc(taken, 1)
                for l in range(2):
                    dve.wait_ge(mm, (l + 1) * KT)
                    dve.tensor_copy(mrow[:, l, :].rearrange("p (j n) -> p j n", j=6), mps[0:2, :, :]).then_inc(rows, 1)
                    dve.wait_ge(colst, l + 1)
                    dve.wait_ge(csd, 2)
                    dve.tensor_tensor(mod[:, l, :, :], tps[:, 0, 0:48].rearrange("p (j s) -> p j s", s=2),
                                      cols[:, 24 * l:24 * l + 24].unsqueeze(2).broadcast_to([P, 24, 2]),
                                      ALU.add).then_inc(colsd, 1)
                    dve.wait_ge(colsd, l + 1)
                    for s in range(2):
                        dve.scalar_tensor_tensor(out=mod[:, l, 8:16, s], in0=mod[:, l, 8:16, s], scalar=1.0,
                                                 in1=cols[:, 48 + 8 * l:56 + 8 * l], op0=ALU.add,
                                                 op1=ALU.mult).then_inc(msem, 1)



def normalise(c, io, consts, l, xt, hi, lo, mod, store):
    nc = c.nc
    parts = [(0, NCTX, 1), (NCTX, NLAT, 0)]
    with c.scope(AREA_MID):
        sq = c.sb(f"sq{l}", [P, 2, T])
        rb = c.sb(f"rb{l}", [P, T])
        t_ = c.sb(f"nt{l}", [P, 2, T])
        sps = c.ps(f"sps{l}", [P, 3, 512])
        sqd, summed, rooted, recd = (c.sem(f"{x}{l}") for x in ("sq_done", "summed", "rooted", "recip_done"))
        scaled, his, los, stored = (c.sem(f"{x}{l}") for x in ("scaled", "h_hi", "h_lo", "x_stored"))
        with c.block() as block:
            @block.sync
            def _(sp):
                if store:
                    sp.dma_start(io["xt"], xt[:, :, :]).then_inc(stored, 16)
                    sp.wait_ge(stored, 16)

            @block.scalar
            def _(act):
                for k in range(KT):
                    if k >= 2:
                        act.wait_ge(summed, k - 1)
                    act.activation(sq[:, k % 2, :], xt[:, k, :], ACT.Square).then_inc(sqd, 1)
                act.wait_ge(summed, KT)
                for j, (a, n) in enumerate(ALL_CHUNKS):
                    act.activation(rb[:, a:a + n], sps[:, j, 0:n], ACT.Sqrt, bias=consts["eps"][:, :],
                                   scale=1.0 / D).then_inc(rooted, 1)
                for k in range(KT):
                    for j, (a, n, s) in enumerate(parts):
                        act.wait_ge(scaled, 2 * k + j + 1)
                        act.activation(hi[:, k, a:a + n], t_[:, k % 2, a:a + n], ACT.Identity,
                                       bias=mod[:, l, k, s:s + 1]).then_inc(his, 1)

            @block.tensor
            def _(pe):
                for k in range(KT):
                    pe.wait_ge(sqd, k + 1)
                    for j, (a, n) in enumerate(ALL_CHUNKS):
                        last = pe.matmul(sps[:, j, 0:n], consts["ones"][:, :], sq[:, k % 2, a:a + n],
                                         start=(k == 0), stop=(k == KT - 1))
                    last.then_inc(summed, 1)

            @block.vector
            def _(dve):
                dve.wait_ge(rooted, 3)
                dve.reciprocal(rb[:, :], rb[:, :]).then_inc(recd, 1)
                dve.wait_ge(recd, 1)
                def low(k):
                    for j, (a, n, s) in enumerate(parts):
                        dve.wait_ge(his, 2 * k + j + 1)
                        dve.scalar_tensor_tensor(out=lo[:, k, a:a + n], in0=t_[:, k % 2, a:a + n],
                                                 scalar=mod[:, l, k, s:s + 1], in1=hi[:, k, a:a + n],
                                                 op0=ALU.add, op1=ALU.subtract).then_inc(los, 1)
                for k in range(KT):
                    for j, (a, n, s) in enumerate(parts):
                        if k >= 2:
                            dve.wait_ge(los, 2 * (k - 2) + j + 1)
                        dve.scalar_tensor_tensor(out=t_[:, k % 2, a:a + n], in0=xt[:, k, a:a + n],
                                                 scalar=mod[:, l, 8 + k, s:s + 1], in1=rb[:, a:a + n],
                                                 op0=ALU.mult, op1=ALU.mult).then_inc(scaled, 1)
                    if k:
                        low(k - 1)
                low(KT - 1)



def project(c, tag, w, col0, pairs, hi, lo, wbuf, chunks, func=None, scale=1.0, dest=None, dram=None,
            residual=None):
    nc = c.nc
    raw, whi, wlo = wbuf
    width = sum(n for _, n in chunks)
    tok0 = chunks[0][0]
    with c.scope(AREA_STAGE):
        ps = c.ps(f"pp{tag}", [P, 2, 3, 512])
        loaded, w_hi, w_lo, mm = (c.sem(f"{x}_{tag}") for x in ("w_loaded", "w_hi", "w_lo", "mm_done"))
        out_done = c.sem(f"out_done_{tag}")
        stored = [c.sem(f"stored_{tag}_{s}") for s in range(2)]
        x_in = [c.sem(f"x_in_{tag}_{s}") for s in range(2)]
        stage = c.sb(f"stage{tag}", [P, 2, width]) if dram is not None or residual else None
        lanes = [(j, a, n, sum(m for _, m in chunks[:j])) for j, (a, n) in enumerate(chunks)]

        with c.block() as block:
            def load(sp, i):
                cols = bass.ds(col0 + i * 256, 256)
                sp.dma_start(raw[:, :, :], w[:, cols].rearrange("(k p) n -> p k n", p=P)).then_inc(loaded, 16)

            @block.sync
            def _(sp):
                load(sp, 0)
                def rest(i):
                    sp.wait_ge(w_lo, 2 * i + 2)
                    load(sp, i + 1)
                def stores(i):
                    for s in range(2):
                        if dram is not None:
                            sp.wait_ge(out_done, 2 * i + s + 3)
                            sp.dma_start(dram[bass.ds(2 * i + s, 1), :, 0:width].rearrange("a p n -> p (a n)"),
                                         stage[:, s, :]).then_inc(stored[s], 16)
                def fetch(i):
                    for s in range(2):
                        sp.wait_ge(out_done, 2 * i + s + 1)
                        sp.dma_start(stage[:, s, :], residual[1][:, bass.ds(2 * i + s, 1), tok0:tok0 + width]
                                     .rearrange("p a n -> p (a n)")).then_inc(x_in[s], 16)
                if residual:
                    fetch(0)
                if pairs > 1:
                    with sp.Fori(0, pairs - 1) as i:
                        rest(i)
                        stores(i)
                        if residual:
                            fetch(i + 1)
                stores(pairs - 1)
                if dram is not None:
                    for s in range(2):
                        sp.wait_ge(stored[s], 16 * pairs + 16)

            @block.scalar
            def _(act):
                if not residual:
                    act.sem_inc(out_done, 2)
                def high(i, s):
                    act.wait_ge(loaded, 16 * i + 16)
                    act.copy(whi[:, :, s * P:(s + 1) * P], raw[:, :, s * P:(s + 1) * P]).then_inc(w_hi, 1)
                def out(i, s):
                    if residual:
                        act.wait_ge(mm, 2 * i + s + 1)
                        return
                    act.wait_ge(mm, 2 * i + s + 1)
                    if dram is not None:
                        act.wait_ge(stored[s], 16 * i + 16)
                    for j, a, n, o in lanes:
                        if dram is not None:
                            to = stage[:, s, o:o + n]
                        else:
                            to = dest[:, bass.ds(2 * i + s, 1), o:o + n].rearrange("p a n -> p (a n)")
                        last = act.activation(to, ps[:, s, j, 0:n], func, scale=scale)
                    last.then_inc(out_done, 1)
                high(0, 0)
                high(0, 1)
                if pairs > 1:
                    with act.Fori(0, pairs - 1) as i:
                        for s in range(2):
                            out(i, s)
                            high(i + 1, s)
                for s in range(2):
                    out(pairs - 1, s)

            @block.vector
            def _(dve):
                if residual:
                    dve.sem_inc(out_done, 2)
                gate, _, dst = residual or (None, None, None)
                def low(i, s):
                    dve.wait_ge(w_hi, 2 * i + s + 1)
                    dve.tensor_tensor(wlo[:, :, s * P:(s + 1) * P], raw[:, :, s * P:(s + 1) * P],
                                      whi[:, :, s * P:(s + 1) * P], ALU.subtract).then_inc(w_lo, 1)
                def add(i, s):
                    dve.wait_ge(mm, 2 * i + s + 1)
                    dve.wait_ge(x_in[s], 16 * i + 16)
                    m = bass.ds(2 * i + s, 1)
                    for j, a, n, o in lanes:
                        dve_gate = gate[:, bass.ds(16 + 2 * i + s, 1), 1 if a < NCTX else 0]
                        last = dve.scalar_tensor_tensor(
                            out=dst[:, m, a:a + n].rearrange("p a n -> p (a n)"), in0=ps[:, s, j, 0:n],
                            scalar=dve_gate, in1=stage[:, s, o:o + n], op0=ALU.mult, op1=ALU.add)
                    last.then_inc(out_done, 1)
                if not residual:
                    with dve.Fori(0, pairs) as i:
                        low(i, 0)
                        low(i, 1)
                else:
                    low(0, 0)
                    low(0, 1)
                    with dve.Fori(0, pairs - 1) as i:
                        for s in range(2):
                            add(i, s)
                            low(i + 1, s)
                    add(pairs - 1, 0)
                    add(pairs - 1, 1)

            @block.gpsimd
            def _(pool):
                if dram is not None:
                    for s in range(2):
                        pool.sem_inc(stored[s], 16)

            @block.tensor
            def _(pe):
                with pe.Fori(0, pairs) as i:
                    for s in range(2):
                        pe.wait_ge(w_lo, 2 * i + s + 1)
                        pe.wait_ge(out_done, 2 * i + s + 1)
                        for j, a, n, o in lanes:
                            for k in range(KT):
                                ws = slice(s * P, (s + 1) * P)
                                acc = ps[:, s, j, 0:n]
                                pe.matmul(acc, whi[:, k, ws], hi[:, k, a:a + n], start=(k == 0), stop=False)
                                pe.matmul(acc, whi[:, k, ws], lo[:, k, a:a + n], start=False, stop=False)
                                last = pe.matmul(acc, wlo[:, k, ws], hi[:, k, a:a + n], start=False,
                                                 stop=(k == KT - 1))
                        last.then_inc(mm, 1)


def project_values(c, tag, w, col0, blocks, hi, lo, wbuf, dest=None, split=None):
    nc = c.nc
    raw, whi, wlo = wbuf
    with c.scope():
        ps = c.ps(f"pv{tag}", [P, 2, 512])
        loaded, w_hi, w_lo, mm = (c.sem(f"{x}_{tag}") for x in ("vw_loaded", "vw_hi", "vw_lo", "vmm_done"))
        out_hi, out_lo = c.sem(f"v_hi_{tag}"), c.sem(f"v_done_{tag}")
        with c.block() as block:
            def load(sp, i):
                sp.dma_start(raw[:, :, :], w[:, bass.ds(col0 + i * 256, 256)]
                             .rearrange("(k p) n -> p k n", p=P)).then_inc(loaded, 16)

            @block.sync
            def _(sp):
                load(sp, 0)
                if blocks > 1:
                    with sp.Fori(0, blocks - 1) as i:
                        sp.wait_ge(w_lo, i + 1)
                        load(sp, i + 1)

            @block.scalar
            def _(act):
                with act.Fori(0, blocks) as i:
                    act.wait_ge(loaded, 16 * i + 16)
                    act.wait_ge(out_lo, TT * i + 2)
                    act.copy(whi[:, :, :], raw[:, :, :]).then_inc(w_hi, 1)
                    if split:
                        for t in range(TT):
                            act.wait_ge(mm, TT * i + t + 1)
                            act.copy(split[0][:, t, :], ps[:, t % 2, 0:256]).then_inc(out_hi, 1)

            @block.vector
            def _(dve):
                dve.sem_inc(out_lo, 2)
                with dve.Fori(0, blocks) as i:
                    dve.wait_ge(w_hi, i + 1)
                    dve.tensor_tensor(wlo[:, :, :], raw[:, :, :], whi[:, :, :], ALU.subtract).then_inc(w_lo, 1)
                    for t in range(TT):
                        if split:
                            dve.wait_ge(out_hi, TT * i + t + 1)
                            dve.tensor_tensor(split[1][:, t, :], ps[:, t % 2, 0:256], split[0][:, t, :],
                                              ALU.subtract).then_inc(out_lo, 1)
                        else:
                            dve.wait_ge(mm, TT * i + t + 1)
                            dve.tensor_copy(dest[:, t, bass.ds(i * 256, 256)], ps[:, t % 2, 0:256]).then_inc(out_lo, 1)

            @block.tensor
            def _(pe):
                with pe.Fori(0, blocks) as i:
                    pe.wait_ge(w_lo, i + 1)
                    for t in range(TT):
                        pe.wait_ge(out_lo, TT * i + t + 1)
                        acc = ps[:, t % 2, 0:256]
                        for k in range(KT):
                            tok = slice(t * P, (t + 1) * P)
                            pe.matmul(acc, hi[:, k, tok], whi[:, k, :], start=(k == 0), stop=False)
                            pe.matmul(acc, hi[:, k, tok], wlo[:, k, :], start=False, stop=False)
                            last = pe.matmul(acc, lo[:, k, tok], whi[:, k, :], start=False, stop=(k == KT - 1))
                        last.then_inc(mm, 1)



def norm_and_rotate(c, io, consts, cols, qk, khi, klo):
    nc = c.nc
    N = QH + KVH
    with c.scope(AREA_H):
        sq = c.sb("qsq", [P, 2, T])
        rs = c.sb("qrs", [N, T])
        cos, sin = c.sb("cos", [P, T]), c.sb("sin", [P, T])
        rot = c.sb("rot", [P, 2, T])
        cq = c.sb("q_cos", [P, 2, T])
        pa, pb = c.ps("qpa", [P, 3, 512]), c.ps("qpb", [P, 3, 512])
        pab = [pa, pb]
        swapped = [c.sem(f"swapped{s}") for s in range(2)]
        tabs, sqd, summed, rooted, recd = (c.sem(x) for x in ("tables_in", "qsq_done", "qsummed", "qrooted", "qrecip"))
        gsc, spread, normed, cosd, sind, done, khd, kld = (c.sem(x) for x in (
            "qgain", "spread_done", "normed", "cos_done", "sin_done", "rotated", "k_hi", "k_lo"))
        with c.block() as block:
            @block.sync
            def _(sp):
                sp.dma_start(cos[:, :], io["cos"]).then_inc(tabs, 16)
                sp.dma_start(sin[:, :], io["sin"]).then_inc(tabs, 16)
                for m in range(N):
                    sp.wait_ge(normed, 3 * (m + 1))
                    if m >= 2:
                        sp.wait_ge(done, m - 1)
                    for b in range(4):
                        f = b ^ 1
                        sp.dma_start(rot[32 * b:32 * b + 32, m % 2, :],
                                     qk[32 * f:32 * f + 32, m, :]).then_inc(swapped[m % 2], 16)

            @block.scalar
            def _(act):
                for m in range(N):
                    if m >= 2:
                        act.wait_ge(summed, m - 1)
                    act.activation(sq[:, m % 2, :], qk[:, m, :], ACT.Square).then_inc(sqd, 1)
                act.wait_ge(summed, N)
                for j, (a, n) in enumerate(ALL_CHUNKS):
                    act.activation(rs[:, a:a + n], pb[0:N, j, 0:n], ACT.Sqrt, bias=consts["eps"][0:N, :],
                                   scale=1.0 / HD).then_inc(rooted, 1)
                for m in range(KVH):
                    act.wait_ge(done, QH + m + 1)
                    act.copy(khi[:, m, :], qk[:, QH + m, :]).then_inc(khd, 1)

            @block.tensor
            def _(pe):
                for m in range(N):
                    pe.wait_ge(sqd, m + 1)
                    for j, (a, n) in enumerate(ALL_CHUNKS):
                        last = pe.matmul(pb[0:N, j, 0:n], consts["sel"][:, N - 1 - m:2 * N - 1 - m],
                                         sq[:, m % 2, a:a + n], start=(m == 0), stop=(m == N - 1))
                    last.then_inc(summed, 1)
                pe.wait_ge(recd, 1)
                for m in range(N):
                    if m >= 2:
                        pe.wait_ge(normed, 3 * (m - 1))
                    for j, (a, n) in enumerate(ALL_CHUNKS):
                        last = pe.matmul(pab[m % 2][:, j, 0:n], consts["spread"][0:N, m, :], rs[:, a:a + n],
                                         start=True, stop=True)
                    last.then_inc(spread, 1)

            @block.vector
            def _(dve):
                dve.tensor_scalar(cols[:, 64:65], cols[:, 64:65], HD ** -0.5, None, ALU.mult).then_inc(gsc, 1)
                dve.wait_ge(rooted, 3)
                dve.reciprocal(rs[:, :], rs[:, :]).then_inc(recd, 1)
                dve.wait_ge(gsc, 1)
                dve.wait_ge(tabs, 32)
                def finish(m):
                    dve.wait_ge(swapped[m % 2], 64 * (m // 2 + 1))
                    dve.tensor_tensor(rot[:, m % 2, :], rot[:, m % 2, :], sin[:, :], ALU.mult).then_inc(sind, 1)
                    dve.wait_ge(cosd, m + 1)
                    dve.wait_ge(sind, m + 1)
                    dve.tensor_tensor(qk[:, m, :], cq[:, m % 2, :], rot[:, m % 2, :], ALU.add).then_inc(done, 1)
                    if m >= QH:
                        k = m - QH
                        dve.wait_ge(khd, k + 1)
                        dve.tensor_tensor(klo[:, k, :], qk[:, m, :], khi[:, k, :], ALU.subtract).then_inc(kld, 1)
                for m in range(N):
                    dve.wait_ge(spread, m + 1)
                    g = 64 if m < QH else 65
                    for j, (a, n) in enumerate(ALL_CHUNKS):
                        dve.scalar_tensor_tensor(out=qk[:, m, a:a + n], in0=qk[:, m, a:a + n],
                                                 scalar=cols[:, g:g + 1], in1=pab[m % 2][:, j, 0:n],
                                                 op0=ALU.mult, op1=ALU.mult).then_inc(normed, 1)
                    if m:
                        finish(m - 1)
                finish(N - 1)

            @block.gpsimd
            def _(pool):
                pool.wait_ge(tabs, 32)
                for m in range(N):
                    pool.wait_ge(normed, 3 * (m + 1))
                    if m >= 2:
                        pool.wait_ge(done, m - 1)
                    pool.tensor_tensor(cq[:, m % 2, :], qk[:, m, :], cos[:, :], ALU.mult).then_inc(cosd, 1)



GQA_TILES = [(NCTX + P * j, T) for j in range(NLAT // P)] + [(P * j, NCTX) for j in range(CT)]
GQA_N = len(GQA_TILES)
GQA_GROUPS = GQA_N // 2
S_RING = 5


def key_chunks(p):
    n = GQA_TILES[p % GQA_N][1]
    return [(a, min(512, n - a)) for a in range(0, n, 512)]


CHUNKS_BEFORE = [sum(len(key_chunks(q)) for q in range(p)) for p in range(GQA_N + 1)]
CHUNKS = CHUNKS_BEFORE[-1]


def chunk_no(p, k):
    return CHUNKS_BEFORE[p % GQA_N] + k + (p // GQA_N) * CHUNKS


def score_bank(p, k):
    return (3 * (p % GQA_N) + k) % S_RING


def bank_user_before(p, k):
    q, j = p, k
    while True:
        j -= 1
        if j < 0:
            q -= 1
            j = len(key_chunks(q)) - 1
        if score_bank(q, j) == score_bank(p, k):
            return chunk_no(q, j)


def at_least(eng, sem, per, h, no):
    if isinstance(h, int) and per * h + no + 1 <= 0:
        return
    eng.wait_ge(sem, h * per + (no + 1))


def grouped_attention(c, io, consts, qk, khi, klo, vhi, vlo):
    nc = c.nc
    with c.scope(AREA_H, (AREA_QKV[1], AREA_W[1])):
        qhi, qlo = c.sb("qhi", [P, T], F32R), c.sb("qlo", [P, T], F32R)
        prob = c.sb("prob", [P, 5, T])
        pthi = c.sb("pthi", [P, 2, TT, 256], F32R)
        ptlo = c.sb("ptlo", [P, 2, TT, 256], F32R)
        cthi = c.sb("cthi", [P, CT, 256], F32R)
        ctlo = c.sb("ctlo", [P, CT, 256], F32R)
        g = c.sb("gate_in", [P, T])
        mx, sums = c.sb("mx", [P, 5, 3]), c.sb("sums", [P, 5, 3])
        nm, tot, rec = c.sb("nm", [P, 5]), c.sb("tot", [P, 5]), c.sb("rec", [P, 5])
        S, TB, O = c.ps("S", [P, S_RING, 512]), c.ps("TB", [P, 2, 512]), c.ps("O", [P, 512])
        q_hi, q_lo = c.sem("gq_hi"), c.sem("gq_lo")
        qkd, mxd, nmd, expd = c.sem("g_scores"), c.sem("g_max"), c.sem("g_negmax"), c.sem("g_exp")
        totd, recd, poolp, actp = c.sem("g_total"), c.sem("g_recip"), c.sem("g_probs_pool"), c.sem("g_probs_act")
        td, hid, lod, pvd, od, gl = (c.sem("g_turned"), c.sem("g_pt_hi"), c.sem("g_pt_lo"), c.sem("g_pv"),
                                     c.sem("g_out"), c.sem("g_gate_in"))
        skewed = c.sem("bias_skewed")
        POOLP, ACTP = 18, 8

        def pool_no(p, k):
            q = p % GQA_N
            return (2 * q + k if q < 8 else 16 + (q - 8)) + (p // GQA_N) * POOLP

        def pt(p):
            q = p % GQA_N
            half = slice((q % 2) * P, (q % 2) * P + P)
            if q >= 8:
                return cthi[:, :, half], ctlo[:, :, half]
            return pthi[:, (q // 2) % 2, :, half], ptlo[:, (q // 2) % 2, :, half]

        def pt_user_before(p):
            q, back = p % GQA_N, (p // GQA_N) * GQA_GROUPS
            gr = q // 2
            return back + {0: -3, 1: -2, 2: 0, 3: 1, 4: -1}[gr]

        def steps(h, tail=False):
            for p in range(3 if tail else GQA_N):
                behind = p - 2
                group = (p - 4) // 2 if p % 2 == 0 else None
                yield p, behind, group

        Q0, Q1, QC = (NCTX, 512), (NCTX + 512, 512), (0, NCTX)

        def runs(eng, body, tail):
            body(0, 0, None)
            with eng.Fori(1, GROUP) as h:
                body(h, 0, 0)
            body(GROUP, 1, 0)
            with eng.Fori(GROUP + 1, QH) as h:
                body(h, 1, 1)
            tail(QH, KVH - 1)

        with c.block() as block:
            @block.sync
            def _(sp):
                def load(h):
                    at_least(sp, od, GQA_GROUPS, h, -1)
                    sp.dma_start(g[:, :], io["gd"][bass.ds(h, 1), :, :].rearrange("a p n -> p (a n)")).then_inc(gl, 16)
                load(0)
                for head in range(NH):
                    src = bass.AP(tensor=io["bias"].tensor, offset=head * BIAS_ROWS * BIAS_W,
                                  ap=[[0, GRID_W], [BIAS_W, BIAS_ROWS], [1, BIAS_W]])
                    dst = bass.AP(tensor=io["skew"].tensor, offset=head * GRID_W * BIAS_ROWS * SKEW_W,
                                  ap=[[BIAS_ROWS * SKEW_W + 1, GRID_W], [SKEW_W, BIAS_ROWS], [1, BIAS_W]])
                    sp.dma_start(dst, src).then_inc(skewed, 16)
                with sp.Fori(1, QH) as h:
                    load(h)
                sp.wait_ge(skewed, 16 * NH)

            @block.tensor
            def _(pe):
                def scores(h, kv, p, k):
                    tok, _ = GQA_TILES[p]
                    a, n = key_chunks(p)[k]
                    if k == 0 and p in (0, 4, 8):
                        at_least(pe, q_lo, 3, h, (0, 4, 8).index(p))
                    at_least(pe, expd, CHUNKS, h, bank_user_before(p, k))
                    acc = S[:, score_bank(p, k), 0:n]
                    qs = slice(tok, tok + P)
                    pe.matmul(acc, qhi[:, qs], khi[:, kv, a:a + n], start=True, stop=False)
                    pe.matmul(acc, qhi[:, qs], klo[:, kv, a:a + n], start=False, stop=False)
                    pe.matmul(acc, qlo[:, qs], khi[:, kv, a:a + n], start=False, stop=True).then_inc(qkd, 1)

                def turn(h, p, k):
                    a, n = key_chunks(p)[k]
                    if k == 2:
                        at_least(pe, actp, ACTP, h, p % GQA_N + (p // GQA_N) * ACTP)
                    else:
                        at_least(pe, poolp, POOLP, h, pool_no(p, k))
                    no = chunk_no(p, k)
                    at_least(pe, lod, CHUNKS, h, no - 2)
                    for b in range(n // P):
                        last = pe.transpose(TB[:, no % 2, b * P:(b + 1) * P],
                                            prob[:, p % 5, a + b * P:a + (b + 1) * P], consts["ident"][:, :])
                    last.then_inc(td, 1)

                def product(h, kv, gr):
                    q = (2 * gr + 1) % GQA_N
                    at_least(pe, lod, CHUNKS, h, chunk_no(2 * gr + 1, len(key_chunks(q)) - 1))
                    at_least(pe, od, GQA_GROUPS, h, gr - 1)
                    n = GQA_TILES[q][1] // P
                    hi, lo = (cthi, ctlo) if q >= 8 else (pthi[:, (q // 2) % 2, :, :], ptlo[:, (q // 2) % 2, :, :])
                    for t in range(n):
                        vs = slice(kv * HD, (kv + 1) * HD)
                        pe.matmul(O[:, 0:256], vhi[:, t, vs], hi[:, t, :], start=(t == 0), stop=False)
                        pe.matmul(O[:, 0:256], vhi[:, t, vs], lo[:, t, :], start=False, stop=False)
                        last = pe.matmul(O[:, 0:256], vlo[:, t, vs], hi[:, t, :], start=False, stop=(t == n - 1))
                    last.then_inc(pvd, 1)

                def body(h, kv, kvp, tail=False):
                    for p, q, gr in steps(h, tail):
                        chunks = [] if tail else key_chunks(p)
                        turns = key_chunks(q) if kvp is not None or q >= 0 else []
                        if tail and q >= 0:
                            turns = []
                        for k in range(max(len(chunks), len(turns))):
                            if k < len(chunks):
                                scores(h, kv, p, k)
                            if k < len(turns):
                                turn(h, q, k)
                        if gr is not None and (gr >= 0 or kvp is not None) and not (tail and gr >= 0):
                            product(h, kvp if gr < 0 else kv, gr)
                runs(pe, body, lambda h, kv: body(h, kv, kv, tail=True))

            @block.vector
            def _(dve):
                def q_low(h, piece, no, user):
                    a, n = piece
                    dve.wait_ge(q_hi, h * 3 + no + 1)
                    dve.tensor_tensor(qlo[:, a:a + n], qk[:, bass.ds(h, 1), a:a + n].rearrange("p a n -> p (a n)"),
                                      qhi[:, a:a + n], ALU.subtract).then_inc(q_lo, 1)

                def biggest(h, p, k):
                    a, n = key_chunks(p)[k]
                    at_least(dve, qkd, CHUNKS, h, chunk_no(p, k))
                    dve.tensor_reduce(mx[:, p % 5, k:k + 1], S[:, score_bank(p, k), 0:n], AX, ALU.max).then_inc(mxd, 1)

                def negmax(h, p):
                    n = len(key_chunks(p))
                    at_least(dve, mxd, CHUNKS, h, chunk_no(p, n - 1))
                    dve.tensor_reduce(nm[:, p % 5:p % 5 + 1], mx[:, p % 5, 0:n], AX, ALU.max,
                                      negate=True).then_inc(nmd, 1)

                def reciprocal(h, p):
                    n = len(key_chunks(p))
                    at_least(dve, expd, CHUNKS, h, chunk_no(p, n - 1))
                    dve.tensor_reduce(tot[:, p % 5:p % 5 + 1], sums[:, p % 5, 0:n], AX, ALU.add).then_inc(totd, 1)
                    at_least(dve, totd, GQA_N, h, p)
                    dve.reciprocal(rec[:, p % 5:p % 5 + 1], tot[:, p % 5:p % 5 + 1]).then_inc(recd, 1)

                def low(h, p, k):
                    a, n = key_chunks(p)[k]
                    no = chunk_no(p, k)
                    at_least(dve, hid, CHUNKS, h, no)
                    hi, lo = pt(p)
                    blocks = slice(a // P, (a + n) // P)
                    dve.tensor_tensor(lo[:, blocks, :], TB[:, no % 2, 0:n].rearrange("p (b q) -> p b q", q=P),
                                      hi[:, blocks, :], ALU.subtract).then_inc(lod, 1)

                def out(h, gr):
                    at_least(dve, pvd, GQA_GROUPS, h, gr)
                    head = h - 1 if gr < 0 else h
                    at_least(dve, gl, 1, 16 * head, 15)
                    tok = GQA_TILES[(2 * gr) % GQA_N][0]
                    dve.tensor_tensor(qk[:, bass.ds(head, 1), tok:tok + 256].rearrange("p a n -> p (a n)"),
                                      O[:, 0:256], g[:, tok:tok + 256], ALU.mult).then_inc(od, 1)

                def body(h, kv, kvp, tail=False):
                    for p, q, gr in steps(h, tail):
                        prev = kvp is not None
                        chunks = [] if tail else key_chunks(p)
                        turns = key_chunks(q) if prev or q >= 0 else []
                        if tail and q >= 0:
                            turns = []
                        if p % 2 == 1 and (p >= 5 or prev) and not (tail and p >= 5):
                            out(h, (p - 5) // 2)
                        for k in range(max(len(chunks), len(turns))):
                            if k < len(chunks):
                                biggest(h, p, k)
                            if k == 0 and (p >= 1 or prev) and not (tail and p >= 1):
                                reciprocal(h, p - 1)
                            if k < len(turns):
                                low(h, q, k)
                        if not tail:
                            negmax(h, p)
                            if p == 1:
                                q_low(h, Q1, 1, None)
                            if p == 3:
                                q_low(h, QC, 2, None)
                            if p == 5:
                                q_low(h + 1, Q0, 0, None)
                    if tail:
                        out(h, -1)

                q_low(0, Q0, 0, None)
                runs(dve, body, lambda h, kv: body(h, kv, kv, tail=True))

            @block.scalar
            def _(act):
                def q_high(h, piece, no, user, users_head):
                    a, n = piece
                    at_least(act, qkd, CHUNKS, users_head, user)
                    act.copy(qhi[:, a:a + n], qk[:, bass.ds(h, 1), a:a + n].rearrange("p a n -> p (a n)")).then_inc(q_hi, 1)

                def exps(h, p):
                    at_least(act, nmd, GQA_N, h, p)
                    at_least(act, td, CHUNKS, h, chunk_no(p - 5, len(key_chunks(p - 5)) - 1))
                    for k, (a, n) in enumerate(key_chunks(p)):
                        act.activation(prob[:, p % 5, a:a + n], S[:, score_bank(p, k), 0:n], ACT.Exp,
                                       bias=nm[:, p % 5:p % 5 + 1],
                                       accum_out=sums[:, p % 5, k:k + 1]).then_inc(expd, 1)

                def norm(h, p):
                    at_least(act, recd, GQA_N, h, p)
                    a, n = key_chunks(p)[2]
                    act.activation(prob[:, p % 5, a:a + n], prob[:, p % 5, a:a + n], ACT.Copy,
                                   scale=rec[:, p % 5:p % 5 + 1]).then_inc(actp, 1)

                def high(h, p, k):
                    a, n = key_chunks(p)[k]
                    no = chunk_no(p, k)
                    at_least(act, td, CHUNKS, h, no)
                    if k == 0:
                        at_least(act, pvd, GQA_GROUPS, h, pt_user_before(p))
                    hi, _ = pt(p)
                    act.copy(hi[:, a // P:(a + n) // P, :],
                             TB[:, no % 2, 0:n].rearrange("p (b q) -> p b q", q=P)).then_inc(hid, 1)

                def body(h, kv, kvp, tail=False):
                    for p, q, gr in steps(h, tail):
                        prev = kvp is not None
                        if (p >= 1 or prev) and not (tail and p >= 1):
                            exps(h, p - 1)
                        turns = key_chunks(q) if prev or q >= 0 else []
                        if tail and q >= 0:
                            turns = []
                        for k in range(max(1, len(turns))):
                            if k < len(turns):
                                high(h, q, k)
                            if k == 0 and (p >= 1 or prev) and not (tail and p >= 1) and len(key_chunks(p - 1)) == 3:
                                norm(h, p - 1)
                        if not tail:
                            if p == 1:
                                q_high(h, Q1, 1, chunk_no(7, 2) - CHUNKS, h)
                            if p == 3:
                                q_high(h, QC, 2, chunk_no(9, 0) - CHUNKS, h)
                            if p == 5:
                                q_high(h + 1, Q0, 0, chunk_no(3, 2), h)

                q_high(0, Q0, 0, -1, 0)
                runs(act, body, lambda h, kv: body(h, kv, kv, tail=True))

            @block.gpsimd
            def _(pool):
                def body(h, kv, kvp):
                    for p in range(GQA_N):
                        at_least(pool, recd, GQA_N, h, p)
                        for a, n in key_chunks(p)[0:2]:
                            pool.tensor_tensor(prob[:, p % 5, a:a + n], prob[:, p % 5, a:a + n],
                                               rec[:, p % 5:p % 5 + 1].broadcast_to([P, n]),
                                               ALU.mult).then_inc(poolp, 1)
                runs(pool, body, lambda h, kv: None)



NA_TILES = 2 * (NLAT // P)
NA_GROUPS = NA_TILES // 2
NJ = NLAT // P


def first_row(j):
    return max(0, min(2 * j - KH // 2, ROWS - KH))


def is_mid(j):
    return first_row(j) != max(0, min(2 * j + 1 - KH // 2, ROWS - KH))


def group_base(gr):
    return first_row(2 * (gr % (NJ // 2))) // 2


def neighbourhood_attention(c, io, consts, vraw):
    nc = c.nc
    NE, NM = len(END_SLOTS), len(MID_SLOTS)
    with c.scope(AREA_H, (120, AREA_W[1])):
        q2, k2, g2 = c.sb("q2", [P, NLAT]), c.sb("k2", [P, T]), c.sb("g2", [P, NLAT])
        be, bm = c.sb("bias_end", [P, 2, NE, GRID_W]), c.sb("bias_mid", [P, 2, NM, GRID_W])
        mc, mm9 = c.sb("mask_cols", [P, GRID_W]), c.sb("mask_mid", [P, NM, GRID_W])
        qs = c.sb("q_split", [P, 2, NLAT], F32R)
        ka, kb = c.sb("k_split", [P, 2, T], F32R), c.sb("k_swapped", [P, 2, T], F32R)
        vs = c.sb("v_split", [P, 2, TT, P], F32R)
        prob = c.sb("nprob", [P, 4, 832])
        pe_hi, pe_lo = c.sb("pt_end_hi", [P, 2, 6, 256], F32R), c.sb("pt_end_lo", [P, 2, 6, 256], F32R)
        pm_hi, pm_lo = c.sb("pt_mid_hi", [P, 2, 8, 256], F32R), c.sb("pt_mid_lo", [P, 2, 8, 256], F32R)
        ost, half = c.sb("o_out", [P, NLAT]), c.sb("o_half", [P, 256])
        mx, sums = c.sb("nmx", [P, 4, 4]), c.sb("nsums", [P, 4, 2])
        nm, tot, rec = c.sb("nnm", [P, 4]), c.sb("ntot", [P, 4]), c.sb("nrec", [P, 4])
        S, TB, O = c.ps("nS", [P, 2, 2, 512]), c.ps("nTB", [P, 2, 512]), c.ps("nO", [P, 2, 512])
        ql, kl, gl, ml = (c.sem(x) for x in ("n_q_in", "n_k_in", "n_g_in", "n_mask_in"))
        bl = [c.sem(f"n_bias_in{s}") for s in range(2)]
        swd = [c.sem(f"n_swapped{s}") for s in range(2)]
        hid_, lod_ = c.sem("n_split_hi"), c.sem("n_split_lo")
        bmd, zero = c.sem("n_bias_masked"), c.sem("n_zeroed")
        qkd, mxd, nmd, expd, totd, recd = (c.sem(x) for x in (
            "n_scores", "n_max", "n_negmax", "n_exp", "n_total", "n_recip"))
        poolp, actp, td, hid, lod = (c.sem(x) for x in ("n_probs_pool", "n_probs_act", "n_turned", "n_pt_hi", "n_pt_lo"))
        pvd, halfd, addd, od, std = (c.sem(x) for x in ("n_pv", "n_half", "n_added", "n_out", "n_stored"))
        SPL, N, G = 6, NA_TILES, NA_GROUPS
        PAIRS = NH // 2

        def rows(s, lo):
            top = (s == 0) != lo
            return slice(0, 64) if top else slice(64, 128)

        def pt(p):
            gr = (p % N) // 2 % 4
            hs = slice((p % 2) * P, (p % 2) * P + P)
            if gr in (0, 3):
                return pe_hi[:, gr // 3, :, :], pe_lo[:, gr // 3, :, :], hs
            return pm_hi[:, gr - 1, :, :], pm_lo[:, gr - 1, :, :], hs

        def first_block(p):
            j = p % NJ
            return first_row(j) // 2 - group_base(j // 2)

        def ctx_block(p):
            return 6 if (p % N) // 2 % 4 in (1, 2) else 4

        def runs(eng, body):
            body(0, True, False)
            with eng.Fori(1, PAIRS - 1) as i:
                body(i, False, False)
            body(PAIRS - 1, False, True)

        with c.block() as block:
            @block.sync
            def _(sp):
                def qk_in(i):
                    src = lambda a: a[bass.ds(i, 1), :, :].rearrange("a p n -> p (a n)")
                    at_least(sp, lod_, SPL, i, -2)
                    sp.dma_start(q2[:, :], src(io["qd"][:, :, 0:NLAT])).then_inc(ql, 16)
                    sp.dma_start(k2[:, :], src(io["kd"])).then_inc(kl, 16)

                def swap(i, s):
                    at_least(sp, lod_, SPL, i, 3 * s + 1)
                    for b in range(2):
                        sp.dma_start(kb[64 * b:64 * b + 64, s, :].bitcast(F32),
                                     ka[64 * (1 - b):64 * (1 - b) + 64, s, :].bitcast(F32)).then_inc(swd[s], 16)

                def bias_in(i, s):
                    at_least(sp, mxd, N, i, 8 * s - 9)
                    head = 2 * i + s
                    for rr in range(2):
                        sp.dma_start(be[64 * rr:64 * rr + 64, s, :, :],
                                     io["skew"][bass.ds(head, 1), :, END_SLOTS[0] - rr:END_SLOTS[-1] + 1 - rr, GRID_W - 1:2 * GRID_W - 1]
                                     .rearrange("a c e w -> c (a e) w")).then_inc(bl[s], 16)

                def g_in(i):
                    at_least(sp, od, G, i, -1)
                    sp.dma_start(g2[:, :], io["gd"][bass.ds(i, 1), :, 0:NLAT].rearrange("a p n -> p (a n)")).then_inc(gl, 16)

                def store(i):
                    at_least(sp, od, G, i, G - 1)
                    sp.dma_start(io["od"][bass.ds(i, 1), :, :].rearrange("a p n -> p (a n)"), ost[:, :]).then_inc(std, 16)

                sp.dma_start(mc[:, :], io["mask_cols"]).then_inc(ml, 16)
                sp.dma_start(mm9[:, :, :], io["mask_mid"]).then_inc(ml, 16)
                qk_in(0)
                bias_in(0, 0)
                swap(0, 0)

                def body(i, first, last):
                    bias_in(i, 1)
                    swap(i, 1)
                    if not first:
                        store(i - 1)
                    g_in(i)
                    if not last:
                        qk_in(i + 1)
                        bias_in(i + 1, 0)
                        swap(i + 1, 0)
                runs(sp, body)
                store(PAIRS - 1)
                sp.wait_ge(std, 16 * PAIRS)

            @block.tensor
            def _(pe):
                def scores(i, p):
                    s, j = p // NJ, p % NJ
                    r0 = first_row(j)
                    if j == 0:
                        at_least(pe, swd[s], 32, i, 31)
                    at_least(pe, expd, 2 * N, i, 2 * (p - 2) + 1)
                    q = qs[:, s, j * P:(j + 1) * P]
                    loc = NCTX + r0 * GRID_W
                    out = [(S[:, p % 2, 0, 0:512], loc, 512)]
                    if is_mid(j):
                        out.append((S[:, p % 2, 1, 256:320], loc + 512, 64))
                    out.append((S[:, p % 2, 1, 0:256], 0, NCTX))
                    for acc, a, n in out:
                        pe.matmul(acc, q, ka[:, s, a:a + n], start=True, stop=False)
                        last = pe.matmul(acc, q, kb[:, s, a:a + n], start=False, stop=True)
                    last.then_inc(qkd, 1)

                def turn(i, p, k):
                    at_least(pe, lod, 2 * N, i, 2 * p + k - 2)
                    if k == 0:
                        at_least(pe, poolp, N, i, p)
                        for b in range(4):
                            last = pe.transpose(TB[:, 0, b * P:(b + 1) * P], prob[:, p % 4, b * P:(b + 1) * P],
                                                consts["ident"][:, :])
                    else:
                        at_least(pe, actp, N, i, p)
                        for b in range(2):
                            last = pe.transpose(TB[:, 1, b * P:(b + 1) * P],
                                                prob[:, p % 4, 576 + b * P:576 + (b + 1) * P], consts["ident"][:, :])
                        if is_mid(p % NJ):
                            last = pe.transpose(TB[0:64, 1, 256:384], prob[:, p % 4, 512:576], consts["ident"][:, :])
                    last.then_inc(td, 1)

                def product(i, gr):
                    s = (gr % G) // 4
                    at_least(pe, lod, 2 * N, i, 2 * (2 * gr + 1) + 1)
                    at_least(pe, od, G, i, gr - 2)
                    hi, lo, _ = pt(2 * gr)
                    nloc = 6 if gr % 4 in (1, 2) else 4
                    keys = [(b, nloc + b) for b in range(CT)] + [(CT + group_base(gr) + b, b) for b in range(nloc)]
                    for n, (v, b) in enumerate(keys):
                        pe.matmul(O[:, gr % 2, 0:256], vs[:, s, v, :], hi[:, b, :], start=(n == 0), stop=False)
                        last = pe.matmul(O[:, gr % 2, 0:256], vs[:, s, v, :], lo[:, b, :], start=False,
                                         stop=(n == len(keys) - 1))
                    last.then_inc(pvd, 1)

                def body(i, first, last, tail=False):
                    for p in range(3 if tail else N):
                        q, gr = p - 2, (p - 4) // 2
                        if not tail:
                            scores(i, p)
                        if (q >= 0 or not first) and not (tail and q >= 0):
                            turn(i, q, 0)
                            turn(i, q, 1)
                        if p % 2 == 0 and (gr >= 0 or not first):
                            if p == 0 or gr >= 0 or p == 2:
                                product(i, gr)
                pe.wait_ge(zero, 4)
                runs(pe, body)
                body(PAIRS, False, True, tail=True)

            def split_steps(i, first, last, p):
                if p in (1, 2, 3):
                    return [(i, 1, p - 1)]
                if p in (11, 12, 13) and not last:
                    return [(i + 1, 0, p - 11)]
                return []

            def parts(i, s, what):
                src, hi, lo = rows(s, False), rows(s, False), rows(s, True)
                if what == 0:
                    return q2[src, :], qs[hi, s, :], qs[lo, s, :]
                if what == 1:
                    return k2[src, :], ka[hi, s, :], ka[lo, s, :]
                v = vraw[:, :, bass.ds(i * P + s * ND, ND)]
                return v, vs[:, s, :, 0:ND], vs[:, s, :, ND:2 * ND]

            @block.scalar
            def _(act):
                def split(i, s, what):
                    if what == 0:
                        at_least(act, ql, 16, i, 15)
                        at_least(act, qkd, N, i, 8 * s + 7 - N)
                    if what == 1:
                        at_least(act, kl, 16, i, 15)
                    if what == 2:
                        at_least(act, pvd, G, i, 4 * s + 3 - G)
                    v, hi, _ = parts(i, s, what)
                    act.copy(hi, v).then_inc(hid_, 1)

                def exps(i, p):
                    at_least(act, nmd, N, i, p)
                    n = 576 if is_mid(p % NJ) else 512
                    pr = prob[:, p % 4, 0:n]
                    b = nm[:, p % 4:p % 4 + 1]
                    act.activation(pr, pr, ACT.Exp, bias=b, accum_out=sums[:, p % 4, 0:1]).then_inc(expd, 1)
                    act.activation(prob[:, p % 4, 576:832], S[:, p % 2, 1, 0:256], ACT.Exp, bias=b,
                                   accum_out=sums[:, p % 4, 1:2]).then_inc(expd, 1)

                def norm(i, p):
                    at_least(act, recd, N, i, p)
                    pr = prob[:, p % 4, 512:832] if is_mid(p % NJ) else prob[:, p % 4, 576:832]
                    act.activation(pr, pr, ACT.Copy, scale=rec[:, p % 4:p % 4 + 1]).then_inc(actp, 1)

                def high(i, p, k):
                    at_least(act, td, 2 * N, i, 2 * p + k)
                    hi, _, hs = pt(p)
                    if k == 0:
                        at_least(act, pvd, G, i, p // 2 - 4)
                        b = first_block(p)
                        act.copy(hi[:, b:b + 4, hs], TB[:, 0, :].rearrange("p (b q) -> p b q", q=P)).then_inc(hid, 1)
                    else:
                        b = ctx_block(p)
                        if is_mid(p % NJ):
                            act.copy(hi[0:64, first_block(p) + 4, hs], TB[0:64, 1, 256:384])
                        act.copy(hi[:, b:b + 2, hs], TB[:, 1, 0:256].rearrange("p (b q) -> p b q", q=P)).then_inc(hid, 1)

                def fold(i, gr):
                    s = (gr % G) // 4
                    at_least(act, pvd, G, i, gr)
                    at_least(act, addd, G, i, gr - 1)
                    act.copy(half[rows(s, False), :], O[rows(s, True), gr % 2, 0:256]).then_inc(halfd, 1)

                def body(i, first, last, tail=False):
                    for p in range(4 if tail else N):
                        q = p - 2
                        prev = not first
                        if (p >= 1 or prev) and not (tail and p >= 1):
                            exps(i, p - 1)
                        if (q >= 0 or prev) and not (tail and q >= 0):
                            high(i, q, 0)
                            high(i, q, 1)
                        if (p >= 1 or prev) and not (tail and p >= 1):
                            norm(i, p - 1)
                        if p % 2 == 1 and (p >= 5 or prev) and not (tail and p >= 5):
                            fold(i, (p - 5) // 2)
                        if not tail:
                            for a in split_steps(i, first, last, p):
                                split(*a)
                act.wait_ge(zero, 4)
                for what in range(3):
                    split(0, 0, what)
                runs(act, body)
                body(PAIRS, False, True, tail=True)

            @block.vector
            def _(dve):
                def split(i, s, what):
                    at_least(dve, hid_, SPL, i, 3 * s + what)
                    if what == 1:
                        at_least(dve, swd[s], 32, i, -1)
                    v, hi, lo = parts(i, s, what)
                    dve.tensor_tensor(lo, v, hi, ALU.subtract).then_inc(lod_, 1)

                def mask(i, s):
                    at_least(dve, bl[s], 32, i, 31)
                    a = MID_SLOTS[0] - END_SLOTS[0]
                    dve.tensor_tensor(bm[:, s, :, :], be[:, s, a:a + NM, :], mm9[:, :, :], ALU.add).then_inc(bmd, 1)
                    at_least(dve, bmd, 4, i, 2 * s)
                    dve.tensor_tensor(be[:, s, :, :], be[:, s, :, :],
                                      mc[:, :].unsqueeze(1).broadcast_to([P, NE, GRID_W]), ALU.add).then_inc(bmd, 1)

                def biggest(i, p):
                    s, j = p // NJ, p % NJ
                    r0 = first_row(j)
                    if j == 0:
                        at_least(dve, bmd, 4, i, 2 * s + 1)
                    at_least(dve, qkd, N, i, p)
                    at_least(dve, td, 2 * N, i, 2 * (p - 4) + 1)
                    e = r0 - 2 * j + 7
                    sl = p % 4
                    dve.tensor_reduce(mx[:, sl, 1:2], S[:, p % 2, 1, 0:256], AX, ALU.max)
                    if is_mid(j):
                        e -= MID_SLOTS[0]
                        dve.tensor_tensor_reduce(out=prob[:, sl, 512:576], in0=S[:, p % 2, 1, 256:320],
                                                 in1=bm[:, s, e + 8, :], scale=1.0, scalar=-3e38, op0=ALU.add,
                                                 op1=ALU.max, accum_out=mx[:, sl, 2:3])
                        tab = bm[:, s, e:e + 8, :]
                    else:
                        e -= END_SLOTS[0]
                        tab = be[:, s, e:e + 8, :]
                    last = dve.tensor_tensor_reduce(
                        out=prob[:, sl, 0:512], in0=S[:, p % 2, 0, 0:512], in1=tab.rearrange("p e w -> p (e w)"),
                        scale=1.0, scalar=-3e38, op0=ALU.add, op1=ALU.max, accum_out=mx[:, sl, 0:1])
                    last.then_inc(mxd, 1)
                    at_least(dve, mxd, N, i, p)
                    dve.tensor_reduce(nm[:, sl:sl + 1], mx[:, sl, 0:3 if is_mid(j) else 2], AX, ALU.max,
                                      negate=True).then_inc(nmd, 1)

                def reciprocal(i, p):
                    sl = p % 4
                    at_least(dve, expd, 2 * N, i, 2 * p + 1)
                    dve.tensor_reduce(tot[:, sl:sl + 1], sums[:, sl, :], AX, ALU.add).then_inc(totd, 1)
                    at_least(dve, totd, N, i, p)
                    dve.reciprocal(rec[:, sl:sl + 1], tot[:, sl:sl + 1]).then_inc(recd, 1)

                def low(i, p, k):
                    at_least(dve, hid, 2 * N, i, 2 * p + k)
                    hi, lo, hs = pt(p)
                    if k == 0:
                        b = first_block(p)
                        dve.tensor_tensor(lo[:, b:b + 4, hs], TB[:, 0, :].rearrange("p (b q) -> p b q", q=P),
                                          hi[:, b:b + 4, hs], ALU.subtract).then_inc(lod, 1)
                    else:
                        b = ctx_block(p)
                        if is_mid(p % NJ):
                            f = first_block(p) + 4
                            dve.tensor_tensor(lo[0:64, f, hs], TB[0:64, 1, 256:384], hi[0:64, f, hs], ALU.subtract)
                        dve.tensor_tensor(lo[:, b:b + 2, hs], TB[:, 1, 0:256].rearrange("p (b q) -> p b q", q=P),
                                          hi[:, b:b + 2, hs], ALU.subtract).then_inc(lod, 1)

                def out(i, gr):
                    s = (gr % G) // 4
                    r = rows(s, False)
                    a = (gr % 4) * 256
                    at_least(dve, halfd, G, i, gr)
                    if gr % G == 0:
                        pair = i - 1 if gr < 0 else i
                        at_least(dve, std, 16, pair, -1)
                        at_least(dve, gl, 16, pair, 15)
                    dve.tensor_tensor(ost[r, a:a + 256], O[r, gr % 2, 0:256], half[r, :], ALU.add).then_inc(addd, 1)
                    at_least(dve, addd, G, i, gr)
                    dve.tensor_tensor(ost[r, a:a + 256], ost[r, a:a + 256], g2[r, a:a + 256], ALU.mult).then_inc(od, 1)

                def body(i, first, last, tail=False):
                    for p in range(4 if tail else N):
                        q, prev = p - 2, not first
                        if not tail:
                            biggest(i, p)
                        if (p >= 1 or prev) and not (tail and p >= 1):
                            reciprocal(i, p - 1)
                        if (q >= 0 or prev) and not (tail and q >= 0):
                            low(i, q, 0)
                            low(i, q, 1)
                        if p % 2 == 1 and (p >= 5 or prev) and not (tail and p >= 5):
                            out(i, (p - 5) // 2)
                        if not tail:
                            for a in split_steps(i, first, last, p):
                                split(*a)
                            if p == 4:
                                mask(i, 1)
                            if p == 14 and not last:
                                mask(i + 1, 0)
                dve.wait_ge(zero, 4)
                dve.wait_ge(ml, 32)
                for what in range(3):
                    split(0, 0, what)
                mask(0, 0)
                runs(dve, body)
                body(PAIRS, False, True, tail=True)

            @block.gpsimd
            def _(pool):
                for t in (pm_hi, pm_lo):
                    for gq in range(2):
                        last = pool.memset(t[:, gq, :, :].rearrange("p b q -> p (b q)").bitcast(F32), 0.0)
                        last.then_inc(zero, 1)

                def body(i, first, last):
                    for p in range(N):
                        at_least(pool, recd, N, i, p)
                        pool.tensor_tensor(prob[:, p % 4, 0:512], prob[:, p % 4, 0:512],
                                           rec[:, p % 4:p % 4 + 1].broadcast_to([P, 512]),
                                           ALU.mult).then_inc(poolp, 1)
                runs(pool, body)



def split_tiles(c, tag, hi, lo, width, src=None, dram=None):
    nc = c.nc
    with c.scope(AREA_MID):
        raw = c.sb(f"raw{tag}", [P, 2, width]) if dram is not None else None
        il = [c.sem(f"s_in_{tag}_{s}") for s in range(2)]
        h, l = c.sem(f"s_hi_{tag}"), c.sem(f"s_lo_{tag}")
        part = (lambda k: raw[:, k % 2, :]) if dram is not None else (lambda k: src[:, k, :])
        with c.block() as block:
            @block.sync
            def _(sp):
                if dram is not None:
                    for k in range(KT):
                        if k >= 2:
                            sp.wait_ge(l, k - 1)
                        sp.dma_start(raw[:, k % 2, :], dram[k, :, 0:width]).then_inc(il[k % 2], 16)

            @block.scalar
            def _(act):
                for k in range(KT):
                    if dram is not None:
                        act.wait_ge(il[k % 2], 16 * (k // 2) + 16)
                    act.copy(hi[:, k, T - width:], part(k)).then_inc(h, 1)

            @block.vector
            def _(dve):
                for k in range(KT):
                    dve.wait_ge(h, k + 1)
                    dve.tensor_tensor(lo[:, k, T - width:], part(k), hi[:, k, T - width:], ALU.subtract).then_inc(l, 1)


def finish(c, io, consts, xt):
    nc = c.nc
    LT = NLAT // P
    with c.scope(AREA_H):
        fg = c.sb("final_gain", [P, D])
        xo, sq = c.sb("x_out", [P, 2, D]), c.sb("x_sq", [P, D])
        ss, rt, rc = c.sb("ss", [P, LT]), c.sb("rt", [P, LT]), c.sb("rc", [P, LT])
        ps = c.ps("fps", [P, 2, 2, 512])
        fgl, td, sd, rd, rcd, fd = (c.sem(x) for x in (
            "fg_in", "f_turned", "f_squared", "f_root", "f_recip", "f_done"))
        st = [c.sem(f"f_stored{s}") for s in range(2)]
        with c.block() as block:
            @block.sync
            def _(sp):
                sp.dma_start(fg[:, :], io["final_g"].rearrange("(a d) -> a d", a=1).broadcast_to([P, D])).then_inc(fgl, 16)
                for t in range(LT):
                    sp.wait_ge(fd, t + 1)
                    sp.dma_start(io["out"][0, t * P:(t + 1) * P, :], xo[:, t % 2, :]).then_inc(st[t % 2], 16)
                for s in range(2):
                    sp.wait_ge(st[s], 16 * LT // 2)

            @block.tensor
            def _(pe):
                for t in range(LT):
                    if t >= 2:
                        pe.wait_ge(fd, t - 1)
                    for k in range(KT):
                        last = pe.transpose(ps[:, t % 2, k // 4, (k % 4) * P:(k % 4 + 1) * P],
                                            xt[:, k, NCTX + t * P:NCTX + (t + 1) * P], consts["ident"][:, :])
                    last.then_inc(td, 1)

            @block.scalar
            def _(act):
                for t in range(LT):
                    act.wait_ge(td, t + 1)
                    if t:
                        act.wait_ge(sd, t)
                    act.activation(sq[:, :], ps[:, t % 2, :, :].rearrange("p a n -> p (a n)"), ACT.Square,
                                   accum_out=ss[:, t:t + 1]).then_inc(sd, 1)
                    act.wait_ge(sd, t + 1)
                    act.activation(rt[:, t:t + 1], ss[:, t:t + 1], ACT.Sqrt, bias=consts["eps"][:, :],
                                   scale=1.0 / D).then_inc(rd, 1)

            @block.vector
            def _(dve):
                dve.wait_ge(fgl, 16)
                for t in range(LT):
                    dve.wait_ge(rd, t + 1)
                    dve.reciprocal(rc[:, t:t + 1], rt[:, t:t + 1]).then_inc(rcd, 1)
                    dve.wait_ge(rcd, t + 1)
                    if t >= 2:
                        dve.wait_ge(st[t % 2], 16 * (t // 2))
                    dve.scalar_tensor_tensor(out=xo[:, t % 2, :], in0=ps[:, t % 2, :, :].rearrange("p a n -> p (a n)"),
                                             scalar=rc[:, t:t + 1], in1=fg[:, :], op0=ALU.mult,
                                             op1=ALU.mult).then_inc(fd, 1)



def backbone(nc, io, stop=None):
    with ExitStack() as stack:
        c = Core(nc, stack)
        with c.scope(AREA_CONST):
            consts = {"ident": c.sb("ident", [P, P]), "ones": c.sb("ones", [P, P]), "eps": c.sb("eps", [P, 1]),
                      "sel": c.sb("sel", [P, 2 * (QH + KVH) - 1]), "spread": c.sb("spread", [QH + KVH, QH + KVH, P])}
            mod, cols = c.sb("mod", [P, 2, 24, 2]), c.sb("cols", [P, 66])

        def scratch(name, shape):
            return nc.dram_tensor(name, shape, F32).ap()
        io["xt"] = scratch("xt_scratch", [P, KT, T])
        io["skew"] = scratch("bias_scratch", [NH, GRID_W, BIAS_ROWS, SKEW_W])
        io["gd"] = scratch("gate_scratch", [KT, P, T])
        io["qd"] = scratch("q_scratch", [KT, P, NLAT])
        io["kd"] = scratch("k_scratch", [KT, P, T])
        io["od"] = scratch("o_scratch", [KT, P, NLAT])

        with c.scope(AREA_H):
            hi, lo = c.sb("h_hi", [P, KT, T], F32R), c.sb("h_lo", [P, KT, T], F32R)
        with c.scope(AREA_X):
            xt = c.sb("xt", [P, KT, T])
        with c.scope(AREA_X):
            vraw = c.sb("v_raw", [P, TT, D])
        with c.scope(AREA_QKV):
            qk = c.sb("qk", [P, QH + KVH, T])
            vhi, vlo = c.sb("v_hi0", [P, TT, 256], F32R), c.sb("v_lo0", [P, TT, 256], F32R)
            khi, klo = c.sb("k_hi0", [P, KVH, T], F32R), c.sb("k_lo0", [P, KVH, T], F32R)
        with c.scope(AREA_W):
            wbuf = c.sb("w_raw", [P, KT, 256]), c.sb("w_hi", [P, KT, 256], F32R), c.sb("w_lo", [P, KT, 256], F32R)

        qw, kw = QH * HD, KVH * HD
        w = io["ga_w_in"]
        steps = [
            lambda: load_and_modulate(c, io, consts, xt, mod, cols),
            lambda: normalise(c, io, consts, 0, xt, hi, lo, mod, store=False),
            lambda: project(c, "q0", w, 0, (QH + KVH) // 2, hi, lo, wbuf, ALL_CHUNKS, ACT.Copy, dest=qk),
            lambda: project_values(c, "v0", w, qw + kw, 1, hi, lo, wbuf, split=(vhi, vlo)),
            lambda: project(c, "g0", w, qw + 2 * kw, KT // 2, hi, lo, wbuf, ALL_CHUNKS, ACT.Silu, dram=io["gd"]),
            lambda: norm_and_rotate(c, io, consts, cols, qk, khi, klo),
            lambda: grouped_attention(c, io, consts, qk, khi, klo, vhi, vlo),
            lambda: split_tiles(c, "o0", hi, lo, T, src=qk),
            lambda: project(c, "o0", io["ga_w_out"], 0, KT // 2, hi, lo, wbuf, ALL_CHUNKS,
                            residual=(mod[:, 0], io["xt"], xt)),
            lambda: normalise(c, io, consts, 1, xt, hi, lo, mod, store=True),
            lambda: project(c, "q1", io["na_w_in"], 0, KT // 2, hi, lo, wbuf, LAT_CHUNKS, ACT.Copy,
                            scale=ND ** -0.5, dram=io["qd"]),
            lambda: project(c, "k1", io["na_w_in"], D, KT // 2, hi, lo, wbuf, ALL_CHUNKS, ACT.Copy, dram=io["kd"]),
            lambda: project_values(c, "v1", io["na_w_in"], 2 * D, D // 256, hi, lo, wbuf, dest=vraw),
            lambda: project(c, "g1", io["na_w_in"], 3 * D, KT // 2, hi, lo, wbuf, LAT_CHUNKS, ACT.Silu, dram=io["gd"]),
            lambda: neighbourhood_attention(c, io, consts, vraw),
            lambda: split_tiles(c, "o1", hi, lo, NLAT, dram=io["od"]),
            lambda: project(c, "o1", io["na_w_out"], 0, KT // 2, hi, lo, wbuf, LAT_CHUNKS,
                            residual=(mod[:, 1], io["xt"], xt)),
            lambda: finish(c, io, consts, xt),
        ]
        for step in steps[:stop]:
            step()


_INS = ['x', 'c', 'ctx', 'c_ctx', 'mod_w', 'mod_b', 'norm_g', 'final_g', 'ga_w_in', 'ga_q_g', 'ga_k_g', 'ga_w_out',
        'na_w_in', 'na_w_out']


def kernel(**inputs):
    import numpy as _np
    import concourse.bacc as _bacc
    from concourse import mybir as _mybir
    from concourse.bass_utils import run_bass_kernel_spmd as _run

    nc = _bacc.Bacc("TRN2", target_bir_lowering=False, num_devices=1)
    cos, sin = rope_tables()
    mask_cols, mask_mid = window_masks()
    arrays = {n: _np.ascontiguousarray(inputs[n]) for n in _INS}
    wide = GRID_W - KW
    arrays["bias"] = _np.pad(_np.asarray(inputs["na_rpb"])[0], ((0, 0), (0, 0), (wide, wide)))
    arrays |= {"cos": cos, "sin": sin, "mask_cols": mask_cols, "mask_mid": mask_mid}
    io, in_map = {}, {}
    for name, a in arrays.items():
        if name.startswith(("ga_w", "na_w")):
            a = a[0]
        in_map[f"in_{name}"] = a
        io[name] = nc.dram_tensor(f"in_{name}", a.shape, _mybir.dt.from_np(a.dtype), kind="ExternalInput").ap()
    io["out"] = nc.dram_tensor("out", (1, NLAT, D), F32, kind="ExternalOutput").ap()
    backbone(nc, io)
    r = _run(nc, [in_map], core_ids=[0])
    return r.results[0]["out"]
```

```python
from contextlib import ExitStack, contextmanager

import numpy as np

import concourse.bass as bass
from concourse import mybir

ALU = mybir.AluOpType
ACT = mybir.ActivationFunctionType
F32 = mybir.dt.float32
F32R = mybir.dt.float32r
AX = mybir.AxisListType.X

P = 128
D = 1024
KT = D // P
NCTX, NLAT = 256, 1024
T = NCTX + NLAT
TT = T // P
CT = NCTX // P
GRID_W = 64
EPS = 1e-6
THETA = 10000.0

HD = 128
QH, KVH = 8, 2
GROUP = QH // KVH
NH, ND = 16, 64
KH, KW = 8, 16
ROWS = NLAT // GRID_W
MASKED = -1e30
BIAS_ROWS, BIAS_W = 2 * KH - 1, 2 * GRID_W - 1
SKEW_W = BIAS_W + GRID_W - 1
END_SLOTS = range(1, 15)
MID_SLOTS = range(3, 12)

ALL_CHUNKS = [(0, NCTX), (NCTX, 512), (NCTX + 512, 512)]
LAT_CHUNKS = [(NCTX, 512), (NCTX + 512, 512)]


def rope_tables():
    nf = HD // 4
    inv = (np.float32(THETA) ** (-np.arange(nf, dtype=np.float32) / np.float32(nf))).astype(np.float32)
    t = np.arange(NLAT)
    row, col = (t // GRID_W).astype(np.float32), (t % GRID_W).astype(np.float32)
    ar, ac = row[:, None] * inv, col[:, None] * inv
    ang = np.concatenate([ar, ar, ac, ac], axis=-1).T
    cos, sin = np.ones((HD, T), np.float32), np.zeros((HD, T), np.float32)
    sign = np.where((np.arange(HD) // nf) % 2 == 0, -1.0, 1.0).astype(np.float32)[:, None]
    cos[:, NCTX:], sin[:, NCTX:] = np.cos(ang), np.sin(ang) * sign
    return cos, sin


def window_masks():
    q = np.arange(P) % GRID_W
    start = np.clip(q - KW // 2, 0, GRID_W - KW)[:, None]
    k = np.arange(GRID_W)[None]
    cols = np.where((k >= start) & (k < start + KW), 0.0, MASKED).astype(np.float32)
    mid = np.repeat(cols[:, None], len(MID_SLOTS), axis=1)
    mid[P // 2:, 0] = MASKED
    mid[:P // 2, -1] = MASKED
    return cols, mid


AREA_H = (0, 80)
AREA_X = (80, 120)
AREA_MID = (120, 160)
AREA_W = (160, 199)
AREA_QKV = (80, 170)
AREA_STAGE = (184, 199)
AREA_CONST = (199, 207)


class Core:

    BASE = 17 * 1024

    def __init__(self, nc, stack):
        self.nc, self.stack, self.top = nc, stack, stack
        self.free = []
        self.sems, self.old_sems = [], []

    def sb(self, name, shape, dt=F32):
        size = int(np.prod(shape[1:])) * 4
        size = (size + 63) // 64 * 64
        for r in self.free:
            if r[0] + size <= r[1]:
                at = r[0]
                r[0] += size
                return self.nc.alloc_sbuf_tensor_at(name, shape, dt, offset=at)
        raise ValueError(f"{name}: {size} bytes in {self.free}")

    def ps(self, name, shape):
        return self.stack.enter_context(self.nc.psum_tensor(name, shape, F32))

    def sem(self, name):
        self.sems.append(self.nc.alloc_semaphore(name=name))
        return self.sems[-1]

    @contextmanager
    def block(self):
        with self.nc.Block() as block:
            old = self.old_sems

            @block.gpsimd
            def _(pool):
                for sem in old:
                    pool.sem_clear(sem)
            yield block
        for sem in old:
            self.nc.release_semaphore(sem)
        self.old_sems, self.sems = self.sems, []

    @contextmanager
    def scope(self, *ranges):
        keep = self.stack, self.free
        self.free = [[self.BASE + int(a * 1024), self.BASE + int(b * 1024)] for a, b in ranges]
        with ExitStack() as inner:
            self.stack = inner
            yield
        self.stack, self.free = keep



def load_and_modulate(c, io, consts, xt, mod, cols):
    nc = c.nc
    ident, ones = consts["ident"], consts["ones"]
    with c.scope(AREA_H, AREA_MID):
        xin = c.sb("xin", [P, TT, D])
        wmod = c.sb("wmod", [P, 3, 3 * D])
        vec = c.sb("vec_rows", [P, P])
        vec2 = c.sb("vec_rows2", [P, P])
        cs = c.sb("silu_cols", [P, 16])
        mrow = c.sb("mod_rows", [2, 2, 3 * D])
        tps = c.ps("tps", [P, 2, 512])
        mps = c.ps("mps", [P, 6, 512])
        cst, cst0 = c.sem("const_ready"), c.sem("const_zeroed")
        s_vec, s_x, s_w = c.sem("vec_loaded"), c.sem("x_loaded"), [c.sem(f"wmod_loaded{i}") for i in range(3)]
        silu, turned, taken, csd = c.sem("silu_done"), c.sem("turned"), c.sem("turn_taken"), c.sem("cs_done")
        mm, rows, colst, colsd = c.sem("mod_mm"), c.sem("mod_rows_done"), c.sem("mod_turned"), c.sem("mod_cols_done")
        msem, stored = c.sem("mod_step"), c.sem("xt_stored")
        vt, vd = c.sem("vec_turned"), c.sem("vec_taken")

        with c.block() as block:
            @block.gpsimd
            def _(pool):
                pool.memset(ones[:, :], 1.0).then_inc(cst, 1)
                pool.memset(ident[:, :], 0.0).then_inc(cst0, 1)
                pool.memset(consts["eps"][:, :], EPS).then_inc(cst, 1)
                pool.memset(consts["sel"][:, :], 0.0).then_inc(cst0, 1)
                pool.memset(consts["spread"][:, :, :], 1.0).then_inc(cst0, 1)
                pool.wait_ge(cst0, 3)
                pool.affine_select(out=ident[:, :], in_=ident[:, :], compare_op=ALU.not_equal, fill=1.0,
                                   base=0, pattern=[[-1, P]], channel_multiplier=1).then_inc(cst, 1)
                pool.memset(consts["sel"][:, QH + KVH - 1:QH + KVH], 1.0).then_inc(cst, 1)
                pool.affine_select(out=consts["spread"][:, :, :], in_=consts["spread"][:, :, :],
                                   compare_op=ALU.is_equal, fill=0.0, base=0,
                                   pattern=[[-1, QH + KVH], [0, P]], channel_multiplier=1).then_inc(cst, 1)

            @block.sync
            def _(sp):
                row = lambda a, n: a.rearrange("(r p) -> r p", p=P) if n else a
                sp.dma_start(vec[0:8, :], io["c"].rearrange("a (r p) -> (a r) p", p=P)).then_inc(s_vec, 16)
                sp.dma_start(vec[8:16, :], io["c_ctx"].rearrange("(r p) -> r p", p=P)).then_inc(s_vec, 16)
                sp.dma_start(vec2[0:48, :], io["mod_b"].rearrange("l (r p) -> (l r) p", p=P)).then_inc(s_vec, 16)
                sp.dma_start(vec2[48:64, :], io["norm_g"].rearrange("l (r p) -> (l r) p", p=P)).then_inc(s_vec, 16)
                sp.dma_start(vec2[64:65, :], io["ga_q_g"]).then_inc(s_vec, 16)
                sp.dma_start(vec2[65:66, :], io["ga_k_g"]).then_inc(s_vec, 16)
                for t in range(TT):
                    src = io["ctx"][0, t * P:(t + 1) * P] if t < CT else io["x"][0, (t - CT) * P:(t - CT + 1) * P]
                    sp.dma_start(xin[:, t, :], src).then_inc(s_x, 16)
                for n in range(2 * KT):
                    l, k = n // KT, n % KT
                    if n >= 3:
                        sp.wait_ge(mm, n - 2)
                    sp.dma_start(wmod[:, n % 3, :], io["mod_w"][l, k * P:(k + 1) * P, :]).then_inc(s_w[n % 3], 16)
                sp.wait_ge(taken, 2 * TT)
                sp.dma_start(io["xt"], xt[:, :, :]).then_inc(stored, 16)
                sp.wait_ge(stored, 16)

            @block.tensor
            def _(pe):
                pe.wait_ge(cst, 5)
                pe.wait_ge(silu, 1)
                pe.transpose(mps[:, 0, 0:16], vec[0:16, :], ident[0:16, 0:16]).then_inc(vt, 1)
                pe.transpose(mps[:, 1, 0:66], vec2[0:66, :], ident[0:66, 0:66]).then_inc(vt, 1)
                for t in range(TT):
                    pe.wait_ge(s_x, 16 * TT)
                    for b in range(2):
                        n = 2 * t + b
                        if n >= 2:
                            pe.wait_ge(taken, n - 1)
                        for k in range(4):
                            last = pe.transpose(tps[:, b, k * P:(k + 1) * P],
                                                xin[:, t, (4 * b + k) * P:(4 * b + k + 1) * P], ident[:, :])
                        last.then_inc(turned, 1)
                pe.wait_ge(csd, 2)
                for l in range(2):
                    for k in range(KT):
                        n = l * KT + k
                        pe.wait_ge(s_w[n % 3], 16 * (n // 3 + 1))
                        if l and k == 0:
                            pe.wait_ge(rows, 1)
                        for j in range(6):
                            last = pe.matmul(mps[0:2, j, :], cs[:, k:16:KT], wmod[:, n % 3, j * 512:(j + 1) * 512],
                                             start=(k == 0), stop=(k == KT - 1))
                        last.then_inc(mm, 1)
                    pe.wait_ge(rows, l + 1)
                    pe.wait_ge(taken, 2 * TT)
                    if l:
                        pe.wait_ge(colsd, 1)
                    for j in range(24):
                        last = pe.transpose(tps[:, 0, 2 * j:2 * j + 2], mrow[:, l, j * P:(j + 1) * P],
                                            ident[0:2, 0:2])
                    last.then_inc(colst, 1)

            @block.scalar
            def _(act):
                act.wait_ge(s_vec, 16 * 6)
                act.activation(vec[0:16, :], vec[0:16, :], ACT.Silu).then_inc(silu, 1)
                for t in range(TT):
                    act.wait_ge(turned, 2 * t + 1)
                    if t:
                        act.wait_ge(taken, 2 * t)
                    act.copy(xt[:, 0:4, t * P:(t + 1) * P],
                             tps[:, 0, :].rearrange("p (k q) -> p k q", k=4)).then_inc(taken, 1)

            @block.vector
            def _(dve):
                dve.wait_ge(vt, 2)
                dve.tensor_copy(cs[:, :], mps[:, 0, 0:16]).then_inc(csd, 1)
                dve.tensor_copy(cols[:, :], mps[:, 1, 0:66]).then_inc(csd, 1)
                for t in range(TT):
                    dve.wait_ge(turned, 2 * t + 2)
                    dve.wait_ge(taken, 2 * t + 1)
                    dve.tensor_copy(xt[:, 4:8, t * P:(t + 1) * P],
                                    tps[:, 1, :].rearrange("p (k q) -> p k q", k=4)).then_inc(taken, 1)
                for l in range(2):
                    dve.wait_ge(mm, (l + 1) * KT)
                    dve.tensor_copy(mrow[:, l, :].rearrange("p (j n) -> p j n", j=6), mps[0:2, :, :]).then_inc(rows, 1)
                    dve.wait_ge(colst, l + 1)
                    dve.wait_ge(csd, 2)
                    dve.tensor_tensor(mod[:, l, :, :], tps[:, 0, 0:48].rearrange("p (j s) -> p j s", s=2),
                                      cols[:, 24 * l:24 * l + 24].unsqueeze(2).broadcast_to([P, 24, 2]),
                                      ALU.add).then_inc(colsd, 1)
                    dve.wait_ge(colsd, l + 1)
                    for s in range(2):
                        dve.scalar_tensor_tensor(out=mod[:, l, 8:16, s], in0=mod[:, l, 8:16, s], scalar=1.0,
                                                 in1=cols[:, 48 + 8 * l:56 + 8 * l], op0=ALU.add,
                                                 op1=ALU.mult).then_inc(msem, 1)



def normalise(c, io, consts, l, xt, hi, lo, mod, store):
    nc = c.nc
    parts = [(0, NCTX, 1), (NCTX, NLAT, 0)]
    with c.scope(AREA_MID):
        sq = c.sb(f"sq{l}", [P, 2, T])
        rb = c.sb(f"rb{l}", [P, T])
        t_ = c.sb(f"nt{l}", [P, 2, T])
        sps = c.ps(f"sps{l}", [P, 3, 512])
        sqd, summed, rooted, recd = (c.sem(f"{x}{l}") for x in ("sq_done", "summed", "rooted", "recip_done"))
        scaled, his, los, stored = (c.sem(f"{x}{l}") for x in ("scaled", "h_hi", "h_lo", "x_stored"))
        with c.block() as block:
            @block.sync
            def _(sp):
                if store:
                    sp.dma_start(io["xt"], xt[:, :, :]).then_inc(stored, 16)
                    sp.wait_ge(stored, 16)

            @block.scalar
            def _(act):
                for k in range(KT):
                    if k >= 2:
                        act.wait_ge(summed, k - 1)
                    act.activation(sq[:, k % 2, :], xt[:, k, :], ACT.Square).then_inc(sqd, 1)
                act.wait_ge(summed, KT)
                for j, (a, n) in enumerate(ALL_CHUNKS):
                    act.activation(rb[:, a:a + n], sps[:, j, 0:n], ACT.Sqrt, bias=consts["eps"][:, :],
                                   scale=1.0 / D).then_inc(rooted, 1)
                for k in range(KT):
                    for j, (a, n, s) in enumerate(parts):
                        act.wait_ge(scaled, 2 * k + j + 1)
                        act.activation(hi[:, k, a:a + n], t_[:, k % 2, a:a + n], ACT.Identity,
                                       bias=mod[:, l, k, s:s + 1]).then_inc(his, 1)

            @block.tensor
            def _(pe):
                for k in range(KT):
                    pe.wait_ge(sqd, k + 1)
                    for j, (a, n) in enumerate(ALL_CHUNKS):
                        last = pe.matmul(sps[:, j, 0:n], consts["ones"][:, :], sq[:, k % 2, a:a + n],
                                         start=(k == 0), stop=(k == KT - 1))
                    last.then_inc(summed, 1)

            @block.vector
            def _(dve):
                dve.wait_ge(rooted, 3)
                dve.reciprocal(rb[:, :], rb[:, :]).then_inc(recd, 1)
                dve.wait_ge(recd, 1)
                def low(k):
                    for j, (a, n, s) in enumerate(parts):
                        dve.wait_ge(his, 2 * k + j + 1)
                        dve.scalar_tensor_tensor(out=lo[:, k, a:a + n], in0=t_[:, k % 2, a:a + n],
                                                 scalar=mod[:, l, k, s:s + 1], in1=hi[:, k, a:a + n],
                                                 op0=ALU.add, op1=ALU.subtract).then_inc(los, 1)
                for k in range(KT):
                    for j, (a, n, s) in enumerate(parts):
                        if k >= 2:
                            dve.wait_ge(los, 2 * (k - 2) + j + 1)
                        dve.scalar_tensor_tensor(out=t_[:, k % 2, a:a + n], in0=xt[:, k, a:a + n],
                                                 scalar=mod[:, l, 8 + k, s:s + 1], in1=rb[:, a:a + n],
                                                 op0=ALU.mult, op1=ALU.mult).then_inc(scaled, 1)
                    if k:
                        low(k - 1)
                low(KT - 1)



def project(c, tag, w, col0, pairs, hi, lo, wbuf, chunks, func=None, scale=1.0, dest=None, dram=None,
            residual=None):
    nc = c.nc
    raw, whi, wlo = wbuf
    width = sum(n for _, n in chunks)
    tok0 = chunks[0][0]
    with c.scope(AREA_STAGE):
        ps = c.ps(f"pp{tag}", [P, 2, 3, 512])
        loaded, w_hi, w_lo, mm = (c.sem(f"{x}_{tag}") for x in ("w_loaded", "w_hi", "w_lo", "mm_done"))
        out_done = c.sem(f"out_done_{tag}")
        stored = [c.sem(f"stored_{tag}_{s}") for s in range(2)]
        x_in = [c.sem(f"x_in_{tag}_{s}") for s in range(2)]
        stage = c.sb(f"stage{tag}", [P, 2, width]) if dram is not None or residual else None
        lanes = [(j, a, n, sum(m for _, m in chunks[:j])) for j, (a, n) in enumerate(chunks)]

        with c.block() as block:
            def load(sp, i):
                cols = bass.ds(col0 + i * 256, 256)
                sp.dma_start(raw[:, :, :], w[:, cols].rearrange("(k p) n -> p k n", p=P)).then_inc(loaded, 16)

            @block.sync
            def _(sp):
                load(sp, 0)
                def rest(i):
                    sp.wait_ge(w_lo, 2 * i + 2)
                    load(sp, i + 1)
                def stores(i):
                    for s in range(2):
                        if dram is not None:
                            sp.wait_ge(out_done, 2 * i + s + 3)
                            sp.dma_start(dram[bass.ds(2 * i + s, 1), :, 0:width].rearrange("a p n -> p (a n)"),
                                         stage[:, s, :]).then_inc(stored[s], 16)
                def fetch(i):
                    for s in range(2):
                        sp.wait_ge(out_done, 2 * i + s + 1)
                        sp.dma_start(stage[:, s, :], residual[1][:, bass.ds(2 * i + s, 1), tok0:tok0 + width]
                                     .rearrange("p a n -> p (a n)")).then_inc(x_in[s], 16)
                if residual:
                    fetch(0)
                if pairs > 1:
                    with sp.Fori(0, pairs - 1) as i:
                        rest(i)
                        stores(i)
                        if residual:
                            fetch(i + 1)
                stores(pairs - 1)
                if dram is not None:
                    for s in range(2):
                        sp.wait_ge(stored[s], 16 * pairs + 16)

            @block.scalar
            def _(act):
                if not residual:
                    act.sem_inc(out_done, 2)
                def high(i, s):
                    act.wait_ge(loaded, 16 * i + 16)
                    act.copy(whi[:, :, s * P:(s + 1) * P], raw[:, :, s * P:(s + 1) * P]).then_inc(w_hi, 1)
                def out(i, s):
                    if residual:
                        act.wait_ge(mm, 2 * i + s + 1)
                        return
                    act.wait_ge(mm, 2 * i + s + 1)
                    if dram is not None:
                        act.wait_ge(stored[s], 16 * i + 16)
                    for j, a, n, o in lanes:
                        if dram is not None:
                            to = stage[:, s, o:o + n]
                        else:
                            to = dest[:, bass.ds(2 * i + s, 1), o:o + n].rearrange("p a n -> p (a n)")
                        last = act.activation(to, ps[:, s, j, 0:n], func, scale=scale)
                    last.then_inc(out_done, 1)
                high(0, 0)
                high(0, 1)
                if pairs > 1:
                    with act.Fori(0, pairs - 1) as i:
                        for s in range(2):
                            out(i, s)
                            high(i + 1, s)
                for s in range(2):
                    out(pairs - 1, s)

            @block.vector
            def _(dve):
                if residual:
                    dve.sem_inc(out_done, 2)
                gate, _, dst = residual or (None, None, None)
                def low(i, s):
                    dve.wait_ge(w_hi, 2 * i + s + 1)
                    dve.tensor_tensor(wlo[:, :, s * P:(s + 1) * P], raw[:, :, s * P:(s + 1) * P],
                                      whi[:, :, s * P:(s + 1) * P], ALU.subtract).then_inc(w_lo, 1)
                def add(i, s):
                    dve.wait_ge(mm, 2 * i + s + 1)
                    dve.wait_ge(x_in[s], 16 * i + 16)
                    m = bass.ds(2 * i + s, 1)
                    for j, a, n, o in lanes:
                        dve_gate = gate[:, bass.ds(16 + 2 * i + s, 1), 1 if a < NCTX else 0]
                        last = dve.scalar_tensor_tensor(
                            out=dst[:, m, a:a + n].rearrange("p a n -> p (a n)"), in0=ps[:, s, j, 0:n],
                            scalar=dve_gate, in1=stage[:, s, o:o + n], op0=ALU.mult, op1=ALU.add)
                    last.then_inc(out_done, 1)
                if not residual:
                    with dve.Fori(0, pairs) as i:
                        low(i, 0)
                        low(i, 1)
                else:
                    low(0, 0)
                    low(0, 1)
                    with dve.Fori(0, pairs - 1) as i:
                        for s in range(2):
                            add(i, s)
                            low(i + 1, s)
                    add(pairs - 1, 0)
                    add(pairs - 1, 1)

            @block.gpsimd
            def _(pool):
                if dram is not None:
                    for s in range(2):
                        pool.sem_inc(stored[s], 16)

            @block.tensor
            def _(pe):
                with pe.Fori(0, pairs) as i:
                    for s in range(2):
                        pe.wait_ge(w_lo, 2 * i + s + 1)
                        pe.wait_ge(out_done, 2 * i + s + 1)
                        for j, a, n, o in lanes:
                            for k in range(KT):
                                ws = slice(s * P, (s + 1) * P)
                                acc = ps[:, s, j, 0:n]
                                pe.matmul(acc, whi[:, k, ws], hi[:, k, a:a + n], start=(k == 0), stop=False)
                                pe.matmul(acc, whi[:, k, ws], lo[:, k, a:a + n], start=False, stop=False)
                                last = pe.matmul(acc, wlo[:, k, ws], hi[:, k, a:a + n], start=False,
                                                 stop=(k == KT - 1))
                        last.then_inc(mm, 1)


def project_values(c, tag, w, col0, blocks, hi, lo, wbuf, dest=None, split=None):
    nc = c.nc
    raw, whi, wlo = wbuf
    with c.scope():
        ps = c.ps(f"pv{tag}", [P, 2, 512])
        loaded, w_hi, w_lo, mm = (c.sem(f"{x}_{tag}") for x in ("vw_loaded", "vw_hi", "vw_lo", "vmm_done"))
        out_hi, out_lo = c.sem(f"v_hi_{tag}"), c.sem(f"v_done_{tag}")
        with c.block() as block:
            def load(sp, i):
                sp.dma_start(raw[:, :, :], w[:, bass.ds(col0 + i * 256, 256)]
                             .rearrange("(k p) n -> p k n", p=P)).then_inc(loaded, 16)

            @block.sync
            def _(sp):
                load(sp, 0)
                if blocks > 1:
                    with sp.Fori(0, blocks - 1) as i:
                        sp.wait_ge(w_lo, i + 1)
                        load(sp, i + 1)

            @block.scalar
            def _(act):
                with act.Fori(0, blocks) as i:
                    act.wait_ge(loaded, 16 * i + 16)
                    act.wait_ge(out_lo, TT * i + 2)
                    act.copy(whi[:, :, :], raw[:, :, :]).then_inc(w_hi, 1)
                    if split:
                        for t in range(TT):
                            act.wait_ge(mm, TT * i + t + 1)
                            act.copy(split[0][:, t, :], ps[:, t % 2, 0:256]).then_inc(out_hi, 1)

            @block.vector
            def _(dve):
                dve.sem_inc(out_lo, 2)
                with dve.Fori(0, blocks) as i:
                    dve.wait_ge(w_hi, i + 1)
                    dve.tensor_tensor(wlo[:, :, :], raw[:, :, :], whi[:, :, :], ALU.subtract).then_inc(w_lo, 1)
                    for t in range(TT):
                        if split:
                            dve.wait_ge(out_hi, TT * i + t + 1)
                            dve.tensor_tensor(split[1][:, t, :], ps[:, t % 2, 0:256], split[0][:, t, :],
                                              ALU.subtract).then_inc(out_lo, 1)
                        else:
                            dve.wait_ge(mm, TT * i + t + 1)
                            dve.tensor_copy(dest[:, t, bass.ds(i * 256, 256)], ps[:, t % 2, 0:256]).then_inc(out_lo, 1)

            @block.tensor
            def _(pe):
                with pe.Fori(0, blocks) as i:
                    pe.wait_ge(w_lo, i + 1)
                    for t in range(TT):
                        pe.wait_ge(out_lo, TT * i + t + 1)
                        acc = ps[:, t % 2, 0:256]
                        for k in range(KT):
                            tok = slice(t * P, (t + 1) * P)
                            pe.matmul(acc, hi[:, k, tok], whi[:, k, :], start=(k == 0), stop=False)
                            pe.matmul(acc, hi[:, k, tok], wlo[:, k, :], start=False, stop=False)
                            last = pe.matmul(acc, lo[:, k, tok], whi[:, k, :], start=False, stop=(k == KT - 1))
                        last.then_inc(mm, 1)



def norm_and_rotate(c, io, consts, cols, qk, khi, klo):
    nc = c.nc
    N = QH + KVH
    with c.scope(AREA_H):
        sq = c.sb("qsq", [P, 2, T])
        rs = c.sb("qrs", [N, T])
        cos, sin = c.sb("cos", [P, T]), c.sb("sin", [P, T])
        rot = c.sb("rot", [P, 2, T])
        cq = c.sb("q_cos", [P, 2, T])
        pa, pb = c.ps("qpa", [P, 3, 512]), c.ps("qpb", [P, 3, 512])
        pab = [pa, pb]
        swapped = [c.sem(f"swapped{s}") for s in range(2)]
        tabs, sqd, summed, rooted, recd = (c.sem(x) for x in ("tables_in", "qsq_done", "qsummed", "qrooted", "qrecip"))
        gsc, spread, normed, cosd, sind, done, khd, kld = (c.sem(x) for x in (
            "qgain", "spread_done", "normed", "cos_done", "sin_done", "rotated", "k_hi", "k_lo"))
        with c.block() as block:
            @block.sync
            def _(sp):
                sp.dma_start(cos[:, :], io["cos"]).then_inc(tabs, 16)
                sp.dma_start(sin[:, :], io["sin"]).then_inc(tabs, 16)
                for m in range(N):
                    sp.wait_ge(normed, 3 * (m + 1))
                    if m >= 2:
                        sp.wait_ge(done, m - 1)
                    for b in range(4):
                        f = b ^ 1
                        sp.dma_start(rot[32 * b:32 * b + 32, m % 2, :],
                                     qk[32 * f:32 * f + 32, m, :]).then_inc(swapped[m % 2], 16)

            @block.scalar
            def _(act):
                for m in range(N):
                    if m >= 2:
                        act.wait_ge(summed, m - 1)
                    act.activation(sq[:, m % 2, :], qk[:, m, :], ACT.Square).then_inc(sqd, 1)
                act.wait_ge(summed, N)
                for j, (a, n) in enumerate(ALL_CHUNKS):
                    act.activation(rs[:, a:a + n], pb[0:N, j, 0:n], ACT.Sqrt, bias=consts["eps"][0:N, :],
                                   scale=1.0 / HD).then_inc(rooted, 1)
                for m in range(KVH):
                    act.wait_ge(done, QH + m + 1)
                    act.copy(khi[:, m, :], qk[:, QH + m, :]).then_inc(khd, 1)

            @block.tensor
            def _(pe):
                for m in range(N):
                    pe.wait_ge(sqd, m + 1)
                    for j, (a, n) in enumerate(ALL_CHUNKS):
                        last = pe.matmul(pb[0:N, j, 0:n], consts["sel"][:, N - 1 - m:2 * N - 1 - m],
                                         sq[:, m % 2, a:a + n], start=(m == 0), stop=(m == N - 1))
                    last.then_inc(summed, 1)
                pe.wait_ge(recd, 1)
                for m in range(N):
                    if m >= 2:
                        pe.wait_ge(normed, 3 * (m - 1))
                    for j, (a, n) in enumerate(ALL_CHUNKS):
                        last = pe.matmul(pab[m % 2][:, j, 0:n], consts["spread"][0:N, m, :], rs[:, a:a + n],
                                         start=True, stop=True)
                    last.then_inc(spread, 1)

            @block.vector
            def _(dve):
                dve.tensor_scalar(cols[:, 64:65], cols[:, 64:65], HD ** -0.5, None, ALU.mult).then_inc(gsc, 1)
                dve.wait_ge(rooted, 3)
                dve.reciprocal(rs[:, :], rs[:, :]).then_inc(recd, 1)
                dve.wait_ge(gsc, 1)
                dve.wait_ge(tabs, 32)
                def finish(m):
                    dve.wait_ge(swapped[m % 2], 64 * (m // 2 + 1))
                    dve.tensor_tensor(rot[:, m % 2, :], rot[:, m % 2, :], sin[:, :], ALU.mult).then_inc(sind, 1)
                    dve.wait_ge(cosd, m + 1)
                    dve.wait_ge(sind, m + 1)
                    dve.tensor_tensor(qk[:, m, :], cq[:, m % 2, :], rot[:, m % 2, :], ALU.add).then_inc(done, 1)
                    if m >= QH:
                        k = m - QH
                        dve.wait_ge(khd, k + 1)
                        dve.tensor_tensor(klo[:, k, :], qk[:, m, :], khi[:, k, :], ALU.subtract).then_inc(kld, 1)
                for m in range(N):
                    dve.wait_ge(spread, m + 1)
                    g = 64 if m < QH else 65
                    for j, (a, n) in enumerate(ALL_CHUNKS):
                        dve.scalar_tensor_tensor(out=qk[:, m, a:a + n], in0=qk[:, m, a:a + n],
                                                 scalar=cols[:, g:g + 1], in1=pab[m % 2][:, j, 0:n],
                                                 op0=ALU.mult, op1=ALU.mult).then_inc(normed, 1)
                    if m:
                        finish(m - 1)
                finish(N - 1)

            @block.gpsimd
            def _(pool):
                pool.wait_ge(tabs, 32)
                for m in range(N):
                    pool.wait_ge(normed, 3 * (m + 1))
                    if m >= 2:
                        pool.wait_ge(done, m - 1)
                    pool.tensor_tensor(cq[:, m % 2, :], qk[:, m, :], cos[:, :], ALU.mult).then_inc(cosd, 1)



GQA_TILES = [(NCTX + P * j, T) for j in range(NLAT // P)] + [(P * j, NCTX) for j in range(CT)]
GQA_N = len(GQA_TILES)
GQA_GROUPS = GQA_N // 2
S_RING = 5


def key_chunks(p):
    n = GQA_TILES[p % GQA_N][1]
    return [(a, min(512, n - a)) for a in range(0, n, 512)]


CHUNKS_BEFORE = [sum(len(key_chunks(q)) for q in range(p)) for p in range(GQA_N + 1)]
CHUNKS = CHUNKS_BEFORE[-1]


def chunk_no(p, k):
    return CHUNKS_BEFORE[p % GQA_N] + k + (p // GQA_N) * CHUNKS


def score_bank(p, k):
    return (3 * (p % GQA_N) + k) % S_RING


def bank_user_before(p, k):
    q, j = p, k
    while True:
        j -= 1
        if j < 0:
            q -= 1
            j = len(key_chunks(q)) - 1
        if score_bank(q, j) == score_bank(p, k):
            return chunk_no(q, j)


def at_least(eng, sem, per, h, no):
    if isinstance(h, int) and per * h + no + 1 <= 0:
        return
    eng.wait_ge(sem, h * per + (no + 1))


def grouped_attention(c, io, consts, qk, khi, klo, vhi, vlo):
    nc = c.nc
    with c.scope(AREA_H, (AREA_QKV[1], AREA_W[1])):
        qhi, qlo = c.sb("qhi", [P, T], F32R), c.sb("qlo", [P, T], F32R)
        prob = c.sb("prob", [P, 5, T])
        pthi = c.sb("pthi", [P, 2, TT, 256], F32R)
        ptlo = c.sb("ptlo", [P, 2, TT, 256], F32R)
        cthi = c.sb("cthi", [P, CT, 256], F32R)
        ctlo = c.sb("ctlo", [P, CT, 256], F32R)
        g = c.sb("gate_in", [P, T])
        inv = c.sb("inv_sums", [P, 256])
        mx, sums = c.sb("mx", [P, 5, 3]), c.sb("sums", [P, GQA_N, 3])
        nm, tot, rec = c.sb("nm", [P, 5]), c.sb("tot", [P, GQA_N]), c.sb("rec", [P, GQA_N])
        S, TB, O = c.ps("S", [P, S_RING, 512]), c.ps("TB", [P, 2, 512]), c.ps("O", [P, 512])
        q_hi, q_lo = c.sem("gq_hi"), c.sem("gq_lo")
        qkd, mxd, nmd, expd = c.sem("g_scores"), c.sem("g_max"), c.sem("g_negmax"), c.sem("g_exp")
        totd, recd, gated, invd = c.sem("g_total"), c.sem("g_recip"), c.sem("g_gated"), c.sem("g_inv")
        td, hid, lod = c.sem("g_turned"), c.sem("g_pt_hi"), c.sem("g_pt_lo")
        pvd, od, gl = c.sem("g_pv"), c.sem("g_out"), c.sem("g_gate_in")
        skewed = c.sem("bias_skewed")
        def pt(p):
            q = p % GQA_N
            half = slice((q % 2) * P, (q % 2) * P + P)
            if q >= 8:
                return cthi[:, :, half], ctlo[:, :, half]
            return pthi[:, (q // 2) % 2, :, half], ptlo[:, (q // 2) % 2, :, half]

        def pt_user_before(p):
            q, back = p % GQA_N, (p // GQA_N) * GQA_GROUPS
            gr = q // 2
            return back + {0: -3, 1: -2, 2: 0, 3: 1, 4: -1}[gr]

        def live(n, prev, tail):
            return (n >= 0 or prev) and not (tail and n >= 0)

        TAIL = 5

        Q0, Q1, QC = (NCTX, 512), (NCTX + 512, 512), (0, NCTX)

        def runs(eng, body, tail):
            body(0, 0, None)
            with eng.Fori(1, GROUP) as h:
                body(h, 0, 0)
            body(GROUP, 1, 0)
            with eng.Fori(GROUP + 1, QH) as h:
                body(h, 1, 1)
            tail(QH, KVH - 1)

        with c.block() as block:
            @block.sync
            def _(sp):
                def load(h):
                    at_least(sp, gated, GQA_GROUPS, h, -1)
                    sp.dma_start(g[:, :], io["gd"][bass.ds(h, 1), :, :].rearrange("a p n -> p (a n)")).then_inc(gl, 16)
                load(0)
                for head in range(NH):
                    src = bass.AP(tensor=io["bias"].tensor, offset=head * BIAS_ROWS * BIAS_W,
                                  ap=[[0, GRID_W], [BIAS_W, BIAS_ROWS], [1, BIAS_W]])
                    dst = bass.AP(tensor=io["skew"].tensor, offset=head * GRID_W * BIAS_ROWS * SKEW_W,
                                  ap=[[BIAS_ROWS * SKEW_W + 1, GRID_W], [SKEW_W, BIAS_ROWS], [1, BIAS_W]])
                    sp.dma_start(dst, src).then_inc(skewed, 16)
                with sp.Fori(1, QH) as h:
                    load(h)
                sp.wait_ge(skewed, 16 * NH)

            @block.tensor
            def _(pe):
                def scores(h, kv, p, k):
                    tok, _ = GQA_TILES[p]
                    a, n = key_chunks(p)[k]
                    if k == 0 and p in (0, 4, 8):
                        at_least(pe, q_lo, 3, h, (0, 4, 8).index(p))
                    at_least(pe, expd, CHUNKS, h, bank_user_before(p, k))
                    acc = S[:, score_bank(p, k), 0:n]
                    qs = slice(tok, tok + P)
                    pe.matmul(acc, qhi[:, qs], khi[:, kv, a:a + n], start=True, stop=False)
                    pe.matmul(acc, qhi[:, qs], klo[:, kv, a:a + n], start=False, stop=False)
                    pe.matmul(acc, qlo[:, qs], khi[:, kv, a:a + n], start=False, stop=True).then_inc(qkd, 1)

                def turn(h, p, k):
                    a, n = key_chunks(p)[k]
                    no = chunk_no(p, k)
                    at_least(pe, expd, CHUNKS, h, no)
                    at_least(pe, lod, CHUNKS, h, no - 2)
                    for b in range(n // P):
                        last = pe.transpose(TB[:, no % 2, b * P:(b + 1) * P],
                                            prob[:, p % 5, a + b * P:a + (b + 1) * P], consts["ident"][:, :])
                    last.then_inc(td, 1)

                def product(h, kv, gr, second, k):
                    q = (2 * gr + 1) % GQA_N
                    if q < 8:
                        blocks = [[range(0), range(0, 2), range(2, 5)], [range(5, 7), range(7, 9), range(9, 10)]][second][k]
                    else:
                        blocks = [[range(0), range(0), range(0, 1)], [range(0), range(0), range(1, 2)]][second][k]
                    if 0 in blocks:
                        at_least(pe, lod, CHUNKS, h, chunk_no(2 * gr + 1, len(key_chunks(q)) - 1))
                        at_least(pe, recd, GQA_GROUPS, h, gr)
                        at_least(pe, od, GQA_GROUPS, h, gr - 1)
                        for s in range(2):
                            pe.transpose(O[:, 256 + s * P:256 + (s + 1) * P],
                                         rec[:, q - 1 + s:q + s].broadcast_to([P, P]), consts["ident"][:, :])
                    n = GQA_TILES[q][1] // P
                    hi, lo = (cthi, ctlo) if q >= 8 else (pthi[:, (q // 2) % 2, :, :], ptlo[:, (q // 2) % 2, :, :])
                    for t in blocks:
                        vs = slice(kv * HD, (kv + 1) * HD)
                        pe.matmul(O[:, 0:256], vhi[:, t, vs], hi[:, t, :], start=(t == 0), stop=False)
                        pe.matmul(O[:, 0:256], vhi[:, t, vs], lo[:, t, :], start=False, stop=False)
                        last = pe.matmul(O[:, 0:256], vlo[:, t, vs], hi[:, t, :], start=False, stop=(t == n - 1))
                        if t == n - 1:
                            last.then_inc(pvd, 1)

                def body(h, kv, kvp, tail=False):
                    prev = kvp is not None
                    for p in range(TAIL - 1 if tail else GQA_N):
                        q, gr = p - 2, (p - 4) // 2
                        chunks = [] if tail else key_chunks(p)
                        turns = key_chunks(q) if live(q, prev, tail) else []
                        for k in range(3):
                            if k < len(turns):
                                turn(h, q, k)
                            if k < len(chunks):
                                scores(h, kv, p, k)
                            if live(gr, prev, tail):
                                product(h, kvp if gr < 0 else kv, gr, p % 2, k)
                runs(pe, body, lambda h, kv: body(h, kv, kv, tail=True))

            @block.vector
            def _(dve):
                def biggest(h, p, k):
                    a, n = key_chunks(p)[k]
                    at_least(dve, qkd, CHUNKS, h, chunk_no(p, k))
                    dve.tensor_reduce(mx[:, p % 5, k:k + 1], S[:, score_bank(p, k), 0:n], AX, ALU.max).then_inc(mxd, 1)

                def negmax(h, p):
                    n = len(key_chunks(p))
                    at_least(dve, mxd, CHUNKS, h, chunk_no(p, n - 1))
                    dve.tensor_reduce(nm[:, p % 5:p % 5 + 1], mx[:, p % 5, 0:n], AX, ALU.max,
                                      negate=True).then_inc(nmd, 1)

                def reciprocal(h, gr):
                    q = (2 * gr) % GQA_N
                    n = len(key_chunks(q))
                    at_least(dve, expd, CHUNKS, h, chunk_no(2 * gr + 1, n - 1))
                    dve.tensor_reduce(tot[:, q:q + 2], sums[:, q:q + 2, 0:n], AX, ALU.add).then_inc(totd, 1)
                    at_least(dve, totd, GQA_GROUPS, h, gr)
                    dve.reciprocal(rec[:, q:q + 2], tot[:, q:q + 2]).then_inc(recd, 1)

                def low(h, p, k):
                    a, n = key_chunks(p)[k]
                    no = chunk_no(p, k)
                    at_least(dve, hid, CHUNKS, h, no)
                    hi, lo = pt(p)
                    blocks = slice(a // P, (a + n) // P)
                    dve.tensor_tensor(lo[:, blocks, :], TB[:, no % 2, 0:n].rearrange("p (b q) -> p b q", q=P),
                                      hi[:, blocks, :], ALU.subtract).then_inc(lod, 1)

                def out(h, gr):
                    head = h - 1 if gr < 0 else h
                    tok = GQA_TILES[(2 * gr) % GQA_N][0]
                    at_least(dve, pvd, GQA_GROUPS, h, gr)
                    dve.tensor_copy(inv[:, :], O[:, 256:512]).then_inc(invd, 1)
                    at_least(dve, invd, GQA_GROUPS, h, gr)
                    dve.tensor_tensor(qk[:, bass.ds(head, 1), tok:tok + 256].rearrange("p a n -> p (a n)"),
                                      O[:, 0:256], inv[:, :], ALU.mult).then_inc(od, 1)

                def body(h, kv, kvp, tail=False):
                    prev = kvp is not None
                    for p in range(TAIL if tail else GQA_N):
                        q = p - 2
                        chunks = [] if tail else key_chunks(p)
                        turns = key_chunks(q) if live(q, prev, tail) else []
                        for k in range(3):
                            if k == 0 and p % 2 == 0 and live((p - 6) // 2, prev, tail):
                                out(h, (p - 6) // 2)
                            if k < len(turns):
                                low(h, q, k)
                            if k < len(chunks):
                                biggest(h, p, k)
                                if k == len(chunks) - 1:
                                    negmax(h, p)
                        if p % 2 == 1 and live((p - 3) // 2, prev, tail):
                            reciprocal(h, (p - 3) // 2)

                runs(dve, body, lambda h, kv: body(h, kv, kv, tail=True))

            @block.scalar
            def _(act):
                def q_high(h, piece, no, user, users_head):
                    a, n = piece
                    at_least(act, qkd, CHUNKS, users_head, user)
                    act.copy(qhi[:, a:a + n], qk[:, bass.ds(h, 1), a:a + n].rearrange("p a n -> p (a n)")).then_inc(q_hi, 1)

                def exps(h, p, k):
                    a, n = key_chunks(p)[k]
                    if k == 0:
                        at_least(act, nmd, GQA_N, h, p)
                        at_least(act, td, CHUNKS, h, chunk_no(p - 5, len(key_chunks(p - 5)) - 1))
                    act.activation(prob[:, p % 5, a:a + n], S[:, score_bank(p, k), 0:n], ACT.Exp,
                                   bias=nm[:, p % 5:p % 5 + 1],
                                   accum_out=sums[:, p % GQA_N, k:k + 1]).then_inc(expd, 1)

                def high(h, p, k):
                    a, n = key_chunks(p)[k]
                    no = chunk_no(p, k)
                    at_least(act, td, CHUNKS, h, no)
                    if k == 0:
                        at_least(act, pvd, GQA_GROUPS, h, pt_user_before(p))
                    hi, _ = pt(p)
                    act.copy(hi[:, a // P:(a + n) // P, :],
                             TB[:, no % 2, 0:n].rearrange("p (b q) -> p b q", q=P)).then_inc(hid, 1)

                def body(h, kv, kvp, tail=False):
                    prev = kvp is not None
                    for p in range(2 if tail else GQA_N):
                        q = p - 2
                        es = key_chunks(p - 1) if live(p - 1, prev, tail) else []
                        turns = key_chunks(q) if live(q, prev, tail) else []
                        for k in range(3):
                            if k < len(turns):
                                high(h, q, k)
                            if k < len(es):
                                exps(h, p - 1, k)
                        if not tail:
                            if p == 1:
                                q_high(h, Q1, 1, chunk_no(7, 2) - CHUNKS, h)
                            if p == 3:
                                q_high(h, QC, 2, chunk_no(9, 0) - CHUNKS, h)
                            if p == 5:
                                q_high(h + 1, Q0, 0, chunk_no(3, 2), h)

                q_high(0, Q0, 0, -1, 0)
                runs(act, body, lambda h, kv: body(h, kv, kv, tail=True))

            @block.gpsimd
            def _(pool):
                def q_low(h, piece, no):
                    a, n = piece
                    pool.wait_ge(q_hi, h * 3 + no + 1)
                    pool.tensor_tensor(qlo[:, a:a + n], qk[:, bass.ds(h, 1), a:a + n].rearrange("p a n -> p (a n)"),
                                       qhi[:, a:a + n], ALU.subtract).then_inc(q_lo, 1)

                def gate(h, gr):
                    head = h - 1 if gr < 0 else h
                    tok = GQA_TILES[(2 * gr) % GQA_N][0]
                    o = qk[:, bass.ds(head, 1), tok:tok + 256].rearrange("p a n -> p (a n)")
                    at_least(pool, gl, 1, 16 * head, 15)
                    at_least(pool, od, GQA_GROUPS, h, gr)
                    pool.tensor_tensor(o, o, g[:, tok:tok + 256], ALU.mult).then_inc(gated, 1)

                def body(h, kv, kvp, tail=False):
                    prev = kvp is not None
                    for p in range(TAIL if tail else GQA_N):
                        if p % 2 == 0 and live((p - 6) // 2, prev, tail):
                            gate(h, (p - 6) // 2)
                        if not tail:
                            if p == 1:
                                q_low(h, Q1, 1)
                            if p == 3:
                                q_low(h, QC, 2)
                            if p == 5:
                                q_low(h + 1, Q0, 0)

                q_low(0, Q0, 0)
                runs(pool, body, lambda h, kv: body(h, kv, kv, tail=True))



NA_TILES = 2 * (NLAT // P)
NA_GROUPS = NA_TILES // 2
NJ = NLAT // P


def first_row(j):
    return max(0, min(2 * j - KH // 2, ROWS - KH))


def is_mid(j):
    return first_row(j) != max(0, min(2 * j + 1 - KH // 2, ROWS - KH))


def group_base(gr):
    return first_row(2 * (gr % (NJ // 2))) // 2


def neighbourhood_attention(c, io, consts, vraw):
    nc = c.nc
    NE, NM = len(END_SLOTS), len(MID_SLOTS)
    with c.scope(AREA_H, (120, AREA_W[1])):
        q2, k2, g2 = c.sb("q2", [P, NLAT]), c.sb("k2", [P, T]), c.sb("g2", [P, NLAT])
        be, bm = c.sb("bias_end", [P, 2, NE, GRID_W]), c.sb("bias_mid", [P, 2, NM, GRID_W])
        mc, mm9 = c.sb("mask_cols", [P, GRID_W]), c.sb("mask_mid", [P, NM, GRID_W])
        qs = c.sb("q_split", [P, 2, NLAT], F32R)
        ka, kb = c.sb("k_split", [P, 2, T], F32R), c.sb("k_swapped", [P, 2, T], F32R)
        vs = c.sb("v_split", [P, 2, TT, P], F32R)
        prob = c.sb("nprob", [P, 4, 832])
        pe_hi, pe_lo = c.sb("pt_end_hi", [P, 2, 6, 256], F32R), c.sb("pt_end_lo", [P, 2, 6, 256], F32R)
        pm_hi, pm_lo = c.sb("pt_mid_hi", [P, 2, 8, 256], F32R), c.sb("pt_mid_lo", [P, 2, 8, 256], F32R)
        ost, half = c.sb("o_out", [P, NLAT]), c.sb("o_half", [P, 256])
        mx, nm = c.sb("nmx", [P, 4, 4]), c.sb("nnm", [P, 4])
        sums, rec = c.sb("nsums", [P, NA_TILES, 2]), c.sb("nrec", [P, NA_TILES])
        tot = c.sb("ntot", [P, 2])
        S, TB, O = c.ps("nS", [P, 2, 2, 512]), c.ps("nTB", [P, 2, 512]), c.ps("nO", [P, 2, 512])
        ql, kl, gl, ml = (c.sem(x) for x in ("n_q_in", "n_k_in", "n_g_in", "n_mask_in"))
        bl = [c.sem(f"n_bias_in{s}") for s in range(2)]
        swd = [c.sem(f"n_swapped{s}") for s in range(2)]
        hid_, lod_ = c.sem("n_split_hi"), c.sem("n_split_lo")
        bmd, zero = c.sem("n_bias_masked"), c.sem("n_zeroed")
        qkd, mxd, nmd, expd, totd, recd = (c.sem(x) for x in (
            "n_scores", "n_max", "n_negmax", "n_exp", "n_total", "n_recip"))
        td, hid, lod = (c.sem(x) for x in ("n_turned", "n_pt_hi", "n_pt_lo"))
        pvd, halfd, addd, gated, od, std = (c.sem(x) for x in (
            "n_pv", "n_half", "n_added", "n_gated", "n_out", "n_stored"))
        SPL, N, G = 6, NA_TILES, NA_GROUPS
        PAIRS = NH // 2

        def rows(s, lo):
            top = (s == 0) != lo
            return slice(0, 64) if top else slice(64, 128)

        def pt(p):
            gr = (p % N) // 2 % 4
            hs = slice((p % 2) * P, (p % 2) * P + P)
            if gr in (0, 3):
                return pe_hi[:, gr // 3, :, :], pe_lo[:, gr // 3, :, :], hs
            return pm_hi[:, gr - 1, :, :], pm_lo[:, gr - 1, :, :], hs

        def first_block(p):
            j = p % NJ
            return first_row(j) // 2 - group_base(j // 2)

        def ctx_block(p):
            return 6 if (p % N) // 2 % 4 in (1, 2) else 4

        def live(n, prev, tail):
            return (n >= 0 or prev) and not (tail and n >= 0)

        TAIL = 5

        def runs(eng, body):
            body(0, True, False)
            with eng.Fori(1, PAIRS - 1) as i:
                body(i, False, False)
            body(PAIRS - 1, False, True)

        with c.block() as block:
            @block.sync
            def _(sp):
                def qk_in(i):
                    src = lambda a: a[bass.ds(i, 1), :, :].rearrange("a p n -> p (a n)")
                    at_least(sp, lod_, SPL, i, -2)
                    sp.dma_start(q2[:, :], src(io["qd"][:, :, 0:NLAT])).then_inc(ql, 16)
                    sp.dma_start(k2[:, :], src(io["kd"])).then_inc(kl, 16)

                def swap(i, s):
                    at_least(sp, lod_, SPL, i, 3 * s + 1)
                    for b in range(2):
                        sp.dma_start(kb[64 * b:64 * b + 64, s, :].bitcast(F32),
                                     ka[64 * (1 - b):64 * (1 - b) + 64, s, :].bitcast(F32)).then_inc(swd[s], 16)

                def bias_in(i, s):
                    at_least(sp, mxd, N, i, 8 * s - 9)
                    head = 2 * i + s
                    for rr in range(2):
                        sp.dma_start(be[64 * rr:64 * rr + 64, s, :, :],
                                     io["skew"][bass.ds(head, 1), :, END_SLOTS[0] - rr:END_SLOTS[-1] + 1 - rr, GRID_W - 1:2 * GRID_W - 1]
                                     .rearrange("a c e w -> c (a e) w")).then_inc(bl[s], 16)

                def g_in(i):
                    at_least(sp, gated, G, i, -1)
                    sp.dma_start(g2[:, :], io["gd"][bass.ds(i, 1), :, 0:NLAT].rearrange("a p n -> p (a n)")).then_inc(gl, 16)

                def store(i):
                    at_least(sp, gated, G, i, G - 1)
                    sp.dma_start(io["od"][bass.ds(i, 1), :, :].rearrange("a p n -> p (a n)"), ost[:, :]).then_inc(std, 16)

                sp.dma_start(mc[:, :], io["mask_cols"]).then_inc(ml, 16)
                sp.dma_start(mm9[:, :, :], io["mask_mid"]).then_inc(ml, 16)
                qk_in(0)
                bias_in(0, 0)
                swap(0, 0)

                def body(i, first, last):
                    bias_in(i, 1)
                    swap(i, 1)
                    if not first:
                        store(i - 1)
                    g_in(i)
                    if not last:
                        qk_in(i + 1)
                        bias_in(i + 1, 0)
                        swap(i + 1, 0)
                runs(sp, body)
                store(PAIRS - 1)
                sp.wait_ge(std, 16 * PAIRS)

            @block.tensor
            def _(pe):
                def scores(i, p):
                    s, j = p // NJ, p % NJ
                    r0 = first_row(j)
                    if j == 0:
                        at_least(pe, swd[s], 32, i, 31)
                    at_least(pe, expd, 2 * N, i, 2 * (p - 2) + 1)
                    q = qs[:, s, j * P:(j + 1) * P]
                    loc = NCTX + r0 * GRID_W
                    out = [(S[:, p % 2, 1, 0:256], 0, NCTX), (S[:, p % 2, 0, 0:512], loc, 512)]
                    if is_mid(j):
                        out.insert(1, (S[:, p % 2, 1, 256:320], loc + 512, 64))
                    for acc, a, n in out:
                        pe.matmul(acc, q, ka[:, s, a:a + n], start=True, stop=False)
                        last = pe.matmul(acc, q, kb[:, s, a:a + n], start=False, stop=True)
                    last.then_inc(qkd, 1)

                def turn(i, p, k):
                    at_least(pe, lod, 2 * N, i, 2 * p + k - 2)
                    if k == 0:
                        at_least(pe, expd, 2 * N, i, 2 * p + 1)
                    for b in range(4 if k == 0 else 2):
                        a = k * 576 + b * P
                        last = pe.transpose(TB[:, k, b * P:(b + 1) * P], prob[:, p % 4, a:a + P], consts["ident"][:, :])
                    if k and is_mid(p % NJ):
                        last = pe.transpose(TB[0:64, 1, 256:384], prob[:, p % 4, 512:576], consts["ident"][:, :])
                    last.then_inc(td, 1)

                def product(i, gr, second):
                    s = (gr % G) // 4
                    if not second:
                        at_least(pe, lod, 2 * N, i, 2 * (2 * gr + 1) + 1)
                        at_least(pe, recd, G, i, gr)
                        at_least(pe, od, G, i, gr - 2)
                        if gr % 4 == 0:
                            at_least(pe, lod_, SPL, i, 3 * s + 2)
                        for r in range(2):
                            at = (2 * gr + r) % N
                            pe.transpose(O[:, gr % 2, 256 + r * P:256 + (r + 1) * P],
                                         rec[:, at:at + 1].broadcast_to([P, P]), consts["ident"][:, :])
                    hi, lo, _ = pt(2 * gr)
                    nloc = 6 if gr % 4 in (1, 2) else 4
                    keys = [(b, nloc + b) for b in range(CT)] + [(CT + group_base(gr) + b, b) for b in range(nloc)]
                    cut = len(keys) // 2
                    for n in range(cut, len(keys)) if second else range(cut):
                        v, b = keys[n]
                        pe.matmul(O[:, gr % 2, 0:256], vs[:, s, v, :], hi[:, b, :], start=(n == 0), stop=False)
                        last = pe.matmul(O[:, gr % 2, 0:256], vs[:, s, v, :], lo[:, b, :], start=False,
                                         stop=(n == len(keys) - 1))
                    if second:
                        last.then_inc(pvd, 1)

                def body(i, first, last, tail=False):
                    prev = not first
                    for p in range(TAIL - 1 if tail else N):
                        q, gr = p - 2, (p - 4) // 2
                        turns = live(q, prev, tail)
                        if turns:
                            turn(i, q, 0)
                        if not tail:
                            scores(i, p)
                        if turns:
                            turn(i, q, 1)
                        if live(gr, prev, tail):
                            product(i, gr, p % 2 == 1)
                pe.wait_ge(zero, 4)
                runs(pe, body)
                body(PAIRS, False, True, tail=True)

            def split_steps(i, first, last, p):
                if p in (1, 2, 6):
                    return [(i, 1, (1, 2, 6).index(p))]
                if p in (11, 12, 13) and not last:
                    return [(i + 1, 0, p - 11)]
                return []

            def parts(i, s, what):
                src, hi, lo = rows(s, False), rows(s, False), rows(s, True)
                if what == 0:
                    return q2[src, :], qs[hi, s, :], qs[lo, s, :]
                if what == 1:
                    return k2[src, :], ka[hi, s, :], ka[lo, s, :]
                v = vraw[:, :, bass.ds(i * P + s * ND, ND)]
                return v, vs[:, s, :, 0:ND], vs[:, s, :, ND:2 * ND]

            @block.scalar
            def _(act):
                def split(i, s, what):
                    if what == 0:
                        at_least(act, ql, 16, i, 15)
                        at_least(act, qkd, N, i, 8 * s + 7 - N)
                    if what == 1:
                        at_least(act, kl, 16, i, 15)
                    if what == 2:
                        at_least(act, pvd, G, i, 4 * s + 3 - G)
                    v, hi, _ = parts(i, s, what)
                    act.copy(hi, v).then_inc(hid_, 1)

                def exps(i, p):
                    at_least(act, nmd, N, i, p)
                    n = 576 if is_mid(p % NJ) else 512
                    b = nm[:, p % 4:p % 4 + 1]
                    pr = prob[:, p % 4, 0:n]
                    act.activation(pr, pr, ACT.Exp, bias=b, accum_out=sums[:, p % N, 0:1]).then_inc(expd, 1)
                    act.activation(prob[:, p % 4, 576:832], S[:, p % 2, 1, 0:256], ACT.Exp, bias=b,
                                   accum_out=sums[:, p % N, 1:2]).then_inc(expd, 1)

                def high(i, p, k):
                    at_least(act, td, 2 * N, i, 2 * p + k)
                    hi, _, hs = pt(p)
                    if k == 0:
                        at_least(act, pvd, G, i, p // 2 - 4)
                        b = first_block(p)
                        act.copy(hi[:, b:b + 4, hs], TB[:, 0, :].rearrange("p (b q) -> p b q", q=P)).then_inc(hid, 1)
                    else:
                        b = ctx_block(p)
                        if is_mid(p % NJ):
                            act.copy(hi[0:64, first_block(p) + 4, hs], TB[0:64, 1, 256:384])
                        act.copy(hi[:, b:b + 2, hs], TB[:, 1, 0:256].rearrange("p (b q) -> p b q", q=P)).then_inc(hid, 1)

                def fold(i, gr):
                    s = (gr % G) // 4
                    at_least(act, pvd, G, i, gr)
                    at_least(act, addd, G, i, gr - 1)
                    act.copy(half[rows(s, False), :], O[rows(s, True), gr % 2, 0:256]).then_inc(halfd, 1)

                def body(i, first, last, tail=False):
                    prev = not first
                    for p in range(TAIL if tail else N):
                        q = p - 2
                        if live(q, prev, tail):
                            high(i, q, 0)
                        if live(p - 1, prev, tail):
                            exps(i, p - 1)
                        if live(q, prev, tail):
                            high(i, q, 1)
                        if p % 2 == 0 and live((p - 6) // 2, prev, tail):
                            fold(i, (p - 6) // 2)
                        if not tail:
                            for a in split_steps(i, first, last, p):
                                split(*a)
                act.wait_ge(zero, 4)
                for what in range(3):
                    split(0, 0, what)
                runs(act, body)
                body(PAIRS, False, True, tail=True)

            @block.vector
            def _(dve):
                def biggest(i, p):
                    s, j = p // NJ, p % NJ
                    r0 = first_row(j)
                    if j == 0:
                        at_least(dve, bmd, 4, i, 2 * s + 1)
                    at_least(dve, qkd, N, i, p)
                    at_least(dve, td, 2 * N, i, 2 * (p - 4) + 1)
                    e = r0 - 2 * j + 7 - (MID_SLOTS[0] if is_mid(j) else END_SLOTS[0])
                    table = bm if is_mid(j) else be
                    sl = p % 4
                    dve.tensor_reduce(mx[:, sl, 2:3], S[:, p % 2, 1, 0:256], AX, ALU.max)
                    pieces = [(0, 512, S[:, p % 2, 0, 0:512], table[:, s, e:e + 8, :].rearrange("p e w -> p (e w)"))]
                    if is_mid(j):
                        pieces.append((512, 64, S[:, p % 2, 1, 256:320], table[:, s, e + 8, :]))
                    for n, (a, w, src, bias) in enumerate(pieces):
                        last = dve.tensor_tensor_reduce(out=prob[:, sl, a:a + w], in0=src, in1=bias, scale=1.0,
                                                        scalar=-3e38, op0=ALU.add, op1=ALU.max,
                                                        accum_out=mx[:, sl, 1 - n:2 - n])
                    last.then_inc(mxd, 1)
                    at_least(dve, mxd, N, i, p)
                    dve.tensor_reduce(nm[:, sl:sl + 1], mx[:, sl, 2 - len(pieces):3], AX, ALU.max,
                                      negate=True).then_inc(nmd, 1)

                def reciprocal(i, gr):
                    q = (2 * gr) % N
                    at_least(dve, expd, 2 * N, i, 2 * (2 * gr + 1) + 1)
                    dve.tensor_reduce(tot[:, :], sums[:, q:q + 2, :], AX, ALU.add).then_inc(totd, 1)
                    at_least(dve, totd, G, i, gr)
                    dve.reciprocal(rec[:, q:q + 2], tot[:, :]).then_inc(recd, 1)

                def low(i, p, k):
                    at_least(dve, hid, 2 * N, i, 2 * p + k)
                    hi, lo, hs = pt(p)
                    if k == 0:
                        b = first_block(p)
                        dve.tensor_tensor(lo[:, b:b + 4, hs], TB[:, 0, :].rearrange("p (b q) -> p b q", q=P),
                                          hi[:, b:b + 4, hs], ALU.subtract).then_inc(lod, 1)
                    else:
                        b = ctx_block(p)
                        if is_mid(p % NJ):
                            f = first_block(p) + 4
                            dve.tensor_tensor(lo[0:64, f, hs], TB[0:64, 1, 256:384], hi[0:64, f, hs], ALU.subtract)
                        dve.tensor_tensor(lo[:, b:b + 2, hs], TB[:, 1, 0:256].rearrange("p (b q) -> p b q", q=P),
                                          hi[:, b:b + 2, hs], ALU.subtract).then_inc(lod, 1)

                def out(i, gr):
                    s = (gr % G) // 4
                    r = rows(s, False)
                    a = (gr % 4) * 256
                    at_least(dve, halfd, G, i, gr)
                    if gr % G == 0:
                        at_least(dve, std, 16, i, -1)
                    dve.tensor_tensor(ost[r, a:a + 256], O[r, gr % 2, 0:256], half[r, :], ALU.add).then_inc(addd, 1)
                    at_least(dve, addd, G, i, gr)
                    dve.tensor_tensor(ost[r, a:a + 256], ost[r, a:a + 256], O[r, gr % 2, 256:512], ALU.mult).then_inc(od, 1)

                def body(i, first, last, tail=False):
                    prev = not first
                    for p in range(TAIL if tail else N):
                        q = p - 2
                        if live(q, prev, tail):
                            low(i, q, 0)
                        if not tail:
                            biggest(i, p)
                        if live(q, prev, tail):
                            low(i, q, 1)
                        if p % 2 == 0 and live((p - 6) // 2, prev, tail):
                            out(i, (p - 6) // 2)
                        if p % 2 == 1 and live((p - 3) // 2, prev, tail):
                            reciprocal(i, (p - 3) // 2)
                runs(dve, body)
                body(PAIRS, False, True, tail=True)

            @block.gpsimd
            def _(pool):
                for t in (pm_hi, pm_lo):
                    for gq in range(2):
                        last = pool.memset(t[:, gq, :, :].rearrange("p b q -> p (b q)").bitcast(F32), 0.0)
                        last.then_inc(zero, 1)

                def split(i, s, what):
                    at_least(pool, hid_, SPL, i, 3 * s + what)
                    if what == 1:
                        at_least(pool, swd[s], 32, i, -1)
                    v, hi, lo = parts(i, s, what)
                    pool.tensor_tensor(lo, v, hi, ALU.subtract).then_inc(lod_, 1)

                def mask(i, s):
                    at_least(pool, bl[s], 32, i, 31)
                    a = MID_SLOTS[0] - END_SLOTS[0]
                    pool.tensor_tensor(bm[:, s, :, :], be[:, s, a:a + NM, :], mm9[:, :, :], ALU.add).then_inc(bmd, 1)
                    at_least(pool, bmd, 4, i, 2 * s)
                    pool.tensor_tensor(be[:, s, :, :], be[:, s, :, :],
                                      mc[:, :].unsqueeze(1).broadcast_to([P, NE, GRID_W]), ALU.add).then_inc(bmd, 1)

                def gate(i, gr):
                    r = rows((gr % G) // 4, False)
                    a = (gr % 4) * 256
                    at_least(pool, od, G, i, gr)
                    if gr % G == 0:
                        at_least(pool, gl, 16, i, 15)
                    pool.tensor_tensor(ost[r, a:a + 256], ost[r, a:a + 256], g2[r, a:a + 256], ALU.mult).then_inc(gated, 1)

                def idle(i, splits, masks, gates):
                    at_least(pool, lod_, SPL, i, splits)
                    at_least(pool, bmd, 4, i, masks)
                    at_least(pool, gated, G, i, gates)

                def body(i, first, last, tail=False):
                    splits, masks, gates = 2, 1, -4
                    for p in range(TAIL if tail else N):
                        if p % 2 == 0:
                            if live((p - 6) // 2, not first, tail):
                                idle(i, splits if not tail else -1, masks if not tail else -1, gates)
                                gate(i, (p - 6) // 2)
                            gates = (p - 6) // 2
                        if tail:
                            continue
                        for a in split_steps(i, first, last, p):
                            idle(i, splits, masks, gates)
                            split(*a)
                            splits += 1
                        if p == 2 or p == 12 and not last:
                            idle(i, splits, masks, gates)
                            mask(*((i, 1) if p == 2 else (i + 1, 0)))
                            masks += 2
                pool.wait_ge(ml, 32)
                for what in range(3):
                    idle(0, what - 1, -1, -1)
                    split(0, 0, what)
                idle(0, 2, -1, -1)
                mask(0, 0)
                runs(pool, body)
                body(PAIRS, False, True, tail=True)



def split_tiles(c, tag, hi, lo, width, src=None, dram=None):
    nc = c.nc
    with c.scope(AREA_MID):
        raw = c.sb(f"raw{tag}", [P, 2, width]) if dram is not None else None
        il = [c.sem(f"s_in_{tag}_{s}") for s in range(2)]
        h, l = c.sem(f"s_hi_{tag}"), c.sem(f"s_lo_{tag}")
        part = (lambda k: raw[:, k % 2, :]) if dram is not None else (lambda k: src[:, k, :])
        with c.block() as block:
            @block.sync
            def _(sp):
                if dram is not None:
                    for k in range(KT):
                        if k >= 2:
                            sp.wait_ge(l, k - 1)
                        sp.dma_start(raw[:, k % 2, :], dram[k, :, 0:width]).then_inc(il[k % 2], 16)

            @block.scalar
            def _(act):
                for k in range(KT):
                    if dram is not None:
                        act.wait_ge(il[k % 2], 16 * (k // 2) + 16)
                    act.copy(hi[:, k, T - width:], part(k)).then_inc(h, 1)

            @block.vector
            def _(dve):
                for k in range(KT):
                    dve.wait_ge(h, k + 1)
                    dve.tensor_tensor(lo[:, k, T - width:], part(k), hi[:, k, T - width:], ALU.subtract).then_inc(l, 1)


def finish(c, io, consts, xt):
    nc = c.nc
    LT = NLAT // P
    with c.scope(AREA_H):
        fg = c.sb("final_gain", [P, D])
        xo, sq = c.sb("x_out", [P, 2, D]), c.sb("x_sq", [P, D])
        ss, rt, rc = c.sb("ss", [P, LT]), c.sb("rt", [P, LT]), c.sb("rc", [P, LT])
        ps = c.ps("fps", [P, 2, 2, 512])
        fgl, td, sd, rd, rcd, fd = (c.sem(x) for x in (
            "fg_in", "f_turned", "f_squared", "f_root", "f_recip", "f_done"))
        st = [c.sem(f"f_stored{s}") for s in range(2)]
        with c.block() as block:
            @block.sync
            def _(sp):
                sp.dma_start(fg[:, :], io["final_g"].rearrange("(a d) -> a d", a=1).broadcast_to([P, D])).then_inc(fgl, 16)
                for t in range(LT):
                    sp.wait_ge(fd, t + 1)
                    sp.dma_start(io["out"][0, t * P:(t + 1) * P, :], xo[:, t % 2, :]).then_inc(st[t % 2], 16)
                for s in range(2):
                    sp.wait_ge(st[s], 16 * LT // 2)

            @block.tensor
            def _(pe):
                for t in range(LT):
                    if t >= 2:
                        pe.wait_ge(fd, t - 1)
                    for k in range(KT):
                        last = pe.transpose(ps[:, t % 2, k // 4, (k % 4) * P:(k % 4 + 1) * P],
                                            xt[:, k, NCTX + t * P:NCTX + (t + 1) * P], consts["ident"][:, :])
                    last.then_inc(td, 1)

            @block.scalar
            def _(act):
                for t in range(LT):
                    act.wait_ge(td, t + 1)
                    if t:
                        act.wait_ge(sd, t)
                    act.activation(sq[:, :], ps[:, t % 2, :, :].rearrange("p a n -> p (a n)"), ACT.Square,
                                   accum_out=ss[:, t:t + 1]).then_inc(sd, 1)
                    act.wait_ge(sd, t + 1)
                    act.activation(rt[:, t:t + 1], ss[:, t:t + 1], ACT.Sqrt, bias=consts["eps"][:, :],
                                   scale=1.0 / D).then_inc(rd, 1)

            @block.vector
            def _(dve):
                dve.wait_ge(fgl, 16)
                for t in range(LT):
                    dve.wait_ge(rd, t + 1)
                    dve.reciprocal(rc[:, t:t + 1], rt[:, t:t + 1]).then_inc(rcd, 1)
                    dve.wait_ge(rcd, t + 1)
                    if t >= 2:
                        dve.wait_ge(st[t % 2], 16 * (t // 2))
                    dve.scalar_tensor_tensor(out=xo[:, t % 2, :], in0=ps[:, t % 2, :, :].rearrange("p a n -> p (a n)"),
                                             scalar=rc[:, t:t + 1], in1=fg[:, :], op0=ALU.mult,
                                             op1=ALU.mult).then_inc(fd, 1)



def backbone(nc, io, stop=None):
    with ExitStack() as stack:
        c = Core(nc, stack)
        with c.scope(AREA_CONST):
            consts = {"ident": c.sb("ident", [P, P]), "ones": c.sb("ones", [P, P]), "eps": c.sb("eps", [P, 1]),
                      "sel": c.sb("sel", [P, 2 * (QH + KVH) - 1]), "spread": c.sb("spread", [QH + KVH, QH + KVH, P])}
            mod, cols = c.sb("mod", [P, 2, 24, 2]), c.sb("cols", [P, 66])

        def scratch(name, shape):
            return nc.dram_tensor(name, shape, F32).ap()
        io["xt"] = scratch("xt_scratch", [P, KT, T])
        io["skew"] = scratch("bias_scratch", [NH, GRID_W, BIAS_ROWS, SKEW_W])
        io["gd"] = scratch("gate_scratch", [KT, P, T])
        io["qd"] = scratch("q_scratch", [KT, P, NLAT])
        io["kd"] = scratch("k_scratch", [KT, P, T])
        io["od"] = scratch("o_scratch", [KT, P, NLAT])

        with c.scope(AREA_H):
            hi, lo = c.sb("h_hi", [P, KT, T], F32R), c.sb("h_lo", [P, KT, T], F32R)
        with c.scope(AREA_X):
            xt = c.sb("xt", [P, KT, T])
        with c.scope(AREA_X):
            vraw = c.sb("v_raw", [P, TT, D])
        with c.scope(AREA_QKV):
            qk = c.sb("qk", [P, QH + KVH, T])
            vhi, vlo = c.sb("v_hi0", [P, TT, 256], F32R), c.sb("v_lo0", [P, TT, 256], F32R)
            khi, klo = c.sb("k_hi0", [P, KVH, T], F32R), c.sb("k_lo0", [P, KVH, T], F32R)
        with c.scope(AREA_W):
            wbuf = c.sb("w_raw", [P, KT, 256]), c.sb("w_hi", [P, KT, 256], F32R), c.sb("w_lo", [P, KT, 256], F32R)

        qw, kw = QH * HD, KVH * HD
        w = io["ga_w_in"]
        steps = [
            lambda: load_and_modulate(c, io, consts, xt, mod, cols),
            lambda: normalise(c, io, consts, 0, xt, hi, lo, mod, store=False),
            lambda: project(c, "q0", w, 0, (QH + KVH) // 2, hi, lo, wbuf, ALL_CHUNKS, ACT.Copy, dest=qk),
            lambda: project_values(c, "v0", w, qw + kw, 1, hi, lo, wbuf, split=(vhi, vlo)),
            lambda: project(c, "g0", w, qw + 2 * kw, KT // 2, hi, lo, wbuf, ALL_CHUNKS, ACT.Silu, dram=io["gd"]),
            lambda: norm_and_rotate(c, io, consts, cols, qk, khi, klo),
            lambda: grouped_attention(c, io, consts, qk, khi, klo, vhi, vlo),
            lambda: split_tiles(c, "o0", hi, lo, T, src=qk),
            lambda: project(c, "o0", io["ga_w_out"], 0, KT // 2, hi, lo, wbuf, ALL_CHUNKS,
                            residual=(mod[:, 0], io["xt"], xt)),
            lambda: normalise(c, io, consts, 1, xt, hi, lo, mod, store=True),
            lambda: project(c, "q1", io["na_w_in"], 0, KT // 2, hi, lo, wbuf, LAT_CHUNKS, ACT.Copy,
                            scale=ND ** -0.5, dram=io["qd"]),
            lambda: project(c, "k1", io["na_w_in"], D, KT // 2, hi, lo, wbuf, ALL_CHUNKS, ACT.Copy, dram=io["kd"]),
            lambda: project_values(c, "v1", io["na_w_in"], 2 * D, D // 256, hi, lo, wbuf, dest=vraw),
            lambda: project(c, "g1", io["na_w_in"], 3 * D, KT // 2, hi, lo, wbuf, LAT_CHUNKS, ACT.Silu, dram=io["gd"]),
            lambda: neighbourhood_attention(c, io, consts, vraw),
            lambda: split_tiles(c, "o1", hi, lo, NLAT, dram=io["od"]),
            lambda: project(c, "o1", io["na_w_out"], 0, KT // 2, hi, lo, wbuf, LAT_CHUNKS,
                            residual=(mod[:, 1], io["xt"], xt)),
            lambda: finish(c, io, consts, xt),
        ]
        for step in steps[:stop]:
            step()


_INS = ['x', 'c', 'ctx', 'c_ctx', 'mod_w', 'mod_b', 'norm_g', 'final_g', 'ga_w_in', 'ga_q_g', 'ga_k_g', 'ga_w_out',
        'na_w_in', 'na_w_out']


def kernel(**inputs):
    import numpy as _np
    import concourse.bacc as _bacc
    from concourse import mybir as _mybir
    from concourse.bass_utils import run_bass_kernel_spmd as _run

    nc = _bacc.Bacc("TRN2", target_bir_lowering=False, num_devices=1)
    cos, sin = rope_tables()
    mask_cols, mask_mid = window_masks()
    arrays = {n: _np.ascontiguousarray(inputs[n]) for n in _INS}
    wide = GRID_W - KW
    arrays["bias"] = _np.pad(_np.asarray(inputs["na_rpb"])[0], ((0, 0), (0, 0), (wide, wide)))
    arrays |= {"cos": cos, "sin": sin, "mask_cols": mask_cols, "mask_mid": mask_mid}
    io, in_map = {}, {}
    for name, a in arrays.items():
        if name.startswith(("ga_w", "na_w")):
            a = a[0]
        in_map[f"in_{name}"] = a
        io[name] = nc.dram_tensor(f"in_{name}", a.shape, _mybir.dt.from_np(a.dtype), kind="ExternalInput").ap()
    io["out"] = nc.dram_tensor("out", (1, NLAT, D), F32, kind="ExternalOutput").ap()
    backbone(nc, io)
    r = _run(nc, [in_map], core_ids=[0])
    return r.results[0]["out"]
```

```python
from contextlib import ExitStack, contextmanager

import numpy as np

import concourse.bass as bass
from concourse import mybir

ALU = mybir.AluOpType
ACT = mybir.ActivationFunctionType
F32 = mybir.dt.float32
F32R = mybir.dt.float32r
AX = mybir.AxisListType.X

P = 128
D = 1024
KT = D // P
NCTX, NLAT = 256, 1024
T = NCTX + NLAT
TT = T // P
CT = NCTX // P
GRID_W = 64
EPS = 1e-6
THETA = 10000.0

HD = 128
QH, KVH = 8, 2
GROUP = QH // KVH
NH, ND = 16, 64
KH, KW = 8, 16
ROWS = NLAT // GRID_W
MASKED = -1e30
BIAS_ROWS, BIAS_W = 2 * KH - 1, 2 * GRID_W - 1
SKEW_W = BIAS_W + GRID_W - 1
END_SLOTS = range(1, 15)
MID_SLOTS = range(3, 12)

ALL_CHUNKS = [(0, NCTX), (NCTX, 512), (NCTX + 512, 512)]
LAT_CHUNKS = [(NCTX, 512), (NCTX + 512, 512)]


def rope_tables():
    nf = HD // 4
    inv = (np.float32(THETA) ** (-np.arange(nf, dtype=np.float32) / np.float32(nf))).astype(np.float32)
    t = np.arange(NLAT)
    row, col = (t // GRID_W).astype(np.float32), (t % GRID_W).astype(np.float32)
    ar, ac = row[:, None] * inv, col[:, None] * inv
    ang = np.concatenate([ar, ar, ac, ac], axis=-1).T
    cos, sin = np.ones((HD, T), np.float32), np.zeros((HD, T), np.float32)
    sign = np.where((np.arange(HD) // nf) % 2 == 0, -1.0, 1.0).astype(np.float32)[:, None]
    cos[:, NCTX:], sin[:, NCTX:] = np.cos(ang), np.sin(ang) * sign
    return cos, sin


def window_masks():
    q = np.arange(P) % GRID_W
    start = np.clip(q - KW // 2, 0, GRID_W - KW)[:, None]
    k = np.arange(GRID_W)[None]
    cols = np.where((k >= start) & (k < start + KW), 0.0, MASKED).astype(np.float32)
    mid = np.repeat(cols[:, None], len(MID_SLOTS), axis=1)
    mid[P // 2:, 0] = MASKED
    mid[:P // 2, -1] = MASKED
    return cols, mid


AREA_H = (0, 80)
AREA_X = (80, 120)
AREA_MID = (120, 160)
AREA_SQUARES = (120, 136)
AREA_NORM = (136, 160)
AREA_W = (160, 199)
AREA_QKV = (80, 170)
AREA_STAGE = (184, 199)
AREA_CONST = (199, 207)


class Core:

    BASE = 17 * 1024

    def __init__(self, nc, stack):
        self.nc, self.stack, self.top = nc, stack, stack
        self.free = []
        self.sems, self.old_sems = [], []

    def sb(self, name, shape, dt=F32):
        size = int(np.prod(shape[1:])) * 4
        size = (size + 63) // 64 * 64
        for r in self.free:
            if r[0] + size <= r[1]:
                at = r[0]
                r[0] += size
                return self.nc.alloc_sbuf_tensor_at(name, shape, dt, offset=at)
        raise ValueError(f"{name}: {size} bytes in {self.free}")

    def ps(self, name, shape):
        return self.stack.enter_context(self.nc.psum_tensor(name, shape, F32))

    def sem(self, name):
        self.sems.append(self.nc.alloc_semaphore(name=name))
        return self.sems[-1]

    @contextmanager
    def block(self):
        with self.nc.Block() as block:
            old = self.old_sems

            @block.gpsimd
            def _(pool):
                for sem in old:
                    pool.sem_clear(sem)
            yield block
        for sem in old:
            self.nc.release_semaphore(sem)
        self.old_sems, self.sems = self.sems, []

    @contextmanager
    def scope(self, *ranges):
        keep = self.stack, self.free
        self.free = [[self.BASE + int(a * 1024), self.BASE + int(b * 1024)] for a, b in ranges]
        with ExitStack() as inner:
            self.stack = inner
            yield
        self.stack, self.free = keep

    @contextmanager
    def place(self, *ranges):
        keep = self.free
        self.free = [[self.BASE + int(a * 1024), self.BASE + int(b * 1024)] for a, b in ranges]
        yield
        self.free = keep



class NormSteps:
    PARTS = [(0, NCTX, 1), (NCTX, NLAT, 0)]

    def __init__(self, c, consts, l, xt, hi, lo, mod, sums):
        self.consts, self.l, self.xt, self.hi, self.lo, self.mod, self.sums = consts, l, xt, hi, lo, mod, sums
        self.t_ = c.sb(f"scaled{l}", [P, 2, T])
        self.root, self.inv = c.sb(f"root{l}", [P, TT]), c.sb(f"inv{l}", [P, TT])
        self.rb = c.ps(f"rb{l}", [P, 3, 512])
        self.summed, self.rooted, self.recd, self.spread = (
            c.sem(f"{x}{l}") for x in ("summed", "rooted", "recip_done", "inv_spread"))
        self.scaled, self.his, self.los = (c.sem(f"{x}{l}") for x in ("scaled", "h_hi", "h_lo"))

    def roots(self, act):
        act.wait_ge(self.summed, 1)
        act.activation(self.root[:, :], self.sums, ACT.Sqrt, bias=self.consts["eps"][:, :],
                       scale=1.0 / D).then_inc(self.rooted, 1)

    def reciprocals(self, dve):
        dve.wait_ge(self.rooted, 1)
        dve.reciprocal(self.inv[:, :], self.root[:, :]).then_inc(self.recd, 1)

    def spread_inverses(self, pe):
        pe.wait_ge(self.recd, 1)
        for t in range(TT):
            at = t * P + (512 - NCTX if t >= CT else 0)
            last = pe.transpose(self.rb[:, at // 512, at % 512:at % 512 + P],
                                self.inv[:, t:t + 1].broadcast_to([P, P]), self.consts["ident"][:, :])
        last.then_inc(self.spread, 1)

    def high_parts(self, act):
        for k in range(KT):
            for j, (a, n, s) in enumerate(self.PARTS):
                act.wait_ge(self.scaled, 2 * k + j + 1)
                act.activation(self.hi[:, k, a:a + n], self.t_[:, k % 2, a:a + n], ACT.Identity,
                               bias=self.mod[:, self.l, k, s:s + 1]).then_inc(self.his, 1)

    def scale_and_low(self, dve, midway=lambda: None):
        rb = self.rb[:, :, :].rearrange("p a n -> p (a n)")

        def low(k):
            for j, (a, n, s) in enumerate(self.PARTS):
                dve.wait_ge(self.his, 2 * k + j + 1)
                dve.scalar_tensor_tensor(out=self.lo[:, k, a:a + n], in0=self.t_[:, k % 2, a:a + n],
                                         scalar=self.mod[:, self.l, k, s:s + 1], in1=self.hi[:, k, a:a + n],
                                         op0=ALU.add, op1=ALU.subtract).then_inc(self.los, 1)
        dve.wait_ge(self.spread, 1)
        for k in range(KT):
            for j, (a, n, s) in enumerate(self.PARTS):
                if k >= 2:
                    dve.wait_ge(self.los, 2 * (k - 2) + j + 1)
                dve.scalar_tensor_tensor(out=self.t_[:, k % 2, a:a + n], in0=self.xt[:, k, a:a + n],
                                         scalar=self.mod[:, self.l, 8 + k, s:s + 1],
                                         in1=rb[:, 512 * j:512 * j + n],
                                         op0=ALU.mult, op1=ALU.mult).then_inc(self.scaled, 1)
            if k:
                low(k - 1)
            if k == KT // 2 + 1:
                midway()
        low(KT - 1)


class FirstWeights:

    def __init__(self, c, tag, w, col0, wbuf):
        self.w, self.col0, self.wbuf = w, col0, wbuf
        self.loaded = [c.sem(f"fw_loaded{half}_{tag}") for half in range(2)]
        self.whi, self.wlo = c.sem(f"fw_hi_{tag}"), c.sem(f"fw_lo_{tag}")

    def load(self, sp, half):
        cols = slice(half * P, (half + 1) * P)
        sp.dma_start(self.wbuf[0][:, :, cols], self.w[:, self.col0 + half * P:self.col0 + (half + 1) * P]
                     .rearrange("(k p) n -> p k n", p=P)).then_inc(self.loaded[half], 16)

    def split(self, pool, half):
        raw, hi, lo = (b[:, :, half * P:(half + 1) * P] for b in self.wbuf)
        pool.wait_ge(self.loaded[half], 16)
        pool.tensor_copy(hi, raw).then_inc(self.whi, 1)
        pool.wait_ge(self.whi, half + 1)
        pool.tensor_tensor(lo, raw, hi, ALU.subtract).then_inc(self.wlo, 1)
        pool.wait_ge(self.wlo, half + 1)


PIECES = 3 * KT


class ModSteps:

    def __init__(self, c, io, consts, l, mod, cols, cs, slots, turn):
        self.io, self.consts, self.l, self.mod, self.cols, self.cs, self.turn = io, consts, l, mod, cols, cs, turn
        self.slots = slots
        self.w = [c.sb(f"wmod{l}_{i}", [P, D]) for i in range(slots)]
        self.mrow = c.sb(f"mod_rows{l}", [2, D])
        self.mps = c.ps(f"mps{l}", [P, 2, 512])
        self.loaded = [c.sem(f"wmod_loaded{l}_{i}") for i in range(slots)]
        self.mm, self.rows, self.colst, self.colsd, self.gains = (c.sem(f"{x}{l}") for x in (
            "mod_mm", "mod_rows_done", "mod_turned", "mod_cols_done", "mod_gains"))

    def load(self, sp, pieces=range(PIECES)):
        for n in pieces:
            j, k = n // KT, n % KT
            if n >= self.slots:
                sp.wait_ge(self.mm, n - self.slots + 1)
            sp.dma_start(self.w[n % self.slots][:, :], self.io["mod_w"][self.l, k * P:(k + 1) * P, j * D:(j + 1) * D]
                         ).then_inc(self.loaded[n % self.slots], 16)

    def product(self, pe, n):
        j, k = n // KT, n % KT
        if j and k == 0:
            pe.wait_ge(self.rows, j)
        pe.wait_ge(self.loaded[n % self.slots], 16 * (n // self.slots + 1))
        for b in range(2):
            last = pe.matmul(self.mps[0:2, b, :], self.cs[:, k:16:KT],
                             self.w[n % self.slots][:, b * 512:(b + 1) * 512],
                             start=(k == 0), stop=(k == KT - 1))
        last.then_inc(self.mm, 1)
        if k == KT - 1:
            pe.wait_ge(self.rows, j + 1)
            if j:
                pe.wait_ge(self.colsd, j)
            for m in range(KT):
                last = pe.transpose(self.turn[:, 2 * m:2 * m + 2], self.mrow[:, m * P:(m + 1) * P],
                                    self.consts["ident"][0:2, 0:2])
            last.then_inc(self.colst, 1)

    def vectors(self, dve, j):
        l, mod, cols = self.l, self.mod, self.cols
        dve.wait_ge(self.mm, (j + 1) * KT)
        dve.tensor_copy(self.mrow[:, :].rearrange("p (j n) -> p j n", j=2), self.mps[0:2, :, :]).then_inc(self.rows, 1)
        dve.wait_ge(self.colst, j + 1)
        at = 24 * l + KT * j
        dve.tensor_tensor(mod[:, l, KT * j:KT * (j + 1), :], self.turn.rearrange("p (j s) -> p j s", s=2),
                          cols[:, at:at + KT].unsqueeze(2).broadcast_to([P, KT, 2]), ALU.add).then_inc(self.colsd, 1)
        dve.wait_ge(self.colsd, j + 1)
        if j == 1:
            for s in range(2):
                dve.scalar_tensor_tensor(out=mod[:, l, 8:16, s], in0=mod[:, l, 8:16, s], scalar=1.0,
                                         in1=cols[:, 48 + 8 * l:56 + 8 * l], op0=ALU.add,
                                         op1=ALU.mult).then_inc(self.gains, 1)


def prologue(c, io, consts, xt, hi, lo, mod, cols, first):
    nc = c.nc
    ident, ones, cs = consts["ident"], consts["ones"], consts["silu_cols"]
    with c.scope(AREA_MID):
        small = c.ps("small", [P, 512])
        sums, sq = c.sb("x_sums", [P, TT]), c.sb("x_squares", [P, D])
        squared = c.sem("x_squared")
        vec = c.sb("vec_rows", [P, P])
        vec2 = c.sb("vec_rows2", [P, P])
        norm = NormSteps(c, consts, 0, xt, hi, lo, mod, sums[:, :])
        with c.place((AREA_MID[1] - 20, AREA_MID[1]), AREA_STAGE):
            vectors = ModSteps(c, io, consts, 0, mod, cols, cs, 7, small[:, 256:256 + 2 * KT])
        with c.place(AREA_H):
            xin = c.sb("xin", [P, TT, D])
        tps = c.ps("tps", [P, 2, 512])
        cst, cst0 = c.sem("const_ready"), c.sem("const_zeroed")
        s_vec, s_x = c.sem("vec_loaded"), [c.sem(f"x_loaded{t}") for t in range(TT)]
        silu, csd, stored, vt = c.sem("silu_done"), c.sem("cs_done"), c.sem("xt_stored"), c.sem("vec_turned")
        turned = c.sem("turned")
        taken = [c.sem("first_half_taken"), c.sem("second_half_taken")]

        with c.block() as block:
            @block.gpsimd
            def _(pool):
                pool.memset(ones[:, :], 1.0).then_inc(cst, 1)
                pool.memset(ident[:, :], 0.0).then_inc(cst0, 1)
                pool.memset(consts["eps"][:, :], EPS).then_inc(cst, 1)
                pool.wait_ge(cst0, 1)
                pool.affine_select(out=ident[:, :], in_=ident[:, :], compare_op=ALU.not_equal, fill=1.0,
                                   base=0, pattern=[[-1, P]], channel_multiplier=1).then_inc(cst, 1)
                pool.wait_ge(cst, 3)
                first.split(pool, 0)
                first.split(pool, 1)

            @block.sync
            def _(sp):
                sp.dma_start(vec[0:8, :], io["c"].rearrange("a (r p) -> (a r) p", p=P)).then_inc(s_vec, 16)
                sp.dma_start(vec[8:16, :], io["c_ctx"].rearrange("(r p) -> r p", p=P)).then_inc(s_vec, 16)
                sp.dma_start(vec2[0:48, :], io["mod_b"].rearrange("l (r p) -> (l r) p", p=P)).then_inc(s_vec, 16)
                sp.dma_start(vec2[48:64, :], io["norm_g"].rearrange("l (r p) -> (l r) p", p=P)).then_inc(s_vec, 16)
                sp.dma_start(vec2[64:65, :], io["ga_q_g"]).then_inc(s_vec, 16)
                sp.dma_start(vec2[65:66, :], io["ga_k_g"]).then_inc(s_vec, 16)
                for t in range(TT):
                    src = io["ctx"][0, t * P:(t + 1) * P] if t < CT else io["x"][0, (t - CT) * P:(t - CT + 1) * P]
                    sp.dma_start(xin[:, t, :], src).then_inc(s_x[t], 16)
                vectors.load(sp)
                first.load(sp, 0)
                first.load(sp, 1)
                for half in taken:
                    sp.wait_ge(half, TT)
                sp.dma_start(io["xt"], xt[:, :, :]).then_inc(stored, 16)
                sp.wait_ge(stored, 16)

            @block.tensor
            def _(pe):
                pe.wait_ge(cst, 3)
                pe.wait_ge(silu, 1)
                pe.transpose(small[:, 64:80], vec[0:16, :], ident[0:16, 0:16])
                pe.transpose(small[:, 80:146], vec2[0:66, :], ident[0:66, 0:66]).then_inc(vt, 1)
                for t in range(TT):
                    pe.wait_ge(s_x[t], 16)
                    for b in range(2):
                        if t:
                            pe.wait_ge(taken[b], t)
                        for k in range(4):
                            last = pe.transpose(tps[:, b, k * P:(k + 1) * P],
                                                xin[:, t, (4 * b + k) * P:(4 * b + k + 1) * P], ident[:, :])
                        last.then_inc(turned, 1)
                pe.wait_ge(csd, 2)
                norm.spread_inverses(pe)
                for n in range(PIECES):
                    vectors.product(pe, n)

            @block.scalar
            def _(act):
                act.wait_ge(s_vec, 16 * 6)
                act.activation(vec[0:16, :], vec[0:16, :], ACT.Silu).then_inc(silu, 1)
                for t in range(TT):
                    act.wait_ge(turned, 2 * t + 1)
                    act.copy(xt[:, 0:4, t * P:(t + 1) * P],
                             tps[:, 0, :].rearrange("p (k q) -> p k q", k=4)).then_inc(taken[0], 1)
                    if t:
                        act.wait_ge(squared, t)
                    act.activation(sq[:, :], xin[:, t, :], ACT.Square, accum_out=sums[:, t:t + 1]).then_inc(squared, 1)
                act.wait_ge(squared, TT)
                act.sem_inc(norm.summed, 1)
                norm.roots(act)
                norm.high_parts(act)

            @block.vector
            def _(dve):
                dve.wait_ge(vt, 1)
                dve.tensor_copy(cs[:, :], small[:, 64:80]).then_inc(csd, 1)
                dve.tensor_copy(cols[:, :], small[:, 80:146]).then_inc(csd, 1)
                for t in range(TT):
                    dve.wait_ge(turned, 2 * t + 2)
                    dve.tensor_copy(xt[:, 4:8, t * P:(t + 1) * P],
                                    tps[:, 1, :].rearrange("p (k q) -> p k q", k=4)).then_inc(taken[1], 1)
                norm.reciprocals(dve)
                vectors.vectors(dve, 0)
                vectors.vectors(dve, 1)
                dve.wait_ge(vectors.gains, 2)
                norm.scale_and_low(dve, lambda: vectors.vectors(dve, 2))



def project(c, tag, w, col0, pairs, hi, lo, wbuf, chunks, func=None, scale=1.0, dest=None, dram=None,
            residual=None, ahead=None, squares=None, norm=None, raw_h=None):
    nc = c.nc
    raw, whi, wlo = wbuf
    width = sum(n for _, n in chunks)
    tok0 = chunks[0][0]
    with c.scope(AREA_STAGE):
        ps = c.ps(f"pp{tag}", [P, 2, len(chunks), 512])
        if norm:
            layer, x, mod, acc_x, consts, x_dram = norm
            sums = c.ps(f"sums_{tag}", [P, 512])
            with c.place(AREA_NORM):
                steps = NormSteps(c, consts, layer, x, hi, lo, mod, sums[:, 0:TT])
            x_stored = c.sem(f"x_stored_{tag}")
        if raw_h:
            src, src_dram = raw_h
            first = FirstWeights(c, tag, w, col0, wbuf)
            h_hi, h_lo = c.sem(f"s_hi_{tag}"), c.sem(f"s_lo_{tag}")
            if src_dram is not None:
                with c.place(AREA_MID):
                    src = c.sb(f"raw_{tag}", [P, KT, width])
                h_in = [c.sem(f"s_in_{tag}_{k}") for k in range(KT)]
        loaded, w_hi, w_lo, mm = (c.sem(f"{x}_{tag}") for x in ("w_loaded", "w_hi", "w_lo", "mm_done"))
        out_done, zeroed = c.sem(f"out_done_{tag}"), c.sem(f"squares_zeroed_{tag}")
        squared, added = c.sem(f"squared_{tag}"), c.sem(f"squares_added_{tag}")
        stored = [c.sem(f"stored_{tag}_{s}") for s in range(2)]
        x_in = [c.sem(f"x_in_{tag}_{s}") for s in range(2)]
        stage = c.sb(f"stage{tag}", [P, 2, width]) if dram is not None or residual else None
        lanes = [(j, a, n, sum(m for _, m in chunks[:j])) for j, (a, n) in enumerate(chunks)]

        with c.block() as block:
            @block.sync
            def _(sp):
                def rest(i, w=w, col0=col0 + 256):
                    sp.wait_ge(w_lo, 2 * i + 2)
                    sp.dma_start(raw[:, :, :], w[:, bass.ds(col0 + i * 256, 256)]
                                 .rearrange("(k p) n -> p k n", p=P)).then_inc(loaded, 16)
                def stores(i):
                    for s in range(2):
                        if dram is not None:
                            sp.wait_ge(out_done, 2 * i + s + 3)
                            sp.dma_start(dram[bass.ds(2 * i + s, 1), :, 0:width].rearrange("a p n -> p (a n)"),
                                         stage[:, s, :]).then_inc(stored[s], 16)
                def fetch(i):
                    for s in range(2):
                        sp.wait_ge(out_done, 2 * i + s + 1)
                        sp.dma_start(stage[:, s, :], residual[1][:, bass.ds(2 * i + s, 1), tok0:tok0 + width]
                                     .rearrange("p a n -> p (a n)")).then_inc(x_in[s], 16)
                if raw_h:
                    first.load(sp, 0)
                    if src_dram is not None:
                        for k in range(KT):
                            sp.dma_start(src[:, k, :], src_dram[k, :, 0:width]).then_inc(h_in[k], 16)
                            if k == 1:
                                first.load(sp, 1)
                    else:
                        first.load(sp, 1)
                if residual:
                    fetch(0)
                if raw_h:
                    sp.wait_ge(first.wlo, 2)
                if norm:
                    sp.dma_start(x_dram, x[:, :, :]).then_inc(x_stored, 16)
                if pairs > 1:
                    with sp.Fori(0, pairs - 1) as i:
                        rest(i)
                        stores(i)
                        if residual:
                            fetch(i + 1)
                if ahead:
                    rest(pairs - 1, ahead[0], ahead[1] - 256 * (pairs - 1))
                stores(pairs - 1)
                if dram is not None:
                    for s in range(2):
                        sp.wait_ge(stored[s], 16 * pairs + 16)
                if norm:
                    sp.wait_ge(x_stored, 16)

            @block.scalar
            def _(act):
                if not residual:
                    act.sem_inc(out_done, 2)
                if raw_h:
                    for k in range(KT):
                        if src_dram is not None:
                            act.wait_ge(h_in[k], 16)
                        act.copy(hi[:, k, T - width:], src[:, k, :]).then_inc(h_hi, 1)
                if norm:
                    steps.roots(act)
                    steps.high_parts(act)
                def high(i, s):
                    act.wait_ge(loaded, 16 * i + 16)
                    act.copy(whi[:, :, s * P:(s + 1) * P], raw[:, :, s * P:(s + 1) * P]).then_inc(w_hi, 1)
                def out(i, s):
                    if residual:
                        act.wait_ge(mm, 2 * i + s + 1)
                        return
                    act.wait_ge(mm, 2 * i + s + 1)
                    if dram is not None:
                        act.wait_ge(stored[s], 16 * i + 16)
                    for j, a, n, o in lanes:
                        if dram is not None:
                            to = stage[:, s, o:o + n]
                        else:
                            to = dest[:, bass.ds(2 * i + s, 1), o:o + n].rearrange("p a n -> p (a n)")
                        last = act.activation(to, ps[:, s, j, 0:n], func, scale=scale)
                    last.then_inc(out_done, 1)
                def square(i, s):
                    if squares:
                        act.wait_ge(out_done, 2 * i + s + 3)
                        act.wait_ge(added, 2 * i + s + 1)
                        act.activation(squares[0][:, s, :], residual[2][:, bass.ds(2 * i + s, 1), :]
                                       .rearrange("p a n -> p (a n)"), ACT.Square).then_inc(squared, 1)
                if pairs > 1:
                    with act.Fori(0, pairs - 1) as i:
                        for s in range(2):
                            out(i, s)
                            high(i, s)
                            square(i, s)
                for s in range(2):
                    act.wait_ge(mm, 2 * (pairs - 1) + s + 1)
                    if ahead:
                        high(pairs - 1, s)
                    out(pairs - 1, s)
                    square(pairs - 1, s)

            @block.vector
            def _(dve):
                if residual:
                    dve.sem_inc(out_done, 2)
                gate, _, dst = residual or (None, None, None)
                dve.sem_inc(w_lo, 2)
                if raw_h:
                    for k in range(KT):
                        dve.wait_ge(h_hi, k + 1)
                        dve.tensor_tensor(lo[:, k, T - width:], src[:, k, :], hi[:, k, T - width:],
                                          ALU.subtract).then_inc(h_lo, 1)
                    dve.wait_ge(h_lo, KT)
                if norm:
                    steps.reciprocals(dve)
                    steps.scale_and_low(dve)
                def low(i, s):
                    dve.wait_ge(w_hi, 2 * i + s + 1)
                    dve.tensor_tensor(wlo[:, :, s * P:(s + 1) * P], raw[:, :, s * P:(s + 1) * P],
                                      whi[:, :, s * P:(s + 1) * P], ALU.subtract).then_inc(w_lo, 1)
                def add(i, s):
                    dve.wait_ge(mm, 2 * i + s + 1)
                    dve.wait_ge(x_in[s], 16 * i + 16)
                    m = bass.ds(2 * i + s, 1)
                    for j, a, n, o in lanes:
                        dve_gate = gate[:, bass.ds(16 + 2 * i + s, 1), 1 if a < NCTX else 0]
                        last = dve.scalar_tensor_tensor(
                            out=dst[:, m, a:a + n].rearrange("p a n -> p (a n)"), in0=ps[:, s, j, 0:n],
                            scalar=dve_gate, in1=stage[:, s, o:o + n], op0=ALU.mult, op1=ALU.add)
                    last.then_inc(out_done, 1)
                with dve.Fori(0, pairs - 1) as i:
                    for s in range(2):
                        if residual:
                            add(i, s)
                        low(i, s)
                for s in range(2):
                    if residual:
                        add(pairs - 1, s)
                    if ahead:
                        low(pairs - 1, s)

            @block.gpsimd
            def _(pool):
                if dram is not None:
                    for s in range(2):
                        pool.sem_inc(stored[s], 16)
                if raw_h:
                    first.split(pool, 0)
                    first.split(pool, 1)
                if squares:
                    sq, total = squares
                    pool.sem_inc(added, 2)
                    pool.memset(total[:, :], 0.0).then_inc(zeroed, 1)
                    pool.wait_ge(zeroed, 1)
                    with pool.Fori(0, pairs) as i:
                        for s in range(2):
                            pool.wait_ge(squared, 2 * i + s + 1)
                            pool.wait_ge(added, 2 * i + s + 2)
                            pool.tensor_tensor(total[:, :], total[:, :], sq[:, s, :], ALU.add).then_inc(added, 1)

            @block.tensor
            def _(pe):
                def product(s, lane, k):
                    j, a, n, o = lane
                    ws = slice(s * P, (s + 1) * P)
                    acc = ps[:, s, j, 0:n]
                    pe.matmul(acc, whi[:, k, ws], hi[:, k, a:a + n], start=(k == 0), stop=False)
                    pe.matmul(acc, whi[:, k, ws], lo[:, k, a:a + n], start=False, stop=False)
                    return pe.matmul(acc, wlo[:, k, ws], hi[:, k, a:a + n], start=False, stop=(k == KT - 1))

                def tile(i, s):
                    pe.wait_ge(w_lo, 2 * i + s + 1)
                    pe.wait_ge(out_done, 2 * i + s + 1)
                    for lane in lanes:
                        for k in range(KT):
                            last = product(s, lane, k)
                    last.then_inc(mm, 1)

                if norm:
                    for t in range(TT):
                        last = pe.matmul(steps.sums[:, t:t + 1], acc_x[:, t * P:(t + 1) * P], consts["ones"][:, :],
                                         start=True, stop=True)
                    last.then_inc(steps.summed, 1)
                    steps.spread_inverses(pe)
                if norm or raw_h:
                    if raw_h:
                        pe.wait_ge(first.wlo, 1)
                    pe.wait_ge(w_lo, 1)
                    pe.wait_ge(out_done, 1)
                    for k in range(KT):
                        if norm:
                            pe.wait_ge(steps.los, 2 * k + 2)
                        else:
                            pe.wait_ge(h_lo, k + 1)
                        for lane in lanes:
                            last = product(0, lane, k)
                    last.then_inc(mm, 1)
                    if raw_h:
                        pe.wait_ge(first.wlo, 2)
                    tile(0, 1)
                with pe.Fori(1 if norm or raw_h else 0, pairs) as i:
                    for s in range(2):
                        tile(i, s)


def project_values(c, tag, w, col0, blocks, hi, lo, bufs, ahead, dest=None, split=None):
    nc = c.nc
    B = len(bufs)
    assert blocks % B == 0
    with c.scope():
        ps = c.ps(f"pv{tag}", [P, 2, 512])
        loaded, w_hi, w_lo, mm = (c.sem(f"{x}_{tag}") for x in ("vw_loaded", "vw_hi", "vw_lo", "vmm_done"))
        out_hi, out_lo = c.sem(f"v_hi_{tag}"), c.sem(f"v_done_{tag}")

        def rounds(eng, body):
            if blocks > B:
                with eng.Fori(0, blocks // B - 1) as i:
                    for b in range(B):
                        body(i * B + b, b, False)
            for b in range(B):
                body(blocks - B + b, b, b == B - 1)

        with c.block() as block:
            @block.sync
            def _(sp):
                def body(i, b, last):
                    src, at = ahead if last else (w, col0 + 256 * i + 256)
                    sp.wait_ge(w_lo, i + 1)
                    sp.dma_start(bufs[(b + 1) % B][0][:, :, :], src[:, bass.ds(at, 256)]
                                 .rearrange("(k p) n -> p k n", p=P)).then_inc(loaded, 16)
                rounds(sp, body)

            @block.scalar
            def _(act):
                def body(i, b, last):
                    raw, whi, _ = bufs[(b + 1) % B]
                    if B > 1:
                        act.wait_ge(loaded, 16 * i + 16)
                        act.wait_ge(out_lo, TT * i + 2)
                        act.copy(whi[:, :, :], raw[:, :, :]).then_inc(w_hi, 1)
                    if split:
                        for t in range(TT):
                            act.wait_ge(mm, TT * i + t + 1)
                            act.copy(split[0][:, t, :], ps[:, t % 2, 0:256]).then_inc(out_hi, 1)
                    if B == 1:
                        act.wait_ge(loaded, 16 * i + 16)
                        act.wait_ge(mm, TT * i + TT)
                        act.copy(whi[:, :, :], raw[:, :, :]).then_inc(w_hi, 1)
                rounds(act, body)

            @block.vector
            def _(dve):
                dve.sem_inc(w_lo, 1)
                dve.sem_inc(out_lo, 2)
                def body(i, b, last):
                    raw, whi, wlo = bufs[(b + 1) % B]
                    def low():
                        dve.wait_ge(w_hi, i + 1)
                        dve.tensor_tensor(wlo[:, :, :], raw[:, :, :], whi[:, :, :], ALU.subtract).then_inc(w_lo, 1)
                    for t in range(TT):
                        if B > 1 and t == TT // 2:
                            low()
                        if split:
                            dve.wait_ge(out_hi, TT * i + t + 1)
                            dve.tensor_tensor(split[1][:, t, :], ps[:, t % 2, 0:256], split[0][:, t, :],
                                              ALU.subtract).then_inc(out_lo, 1)
                        else:
                            dve.wait_ge(mm, TT * i + t + 1)
                            dve.tensor_copy(dest[:, t, bass.ds(i * 256, 256)], ps[:, t % 2, 0:256]).then_inc(out_lo, 1)
                    if B == 1:
                        low()
                rounds(dve, body)

            @block.tensor
            def _(pe):
                def body(i, b, last):
                    _, whi, wlo = bufs[b]
                    pe.wait_ge(w_lo, i + 1)
                    for t in range(TT):
                        pe.wait_ge(out_lo, TT * i + t + 1)
                        acc = ps[:, t % 2, 0:256]
                        for k in range(KT):
                            tok = slice(t * P, (t + 1) * P)
                            pe.matmul(acc, hi[:, k, tok], whi[:, k, :], start=(k == 0), stop=False)
                            pe.matmul(acc, hi[:, k, tok], wlo[:, k, :], start=False, stop=False)
                            last_mm = pe.matmul(acc, lo[:, k, tok], whi[:, k, :], start=False, stop=(k == KT - 1))
                        last_mm.then_inc(mm, 1)
                rounds(pe, body)



def norm_and_rotate(c, io, consts, mod, cols, qk, khi, klo):
    nc = c.nc
    N = QH + KVH
    ORDER = [*range(QH, N), *range(QH)]
    POOL_SIN = (2, 5, 8)
    with c.scope(AREA_H):
        sq = c.sb("qsq", [P, 2, T])
        sel, rows = c.sb("selector", [P, 2 * N - 1]), c.sb("sum_rows", [N, T])
        root, inv = c.sb("q_root", [P, TT, N]), c.sb("q_inv", [P, TT, N])
        cos, sin = c.sb("cos", [P, T]), c.sb("sin", [P, T])
        rot = c.sb("rot", [P, 3, T])
        cq = c.sb("q_cos", [P, 3, T])
        rb = c.ps("q_inv_spread", [P, 3, 512])
        turn = c.ps("turned", [P, 512])
        with c.place((170, 199)):
            vectors = ModSteps(c, io, consts, 1, mod, cols, consts["silu_cols"], 6, turn[:, 0:2 * KT])
        swapped = [c.sem(f"swapped{s}") for s in range(3)]
        tabs, sqd, summed, rooted, recd = (c.sem(x) for x in ("tables_in", "qsq_done", "qsummed", "qrooted", "qrecip"))
        zero, selected, copied, columns = (c.sem(x) for x in ("sel_zeroed", "sel_ready", "sum_rows_taken", "sums_turned"))
        gsc, spread, normed, cosd, sind, sinp, done, khd, kld = (c.sem(x) for x in (
            "qgain", "spread_done", "normed", "cos_done", "sin_done", "sin_done_pool", "rotated", "k_hi", "k_lo"))

        def wait_sin(eng, m):
            if m in POOL_SIN:
                eng.wait_ge(sinp, POOL_SIN.index(m) + 1)
            else:
                eng.wait_ge(sind, m + 1 - sum(x < m for x in POOL_SIN))

        with c.block() as block:
            @block.sync
            def _(sp):
                sp.dma_start(cos[:, :], io["cos"]).then_inc(tabs, 16)
                sp.dma_start(sin[:, :], io["sin"]).then_inc(tabs, 16)
                vectors.load(sp, range(12))
                for m in range(N):
                    sp.wait_ge(normed, 2 * (m + 1))
                    if m >= 3:
                        sp.wait_ge(done, m - 2)
                    for b in range(4):
                        f = b ^ 1
                        sp.dma_start(rot[32 * b:32 * b + 32, m % 3, :],
                                     qk[32 * f:32 * f + 32, ORDER[m], :]).then_inc(swapped[m % 3], 16)
                    vectors.load(sp, range(12 + 2 * m, min(14 + 2 * m, PIECES)))

            @block.scalar
            def _(act):
                for m in range(N):
                    if m >= 2:
                        act.wait_ge(summed, m - 1)
                    act.activation(sq[:, m % 2, :], qk[:, m, :], ACT.Square).then_inc(sqd, 1)
                act.wait_ge(summed, N)
                act.copy(rows[:, 0:NCTX], rb[0:N, 0, 0:NCTX]).then_inc(copied, 1)
                act.copy(rows[:, NCTX:], rb[0:N, 1:3, :].rearrange("p a n -> p (a n)")).then_inc(copied, 1)
                act.wait_ge(columns, 1)
                act.activation(root[:, :, :].rearrange("p t m -> p (t m)"), turn[:, P:P + TT * N], ACT.Sqrt,
                               bias=consts["eps"][:, :], scale=1.0 / HD).then_inc(rooted, 1)
                for m in range(KVH):
                    act.wait_ge(done, m + 1)
                    act.copy(khi[:, m, :], qk[:, QH + m, :]).then_inc(khd, 1)

            @block.tensor
            def _(pe):
                def spread_head(m):
                    pe.wait_ge(recd, 1)
                    if m:
                        pe.wait_ge(normed, 2 * m)
                    for t in range(TT):
                        at = t * P + (512 - NCTX if t >= CT else 0)
                        last = pe.transpose(rb[:, at // 512, at % 512:at % 512 + P],
                                            inv[:, t, ORDER[m]:ORDER[m] + 1].broadcast_to([P, P]), consts["ident"][:, :])
                    last.then_inc(spread, 1)
                pe.wait_ge(selected, 1)
                for m in range(N):
                    pe.wait_ge(sqd, m + 1)
                    for j, (a, n) in enumerate(ALL_CHUNKS):
                        last = pe.matmul(rb[0:N, j, 0:n], sel[:, N - 1 - m:2 * N - 1 - m],
                                         sq[:, m % 2, a:a + n], start=(m == 0), stop=(m == N - 1))
                    last.then_inc(summed, 1)
                pe.wait_ge(copied, 2)
                for t in range(TT):
                    last = pe.transpose(turn[:, P + t * N:P + (t + 1) * N], rows[:, t * P:(t + 1) * P],
                                        consts["ident"][0:N, 0:N])
                last.then_inc(columns, 1)
                for n in range(6):
                    vectors.product(pe, n)
                for m in range(N):
                    spread_head(m)
                    for n in range(6 + 2 * m, min(8 + 2 * m, PIECES)):
                        vectors.product(pe, n)

            @block.vector
            def _(dve):
                def finish(m):
                    if m not in POOL_SIN:
                        dve.wait_ge(swapped[m % 3], 64 * (m // 3 + 1))
                        dve.tensor_tensor(rot[:, m % 3, :], rot[:, m % 3, :], sin[:, :], ALU.mult).then_inc(sind, 1)
                    dve.wait_ge(cosd, m + 1)
                    wait_sin(dve, m)
                    dve.tensor_tensor(qk[:, ORDER[m], :], cq[:, m % 3, :], rot[:, m % 3, :], ALU.add).then_inc(done, 1)

                dve.tensor_scalar(cols[:, 64:65], cols[:, 64:65], HD ** -0.5, None, ALU.mult).then_inc(gsc, 1)
                dve.wait_ge(gsc, 1)
                dve.wait_ge(tabs, 32)
                dve.wait_ge(rooted, 1)
                dve.reciprocal(inv[:, :, :], root[:, :, :]).then_inc(recd, 1)
                for m in range(N):
                    dve.wait_ge(spread, m + 1)
                    head = ORDER[m]
                    g = 64 if head < QH else 65
                    bank = rb[:, :, :].rearrange("p a n -> p (a n)")
                    for a, n, at in ((0, NCTX, 0), (NCTX, NLAT, 512)):
                        dve.scalar_tensor_tensor(out=qk[:, head, a:a + n], in0=qk[:, head, a:a + n],
                                                 scalar=cols[:, g:g + 1], in1=bank[:, at:at + n],
                                                 op0=ALU.mult, op1=ALU.mult).then_inc(normed, 1)
                    if m in (0, 4, 8):
                        vectors.vectors(dve, m // 4)
                    if m >= 2:
                        finish(m - 2)
                    if m in (4, 5):
                        dve.wait_ge(khd, m - 3)
                        dve.tensor_tensor(klo[:, m - 4, :], qk[:, QH + m - 4, :], khi[:, m - 4, :],
                                          ALU.subtract).then_inc(kld, 1)

                finish(N - 2)
                finish(N - 1)

            @block.gpsimd
            def _(pool):
                def times_sin(m):
                    pool.wait_ge(swapped[m % 3], 64 * (m // 3 + 1))
                    pool.tensor_tensor(rot[:, m % 3, :], rot[:, m % 3, :], sin[:, :], ALU.mult).then_inc(sinp, 1)
                pool.memset(sel[:, :], 0.0).then_inc(zero, 1)
                pool.wait_ge(zero, 1)
                pool.memset(sel[:, N - 1:N], 1.0).then_inc(selected, 1)
                pool.wait_ge(tabs, 32)
                for m in range(N):
                    pool.wait_ge(normed, 2 * (m + 1))
                    if m >= 3:
                        pool.wait_ge(done, m - 2)
                    pool.tensor_tensor(cq[:, m % 3, :], qk[:, ORDER[m], :], cos[:, :], ALU.mult).then_inc(cosd, 1)
                    if m - 1 in POOL_SIN:
                        times_sin(m - 1)



GQA_TILES = [(NCTX + P * j, T) for j in range(NLAT // P)] + [(P * j, NCTX) for j in range(CT)]
GQA_N = len(GQA_TILES)
GQA_GROUPS = GQA_N // 2
S_RING = 5


def key_chunks(p):
    n = GQA_TILES[p % GQA_N][1]
    return [(a, min(512, n - a)) for a in range(0, n, 512)]


CHUNKS_BEFORE = [sum(len(key_chunks(q)) for q in range(p)) for p in range(GQA_N + 1)]
CHUNKS = CHUNKS_BEFORE[-1]


def chunk_no(p, k):
    return CHUNKS_BEFORE[p % GQA_N] + k + (p // GQA_N) * CHUNKS


def score_bank(p, k):
    return (3 * (p % GQA_N) + k) % S_RING


def bank_user_before(p, k):
    q, j = p, k
    while True:
        j -= 1
        if j < 0:
            q -= 1
            j = len(key_chunks(q)) - 1
        if score_bank(q, j) == score_bank(p, k):
            return chunk_no(q, j)


def at_least(eng, sem, per, h, no):
    if isinstance(h, int) and per * h + no + 1 <= 0:
        return
    eng.wait_ge(sem, h * per + (no + 1))


def grouped_attention(c, io, consts, qk, khi, klo, vhi, vlo):
    nc = c.nc
    with c.scope(AREA_H, (AREA_QKV[1], AREA_W[1])):
        qhi, qlo = c.sb("qhi", [P, T], F32R), c.sb("qlo", [P, T], F32R)
        prob = c.sb("prob", [P, 5, T])
        pthi = c.sb("pthi", [P, 2, TT, 256], F32R)
        ptlo = c.sb("ptlo", [P, 2, TT, 256], F32R)
        cthi = c.sb("cthi", [P, CT, 256], F32R)
        ctlo = c.sb("ctlo", [P, CT, 256], F32R)
        g = c.sb("gate_in", [P, T])
        inv = c.sb("inv_sums", [P, 256])
        mx, sums = c.sb("mx", [P, 5, 3]), c.sb("sums", [P, GQA_N, 3])
        nm, tot, rec = c.sb("nm", [P, 5]), c.sb("tot", [P, GQA_N]), c.sb("rec", [P, GQA_N])
        S, TB, O = c.ps("S", [P, S_RING, 512]), c.ps("TB", [P, 2, 512]), c.ps("O", [P, 512])
        q_hi, q_lo = c.sem("gq_hi"), c.sem("gq_lo")
        qkd, mxd, nmd, expd = c.sem("g_scores"), c.sem("g_max"), c.sem("g_negmax"), c.sem("g_exp")
        totd, recd, gated, invd = c.sem("g_total"), c.sem("g_recip"), c.sem("g_gated"), c.sem("g_inv")
        td, hid, lod = c.sem("g_turned"), c.sem("g_pt_hi"), c.sem("g_pt_lo")
        pvd, od, gl = c.sem("g_pv"), c.sem("g_out"), c.sem("g_gate_in")
        skewed = c.sem("bias_skewed")
        def pt(p):
            q = p % GQA_N
            half = slice((q % 2) * P, (q % 2) * P + P)
            if q >= 8:
                return cthi[:, :, half], ctlo[:, :, half]
            return pthi[:, (q // 2) % 2, :, half], ptlo[:, (q // 2) % 2, :, half]

        def pt_user_before(p):
            q, back = p % GQA_N, (p // GQA_N) * GQA_GROUPS
            gr = q // 2
            return back + {0: -3, 1: -2, 2: 0, 3: 1, 4: -1}[gr]

        def live(n, prev, tail):
            return (n >= 0 or prev) and not (tail and n >= 0)

        LAG = 3
        PRODUCT = 2 + LAG
        OUT = PRODUCT + 2
        TAIL = OUT - 1

        Q0, Q1, QC = (NCTX, 512), (NCTX + 512, 512), (0, NCTX)

        def runs(eng, body, tail):
            body(0, 0, None)
            with eng.Fori(1, GROUP) as h:
                body(h, 0, 0)
            body(GROUP, 1, 0)
            with eng.Fori(GROUP + 1, QH) as h:
                body(h, 1, 1)
            tail(QH, KVH - 1)

        with c.block() as block:
            @block.sync
            def _(sp):
                def load(h):
                    at_least(sp, gated, GQA_GROUPS, h, -1)
                    sp.dma_start(g[:, :], io["gd"][bass.ds(h, 1), :, :].rearrange("a p n -> p (a n)")).then_inc(gl, 16)
                load(0)
                for head in range(NH):
                    src = bass.AP(tensor=io["bias"].tensor, offset=head * BIAS_ROWS * BIAS_W,
                                  ap=[[0, GRID_W], [BIAS_W, BIAS_ROWS], [1, BIAS_W]])
                    dst = bass.AP(tensor=io["skew"].tensor, offset=head * GRID_W * BIAS_ROWS * SKEW_W,
                                  ap=[[BIAS_ROWS * SKEW_W + 1, GRID_W], [SKEW_W, BIAS_ROWS], [1, BIAS_W]])
                    sp.dma_start(dst, src).then_inc(skewed, 16)
                with sp.Fori(1, QH) as h:
                    load(h)
                sp.wait_ge(skewed, 16 * NH)

            @block.tensor
            def _(pe):
                def scores(h, kv, p, k):
                    tok, _ = GQA_TILES[p]
                    a, n = key_chunks(p)[k]
                    if k == 0 and p in (0, 4, 8):
                        at_least(pe, q_lo, 3, h, (0, 4, 8).index(p))
                    at_least(pe, expd, CHUNKS, h, bank_user_before(p, k))
                    acc = S[:, score_bank(p, k), 0:n]
                    qs = slice(tok, tok + P)
                    pe.matmul(acc, qhi[:, qs], khi[:, kv, a:a + n], start=True, stop=False)
                    pe.matmul(acc, qhi[:, qs], klo[:, kv, a:a + n], start=False, stop=False)
                    pe.matmul(acc, qlo[:, qs], khi[:, kv, a:a + n], start=False, stop=True).then_inc(qkd, 1)

                def turn(h, p, k):
                    a, n = key_chunks(p)[k]
                    no = chunk_no(p, k)
                    at_least(pe, expd, CHUNKS, h, no)
                    at_least(pe, lod, CHUNKS, h, no - 2)
                    for b in range(n // P):
                        last = pe.transpose(TB[:, no % 2, b * P:(b + 1) * P],
                                            prob[:, p % 5, a + b * P:a + (b + 1) * P], consts["ident"][:, :])
                    last.then_inc(td, 1)

                def product(h, kv, gr, second, k):
                    q = (2 * gr + 1) % GQA_N
                    if q < 8:
                        blocks = [[range(0), range(0, 1), range(1, 4)], [range(4, 6), range(6, 8), range(8, 10)]][second][k]
                    else:
                        blocks = [[range(0), range(0), range(0, 1)], [range(0), range(0), range(1, 2)]][second][k]
                    if 0 in blocks:
                        at_least(pe, lod, CHUNKS, h, chunk_no(2 * gr + 1, len(key_chunks(q)) - 1))
                        at_least(pe, recd, GQA_GROUPS, h, gr)
                        at_least(pe, od, GQA_GROUPS, h, gr - 1)
                        for s in range(2):
                            pe.transpose(O[:, 256 + s * P:256 + (s + 1) * P],
                                         rec[:, q - 1 + s:q + s].broadcast_to([P, P]), consts["ident"][:, :])
                    n = GQA_TILES[q][1] // P
                    hi, lo = (cthi, ctlo) if q >= 8 else (pthi[:, (q // 2) % 2, :, :], ptlo[:, (q // 2) % 2, :, :])
                    for t in blocks:
                        vs = slice(kv * HD, (kv + 1) * HD)
                        pe.matmul(O[:, 0:256], vhi[:, t, vs], hi[:, t, :], start=(t == 0), stop=False)
                        pe.matmul(O[:, 0:256], vhi[:, t, vs], lo[:, t, :], start=False, stop=False)
                        last = pe.matmul(O[:, 0:256], vlo[:, t, vs], hi[:, t, :], start=False, stop=(t == n - 1))
                        if t == n - 1:
                            last.then_inc(pvd, 1)

                def body(h, kv, kvp, tail=False):
                    prev = kvp is not None
                    for p in range(TAIL if tail else GQA_N):
                        q, gr = p - LAG, (p - PRODUCT) // 2
                        chunks = [] if tail else key_chunks(p)
                        turns = key_chunks(q) if live(q, prev, tail) else []
                        for k in range(3):
                            if k < len(turns):
                                turn(h, q, k)
                            if k < len(chunks):
                                scores(h, kv, p, k)
                            if live(gr, prev, tail):
                                product(h, kvp if gr < 0 else kv, gr, (p - PRODUCT) % 2, k)
                runs(pe, body, lambda h, kv: body(h, kv, kv, tail=True))

            @block.vector
            def _(dve):
                def biggest(h, p, k):
                    a, n = key_chunks(p)[k]
                    at_least(dve, qkd, CHUNKS, h, chunk_no(p, k))
                    dve.tensor_reduce(mx[:, p % 5, k:k + 1], S[:, score_bank(p, k), 0:n], AX, ALU.max).then_inc(mxd, 1)

                def negmax(h, p):
                    n = len(key_chunks(p))
                    at_least(dve, mxd, CHUNKS, h, chunk_no(p, n - 1))
                    dve.tensor_reduce(nm[:, p % 5:p % 5 + 1], mx[:, p % 5, 0:n], AX, ALU.max,
                                      negate=True).then_inc(nmd, 1)

                def reciprocal(h, gr):
                    q = (2 * gr) % GQA_N
                    n = len(key_chunks(q))
                    at_least(dve, expd, CHUNKS, h, chunk_no(2 * gr + 1, n - 1))
                    dve.tensor_reduce(tot[:, q:q + 2], sums[:, q:q + 2, 0:n], AX, ALU.add).then_inc(totd, 1)
                    at_least(dve, totd, GQA_GROUPS, h, gr)
                    dve.reciprocal(rec[:, q:q + 2], tot[:, q:q + 2]).then_inc(recd, 1)

                def low(h, p, k):
                    a, n = key_chunks(p)[k]
                    no = chunk_no(p, k)
                    at_least(dve, hid, CHUNKS, h, no)
                    hi, lo = pt(p)
                    blocks = slice(a // P, (a + n) // P)
                    dve.tensor_tensor(lo[:, blocks, :], TB[:, no % 2, 0:n].rearrange("p (b q) -> p b q", q=P),
                                      hi[:, blocks, :], ALU.subtract).then_inc(lod, 1)

                def out(h, gr):
                    head = h - 1 if gr < 0 else h
                    tok = GQA_TILES[(2 * gr) % GQA_N][0]
                    at_least(dve, pvd, GQA_GROUPS, h, gr)
                    dve.tensor_copy(inv[:, :], O[:, 256:512]).then_inc(invd, 1)
                    at_least(dve, invd, GQA_GROUPS, h, gr)
                    dve.tensor_tensor(qk[:, bass.ds(head, 1), tok:tok + 256].rearrange("p a n -> p (a n)"),
                                      O[:, 0:256], inv[:, :], ALU.mult).then_inc(od, 1)

                def body(h, kv, kvp, tail=False):
                    prev = kvp is not None
                    for p in range(TAIL if tail else GQA_N):
                        q = p - LAG
                        chunks = [] if tail else key_chunks(p)
                        turns = key_chunks(q) if live(q, prev, tail) else []
                        for k in range(3):
                            if k == 0 and (p - OUT) % 2 == 0 and live((p - OUT) // 2, prev, tail):
                                out(h, (p - OUT) // 2)
                            if k == 2 and k < len(chunks):
                                biggest(h, p, k)
                            if k < len(turns):
                                low(h, q, k)
                            if k < len(chunks) and k < 2:
                                biggest(h, p, k)
                        if chunks:
                            negmax(h, p)
                        if p % 2 == 1 and live((p - 3) // 2, prev, tail):
                            reciprocal(h, (p - 3) // 2)

                runs(dve, body, lambda h, kv: body(h, kv, kv, tail=True))

            @block.scalar
            def _(act):
                def q_high(h, piece, no, user, users_head):
                    a, n = piece
                    at_least(act, qkd, CHUNKS, users_head, user)
                    act.copy(qhi[:, a:a + n], qk[:, bass.ds(h, 1), a:a + n].rearrange("p a n -> p (a n)")).then_inc(q_hi, 1)

                def exps(h, p, k):
                    a, n = key_chunks(p)[k]
                    if k == 0:
                        at_least(act, nmd, GQA_N, h, p)
                        at_least(act, td, CHUNKS, h, chunk_no(p - 5, len(key_chunks(p - 5)) - 1))
                    act.activation(prob[:, p % 5, a:a + n], S[:, score_bank(p, k), 0:n], ACT.Exp,
                                   bias=nm[:, p % 5:p % 5 + 1],
                                   accum_out=sums[:, p % GQA_N, k:k + 1]).then_inc(expd, 1)

                def high(h, p, k):
                    a, n = key_chunks(p)[k]
                    no = chunk_no(p, k)
                    at_least(act, td, CHUNKS, h, no)
                    if k == 0:
                        at_least(act, pvd, GQA_GROUPS, h, pt_user_before(p))
                    hi, _ = pt(p)
                    act.copy(hi[:, a // P:(a + n) // P, :],
                             TB[:, no % 2, 0:n].rearrange("p (b q) -> p b q", q=P)).then_inc(hid, 1)

                def body(h, kv, kvp, tail=False):
                    prev = kvp is not None
                    for p in range(LAG if tail else GQA_N):
                        q = p - LAG
                        es = key_chunks(p - 1) if live(p - 1, prev, tail) else []
                        turns = key_chunks(q) if live(q, prev, tail) else []
                        for k in range(3):
                            if k < len(turns):
                                high(h, q, k)
                            if k < len(es):
                                exps(h, p - 1, k)
                        if not tail:
                            if p == 1:
                                q_high(h, Q1, 1, chunk_no(7, 2) - CHUNKS, h)
                            if p == 3:
                                q_high(h, QC, 2, chunk_no(9, 0) - CHUNKS, h)
                            if p == 5:
                                q_high(h + 1, Q0, 0, chunk_no(3, 2), h)

                q_high(0, Q0, 0, -1, 0)
                runs(act, body, lambda h, kv: body(h, kv, kv, tail=True))

            @block.gpsimd
            def _(pool):
                def q_low(h, piece, no):
                    a, n = piece
                    pool.wait_ge(q_hi, h * 3 + no + 1)
                    pool.tensor_tensor(qlo[:, a:a + n], qk[:, bass.ds(h, 1), a:a + n].rearrange("p a n -> p (a n)"),
                                       qhi[:, a:a + n], ALU.subtract).then_inc(q_lo, 1)

                def gate(h, gr):
                    head = h - 1 if gr < 0 else h
                    tok = GQA_TILES[(2 * gr) % GQA_N][0]
                    o = qk[:, bass.ds(head, 1), tok:tok + 256].rearrange("p a n -> p (a n)")
                    at_least(pool, gl, 1, 16 * head, 15)
                    at_least(pool, od, GQA_GROUPS, h, gr)
                    pool.tensor_tensor(o, o, g[:, tok:tok + 256], ALU.mult).then_inc(gated, 1)

                def body(h, kv, kvp, tail=False):
                    prev = kvp is not None
                    for p in range(TAIL if tail else GQA_N):
                        if (p - OUT) % 2 == 0 and live((p - OUT) // 2, prev, tail):
                            gate(h, (p - OUT) // 2)
                        if not tail:
                            if p == 1:
                                q_low(h, Q1, 1)
                            if p == 3:
                                q_low(h, QC, 2)
                            if p == 5:
                                q_low(h + 1, Q0, 0)

                q_low(0, Q0, 0)
                runs(pool, body, lambda h, kv: body(h, kv, kv, tail=True))



NA_TILES = 2 * (NLAT // P)
NA_GROUPS = NA_TILES // 2
NJ = NLAT // P


def first_row(j):
    return max(0, min(2 * j - KH // 2, ROWS - KH))


def is_mid(j):
    return first_row(j) != max(0, min(2 * j + 1 - KH // 2, ROWS - KH))


def group_base(gr):
    return first_row(2 * (gr % (NJ // 2))) // 2


def neighbourhood_attention(c, io, consts, vraw):
    nc = c.nc
    NE, NM = len(END_SLOTS), len(MID_SLOTS)
    with c.scope(AREA_H, (120, AREA_W[1])):
        q2, k2, g2 = c.sb("q2", [P, NLAT]), c.sb("k2", [P, T]), c.sb("g2", [P, NLAT])
        be, bm = c.sb("bias_end", [P, 2, NE, GRID_W]), c.sb("bias_mid", [P, 2, NM, GRID_W])
        mc, mm9 = c.sb("mask_cols", [P, GRID_W]), c.sb("mask_mid", [P, NM, GRID_W])
        qs = c.sb("q_split", [P, 2, NLAT], F32R)
        ka, kb = c.sb("k_split", [P, 2, T], F32R), c.sb("k_swapped", [P, 2, T], F32R)
        vs = c.sb("v_split", [P, 2, TT, P], F32R)
        prob = c.sb("nprob", [P, 4, 832])
        pe_hi, pe_lo = c.sb("pt_end_hi", [P, 2, 6, 256], F32R), c.sb("pt_end_lo", [P, 2, 6, 256], F32R)
        pm_hi, pm_lo = c.sb("pt_mid_hi", [P, 2, 8, 256], F32R), c.sb("pt_mid_lo", [P, 2, 8, 256], F32R)
        ost, half = c.sb("o_out", [P, NLAT]), c.sb("o_half", [P, 256])
        mx, nm = c.sb("nmx", [P, 4, 4]), c.sb("nnm", [P, 4])
        sums, rec = c.sb("nsums", [P, NA_TILES, 2]), c.sb("nrec", [P, NA_TILES])
        tot = c.sb("ntot", [P, 2])
        S, TB, O = c.ps("nS", [P, 2, 2, 512]), c.ps("nTB", [P, 2, 512]), c.ps("nO", [P, 2, 512])
        ql, kl, gl, ml = (c.sem(x) for x in ("n_q_in", "n_k_in", "n_g_in", "n_mask_in"))
        bl = [c.sem(f"n_bias_in{s}") for s in range(2)]
        swd = [c.sem(f"n_swapped{s}") for s in range(2)]
        hid_, lod_ = c.sem("n_split_hi"), c.sem("n_split_lo")
        bmd, zero = c.sem("n_bias_masked"), c.sem("n_zeroed")
        qkd, mxd, nmd, expd, totd, recd = (c.sem(x) for x in (
            "n_scores", "n_max", "n_negmax", "n_exp", "n_total", "n_recip"))
        td, hid, lod = (c.sem(x) for x in ("n_turned", "n_pt_hi", "n_pt_lo"))
        pvd, halfd, addd, gated, od, std = (c.sem(x) for x in (
            "n_pv", "n_half", "n_added", "n_gated", "n_out", "n_stored"))
        SPL, N, G = 6, NA_TILES, NA_GROUPS
        PAIRS = NH // 2

        def rows(s, lo):
            top = (s == 0) != lo
            return slice(0, 64) if top else slice(64, 128)

        def pt(p):
            gr = (p % N) // 2 % 4
            hs = slice((p % 2) * P, (p % 2) * P + P)
            if gr in (0, 3):
                return pe_hi[:, gr // 3, :, :], pe_lo[:, gr // 3, :, :], hs
            return pm_hi[:, gr - 1, :, :], pm_lo[:, gr - 1, :, :], hs

        def first_block(p):
            j = p % NJ
            return first_row(j) // 2 - group_base(j // 2)

        def ctx_block(p):
            return 6 if (p % N) // 2 % 4 in (1, 2) else 4

        def live(n, prev, tail):
            return (n >= 0 or prev) and not (tail and n >= 0)

        LAG = 3
        PRODUCT = 2 + LAG
        OUT = PRODUCT + 2
        TAIL = OUT

        def runs(eng, body):
            body(0, True, False)
            with eng.Fori(1, PAIRS - 1) as i:
                body(i, False, False)
            body(PAIRS - 1, False, True)

        with c.block() as block:
            @block.sync
            def _(sp):
                def qk_in(i):
                    src = lambda a: a[bass.ds(i, 1), :, :].rearrange("a p n -> p (a n)")
                    at_least(sp, lod_, SPL, i, -2)
                    sp.dma_start(q2[:, :], src(io["qd"][:, :, 0:NLAT])).then_inc(ql, 16)
                    sp.dma_start(k2[:, :], src(io["kd"])).then_inc(kl, 16)

                def swap(i, s):
                    at_least(sp, lod_, SPL, i, 3 * s + 1)
                    for b in range(2):
                        sp.dma_start(kb[64 * b:64 * b + 64, s, :].bitcast(F32),
                                     ka[64 * (1 - b):64 * (1 - b) + 64, s, :].bitcast(F32)).then_inc(swd[s], 16)

                def bias_in(i, s):
                    at_least(sp, mxd, N, i, 8 * s - 9)
                    head = 2 * i + s
                    for rr in range(2):
                        sp.dma_start(be[64 * rr:64 * rr + 64, s, :, :],
                                     io["skew"][bass.ds(head, 1), :, END_SLOTS[0] - rr:END_SLOTS[-1] + 1 - rr, GRID_W - 1:2 * GRID_W - 1]
                                     .rearrange("a c e w -> c (a e) w")).then_inc(bl[s], 16)

                def g_in(i):
                    at_least(sp, gated, G, i, -1)
                    sp.dma_start(g2[:, :], io["gd"][bass.ds(i, 1), :, 0:NLAT].rearrange("a p n -> p (a n)")).then_inc(gl, 16)

                def store(i):
                    at_least(sp, gated, G, i, G - 1)
                    sp.dma_start(io["od"][bass.ds(i, 1), :, :].rearrange("a p n -> p (a n)"), ost[:, :]).then_inc(std, 16)

                qk_in(0)
                sp.dma_start(mc[:, :], io["mask_cols"]).then_inc(ml, 16)
                sp.dma_start(mm9[:, :, :], io["mask_mid"]).then_inc(ml, 16)
                bias_in(0, 0)
                swap(0, 0)

                def body(i, first, last):
                    bias_in(i, 1)
                    swap(i, 1)
                    if not first:
                        store(i - 1)
                    g_in(i)
                    if not last:
                        qk_in(i + 1)
                        bias_in(i + 1, 0)
                        swap(i + 1, 0)
                runs(sp, body)
                store(PAIRS - 1)
                sp.wait_ge(std, 16 * PAIRS)

            @block.tensor
            def _(pe):
                def scores(i, p):
                    s, j = p // NJ, p % NJ
                    r0 = first_row(j)
                    if j == 0:
                        at_least(pe, swd[s], 32, i, 31)
                    at_least(pe, expd, 2 * N, i, 2 * (p - 2) + 1)
                    q = qs[:, s, j * P:(j + 1) * P]
                    loc = NCTX + r0 * GRID_W
                    out = [(S[:, p % 2, 1, 0:256], 0, NCTX), (S[:, p % 2, 0, 0:512], loc, 512)]
                    if is_mid(j):
                        out.insert(1, (S[:, p % 2, 1, 256:320], loc + 512, 64))
                    for acc, a, n in out:
                        pe.matmul(acc, q, ka[:, s, a:a + n], start=True, stop=False)
                        last = pe.matmul(acc, q, kb[:, s, a:a + n], start=False, stop=True)
                    last.then_inc(qkd, 1)

                def turn(i, p, k):
                    at_least(pe, lod, 2 * N, i, 2 * p + k - 2)
                    if k == 0:
                        at_least(pe, expd, 2 * N, i, 2 * p + 1)
                    for b in range(4 if k == 0 else 2):
                        a = k * 576 + b * P
                        last = pe.transpose(TB[:, k, b * P:(b + 1) * P], prob[:, p % 4, a:a + P], consts["ident"][:, :])
                    if k and is_mid(p % NJ):
                        last = pe.transpose(TB[0:64, 1, 256:384], prob[:, p % 4, 512:576], consts["ident"][:, :])
                    last.then_inc(td, 1)

                def product(i, gr, second):
                    s = (gr % G) // 4
                    if not second:
                        at_least(pe, lod, 2 * N, i, 2 * (2 * gr + 1) + 1)
                        at_least(pe, recd, G, i, gr)
                        at_least(pe, od, G, i, gr - 2)
                        if gr % 4 == 0:
                            at_least(pe, lod_, SPL, i, 3 * s + 2)
                        for r in range(2):
                            at = (2 * gr + r) % N
                            pe.transpose(O[:, gr % 2, 256 + r * P:256 + (r + 1) * P],
                                         rec[:, at:at + 1].broadcast_to([P, P]), consts["ident"][:, :])
                    hi, lo, _ = pt(2 * gr)
                    nloc = 6 if gr % 4 in (1, 2) else 4
                    keys = [(b, nloc + b) for b in range(CT)] + [(CT + group_base(gr) + b, b) for b in range(nloc)]
                    cut = len(keys) // 2
                    for n in range(cut, len(keys)) if second else range(cut):
                        v, b = keys[n]
                        pe.matmul(O[:, gr % 2, 0:256], vs[:, s, v, :], hi[:, b, :], start=(n == 0), stop=False)
                        last = pe.matmul(O[:, gr % 2, 0:256], vs[:, s, v, :], lo[:, b, :], start=False,
                                         stop=(n == len(keys) - 1))
                    if second:
                        last.then_inc(pvd, 1)

                def body(i, first, last, tail=False):
                    prev = not first
                    for p in range(TAIL if tail else N):
                        q, gr = p - LAG, (p - PRODUCT) // 2
                        turns = live(q, prev, tail)
                        if turns:
                            turn(i, q, 0)
                        if not tail:
                            scores(i, p)
                        if turns:
                            turn(i, q, 1)
                        if live(gr, prev, tail):
                            product(i, gr, (p - PRODUCT) % 2 == 1)
                runs(pe, body)
                body(PAIRS, False, True, tail=True)

            def split_steps(i, first, last, p):
                if p in (1, 2, 6):
                    return [(i, 1, (1, 2, 6).index(p))]
                if p in (11, 12, 13) and not last:
                    return [(i + 1, 0, p - 11)]
                return []

            def parts(i, s, what):
                src, hi, lo = rows(s, False), rows(s, False), rows(s, True)
                if what == 0:
                    return q2[src, :], qs[hi, s, :], qs[lo, s, :]
                if what == 1:
                    return k2[src, :], ka[hi, s, :], ka[lo, s, :]
                v = vraw[:, :, bass.ds(i * P + s * ND, ND)]
                return v, vs[:, s, :, 0:ND], vs[:, s, :, ND:2 * ND]

            @block.scalar
            def _(act):
                def split(i, s, what):
                    if what == 0:
                        at_least(act, ql, 16, i, 15)
                        at_least(act, qkd, N, i, 8 * s + 7 - N)
                    if what == 1:
                        at_least(act, kl, 16, i, 15)
                    if what == 2:
                        at_least(act, pvd, G, i, 4 * s + 3 - G)
                    v, hi, _ = parts(i, s, what)
                    act.copy(hi, v).then_inc(hid_, 1)

                def exps(i, p):
                    at_least(act, nmd, N, i, p)
                    n = 576 if is_mid(p % NJ) else 512
                    b = nm[:, p % 4:p % 4 + 1]
                    pr = prob[:, p % 4, 0:n]
                    act.activation(pr, pr, ACT.Exp, bias=b, accum_out=sums[:, p % N, 0:1]).then_inc(expd, 1)
                    act.activation(prob[:, p % 4, 576:832], S[:, p % 2, 1, 0:256], ACT.Exp, bias=b,
                                   accum_out=sums[:, p % N, 1:2]).then_inc(expd, 1)

                def high(i, p, k):
                    at_least(act, td, 2 * N, i, 2 * p + k)
                    hi, _, hs = pt(p)
                    if k == 0:
                        at_least(act, pvd, G, i, p // 2 - 4)
                        b = first_block(p)
                        act.copy(hi[:, b:b + 4, hs], TB[:, 0, :].rearrange("p (b q) -> p b q", q=P)).then_inc(hid, 1)
                    else:
                        b = ctx_block(p)
                        if is_mid(p % NJ):
                            act.copy(hi[0:64, first_block(p) + 4, hs], TB[0:64, 1, 256:384])
                        act.copy(hi[:, b:b + 2, hs], TB[:, 1, 0:256].rearrange("p (b q) -> p b q", q=P)).then_inc(hid, 1)

                def fold(i, gr):
                    s = (gr % G) // 4
                    at_least(act, pvd, G, i, gr)
                    at_least(act, addd, G, i, gr - 1)
                    act.copy(half[rows(s, False), :], O[rows(s, True), gr % 2, 0:256]).then_inc(halfd, 1)

                def body(i, first, last, tail=False):
                    prev = not first
                    for p in range(TAIL if tail else N):
                        q = p - LAG
                        if live(q, prev, tail):
                            high(i, q, 0)
                        if live(p - 1, prev, tail):
                            exps(i, p - 1)
                        if live(q, prev, tail):
                            high(i, q, 1)
                        if (p - OUT) % 2 == 0 and live((p - OUT) // 2, prev, tail):
                            fold(i, (p - OUT) // 2)
                        if not tail:
                            for a in split_steps(i, first, last, p):
                                split(*a)
                for what in range(3):
                    split(0, 0, what)
                act.wait_ge(zero, 4)
                runs(act, body)
                body(PAIRS, False, True, tail=True)

            @block.vector
            def _(dve):
                for t in (pm_hi, pm_lo):
                    for gq in range(2):
                        last = dve.memset(t[:, gq, :, :].rearrange("p b q -> p (b q)").bitcast(F32), 0.0)
                        last.then_inc(zero, 1)

                def biggest(i, p):
                    s, j = p // NJ, p % NJ
                    r0 = first_row(j)
                    if j == 0:
                        at_least(dve, bmd, 4, i, 2 * s + 1)
                    at_least(dve, qkd, N, i, p)
                    at_least(dve, td, 2 * N, i, 2 * (p - 4) + 1)
                    e = r0 - 2 * j + 7 - (MID_SLOTS[0] if is_mid(j) else END_SLOTS[0])
                    table = bm if is_mid(j) else be
                    sl = p % 4
                    dve.tensor_reduce(mx[:, sl, 2:3], S[:, p % 2, 1, 0:256], AX, ALU.max)
                    pieces = [(0, 512, S[:, p % 2, 0, 0:512], table[:, s, e:e + 8, :].rearrange("p e w -> p (e w)"))]
                    if is_mid(j):
                        pieces.append((512, 64, S[:, p % 2, 1, 256:320], table[:, s, e + 8, :]))
                    for n, (a, w, src, bias) in enumerate(pieces):
                        last = dve.tensor_tensor_reduce(out=prob[:, sl, a:a + w], in0=src, in1=bias, scale=1.0,
                                                        scalar=-3e38, op0=ALU.add, op1=ALU.max,
                                                        accum_out=mx[:, sl, 1 - n:2 - n])
                    last.then_inc(mxd, 1)

                def negmax(i, p):
                    sl = p % 4
                    at_least(dve, mxd, N, i, p)
                    dve.tensor_reduce(nm[:, sl:sl + 1], mx[:, sl, 0 if is_mid(p % NJ) else 1:3], AX, ALU.max,
                                      negate=True).then_inc(nmd, 1)

                def total(i, gr):
                    q = (2 * gr) % N
                    at_least(dve, expd, 2 * N, i, 2 * (2 * gr + 1) + 1)
                    dve.tensor_reduce(tot[:, :], sums[:, q:q + 2, :], AX, ALU.add).then_inc(totd, 1)

                def reciprocal(i, gr):
                    q = (2 * gr) % N
                    at_least(dve, totd, G, i, gr)
                    dve.reciprocal(rec[:, q:q + 2], tot[:, :]).then_inc(recd, 1)

                def low(i, p, k):
                    at_least(dve, hid, 2 * N, i, 2 * p + k)
                    hi, lo, hs = pt(p)
                    if k == 0:
                        b = first_block(p)
                        dve.tensor_tensor(lo[:, b:b + 4, hs], TB[:, 0, :].rearrange("p (b q) -> p b q", q=P),
                                          hi[:, b:b + 4, hs], ALU.subtract).then_inc(lod, 1)
                    else:
                        b = ctx_block(p)
                        if is_mid(p % NJ):
                            f = first_block(p) + 4
                            dve.tensor_tensor(lo[0:64, f, hs], TB[0:64, 1, 256:384], hi[0:64, f, hs], ALU.subtract)
                        dve.tensor_tensor(lo[:, b:b + 2, hs], TB[:, 1, 0:256].rearrange("p (b q) -> p b q", q=P),
                                          hi[:, b:b + 2, hs], ALU.subtract).then_inc(lod, 1)

                def out(i, gr, second):
                    s = (gr % G) // 4
                    r = rows(s, False)
                    a = (gr % 4) * 256
                    if not second:
                        at_least(dve, halfd, G, i, gr)
                        if gr % G == 0:
                            at_least(dve, std, 16, i, -1)
                        dve.tensor_tensor(ost[r, a:a + 256], O[r, gr % 2, 0:256], half[r, :], ALU.add).then_inc(addd, 1)
                        return
                    at_least(dve, addd, G, i, gr)
                    dve.tensor_tensor(ost[r, a:a + 256], ost[r, a:a + 256], O[r, gr % 2, 256:512], ALU.mult).then_inc(od, 1)

                def body(i, first, last, tail=False):
                    prev = not first
                    for p in range(TAIL if tail else N):
                        q = p - LAG
                        gr = (p - OUT) // 2
                        if live(q, prev, tail):
                            low(i, q, 0)
                        if (p - OUT) % 2 and live(gr, prev, tail):
                            out(i, gr, True)
                        if p % 2 == 0 and live((p - 4) // 2, prev, tail):
                            reciprocal(i, (p - 4) // 2)
                        if not tail:
                            biggest(i, p)
                        if live(q, prev, tail):
                            low(i, q, 1)
                        if not tail:
                            negmax(i, p)
                        if (p - OUT) % 2 == 0 and live(gr, prev, tail):
                            out(i, gr, False)
                        if p % 2 == 1 and live((p - 3) // 2, prev, tail):
                            total(i, (p - 3) // 2)
                for what in range(3):
                    dve.wait_ge(hid_, what + 1)
                    v, hi, lo = parts(0, 0, what)
                    dve.tensor_tensor(lo, v, hi, ALU.subtract).then_inc(lod_, 1)
                runs(dve, body)
                body(PAIRS, False, True, tail=True)

            @block.gpsimd
            def _(pool):
                def split(i, s, what):
                    at_least(pool, hid_, SPL, i, 3 * s + what)
                    if what == 1:
                        at_least(pool, swd[s], 32, i, -1)
                    v, hi, lo = parts(i, s, what)
                    pool.tensor_tensor(lo, v, hi, ALU.subtract).then_inc(lod_, 1)

                def mask(i, s):
                    at_least(pool, bl[s], 32, i, 31)
                    a = MID_SLOTS[0] - END_SLOTS[0]
                    pool.tensor_tensor(bm[:, s, :, :], be[:, s, a:a + NM, :], mm9[:, :, :], ALU.add).then_inc(bmd, 1)
                    at_least(pool, bmd, 4, i, 2 * s)
                    pool.tensor_tensor(be[:, s, :, :], be[:, s, :, :],
                                      mc[:, :].unsqueeze(1).broadcast_to([P, NE, GRID_W]), ALU.add).then_inc(bmd, 1)

                def gate(i, gr):
                    r = rows((gr % G) // 4, False)
                    a = (gr % 4) * 256
                    at_least(pool, od, G, i, gr)
                    if gr % G == 0:
                        at_least(pool, gl, 16, i, 15)
                    pool.tensor_tensor(ost[r, a:a + 256], ost[r, a:a + 256], g2[r, a:a + 256], ALU.mult).then_inc(gated, 1)

                def idle(i, splits, masks, gates):
                    at_least(pool, lod_, SPL, i, splits)
                    at_least(pool, bmd, 4, i, masks)
                    at_least(pool, gated, G, i, gates)

                def body(i, first, last, tail=False):
                    splits, masks, gates = 2, 1, -4
                    for p in range(TAIL if tail else N):
                        if (p - OUT) % 2 == 0:
                            if live((p - OUT) // 2, not first, tail):
                                idle(i, splits if not tail else -1, masks if not tail else -1, gates)
                                gate(i, (p - OUT) // 2)
                            gates = (p - OUT) // 2
                        if tail:
                            continue
                        for a in split_steps(i, first, last, p):
                            idle(i, splits, masks, gates)
                            split(*a)
                            splits += 1
                        if p == 2 or p == 12 and not last:
                            idle(i, splits, masks, gates)
                            mask(*((i, 1) if p == 2 else (i + 1, 0)))
                            masks += 2
                pool.wait_ge(ml, 32)
                mask(0, 0)
                runs(pool, body)
                body(PAIRS, False, True, tail=True)



def finish(c, io, consts, xt):
    nc = c.nc
    LT = NLAT // P
    with c.scope(AREA_H):
        fg = c.sb("final_gain", [P, D])
        xo, sq = c.sb("x_out", [P, 2, D]), c.sb("x_sq", [P, D])
        ss, rt, rc = c.sb("ss", [P, LT]), c.sb("rt", [P, LT]), c.sb("rc", [P, LT])
        ps = c.ps("fps", [P, 2, 2, 512])
        fgl, td, sd, rd, rcd, fd = (c.sem(x) for x in (
            "fg_in", "f_turned", "f_squared", "f_root", "f_recip", "f_done"))
        st = [c.sem(f"f_stored{s}") for s in range(2)]
        with c.block() as block:
            @block.sync
            def _(sp):
                sp.dma_start(fg[:, :], io["final_g"].rearrange("(a d) -> a d", a=1).broadcast_to([P, D])).then_inc(fgl, 16)
                for t in range(LT):
                    sp.wait_ge(fd, t + 1)
                    sp.dma_start(io["out"][0, t * P:(t + 1) * P, :], xo[:, t % 2, :]).then_inc(st[t % 2], 16)
                for s in range(2):
                    sp.wait_ge(st[s], 16 * LT // 2)

            @block.tensor
            def _(pe):
                for t in range(LT):
                    if t >= 2:
                        pe.wait_ge(fd, t - 1)
                    for k in range(KT):
                        last = pe.transpose(ps[:, t % 2, k // 4, (k % 4) * P:(k % 4 + 1) * P],
                                            xt[:, k, NCTX + t * P:NCTX + (t + 1) * P], consts["ident"][:, :])
                    last.then_inc(td, 1)

            @block.scalar
            def _(act):
                for t in range(LT):
                    act.wait_ge(td, t + 1)
                    if t:
                        act.wait_ge(sd, t)
                    act.activation(sq[:, :], ps[:, t % 2, :, :].rearrange("p a n -> p (a n)"), ACT.Square,
                                   accum_out=ss[:, t:t + 1]).then_inc(sd, 1)
                    act.wait_ge(sd, t + 1)
                    act.activation(rt[:, t:t + 1], ss[:, t:t + 1], ACT.Sqrt, bias=consts["eps"][:, :],
                                   scale=1.0 / D).then_inc(rd, 1)

            @block.vector
            def _(dve):
                dve.wait_ge(fgl, 16)
                for t in range(LT):
                    dve.wait_ge(rd, t + 1)
                    dve.reciprocal(rc[:, t:t + 1], rt[:, t:t + 1]).then_inc(rcd, 1)
                    dve.wait_ge(rcd, t + 1)
                    if t >= 2:
                        dve.wait_ge(st[t % 2], 16 * (t // 2))
                    dve.scalar_tensor_tensor(out=xo[:, t % 2, :], in0=ps[:, t % 2, :, :].rearrange("p a n -> p (a n)"),
                                             scalar=rc[:, t:t + 1], in1=fg[:, :], op0=ALU.mult,
                                             op1=ALU.mult).then_inc(fd, 1)



def backbone(nc, io, stop=None):
    with ExitStack() as stack:
        c = Core(nc, stack)
        with c.scope(AREA_CONST):
            consts = {"ident": c.sb("ident", [P, P]), "ones": c.sb("ones", [P, 1]), "eps": c.sb("eps", [P, 1]),
                      "silu_cols": c.sb("silu_cols", [P, 16])}
            mod, cols = c.sb("mod", [P, 2, 24, 2]), c.sb("cols", [P, 66])

        def scratch(name, shape):
            return nc.dram_tensor(name, shape, F32).ap()
        io["xt"] = scratch("xt_scratch", [P, KT, T])
        io["skew"] = scratch("bias_scratch", [NH, GRID_W, BIAS_ROWS, SKEW_W])
        io["gd"] = scratch("gate_scratch", [KT, P, T])
        io["qd"] = scratch("q_scratch", [KT, P, NLAT])
        io["kd"] = scratch("k_scratch", [KT, P, T])
        io["od"] = scratch("o_scratch", [KT, P, NLAT])

        with c.scope(AREA_H):
            hi, lo = c.sb("h_hi", [P, KT, T], F32R), c.sb("h_lo", [P, KT, T], F32R)
        with c.scope(AREA_X):
            xt = c.sb("xt", [P, KT, T])
        with c.scope(AREA_X):
            vraw = c.sb("v_raw", [P, TT, D])
        with c.scope(AREA_QKV):
            qk = c.sb("qk", [P, QH + KVH, T])
            vhi, vlo = c.sb("v_hi0", [P, TT, 256], F32R), c.sb("v_lo0", [P, TT, 256], F32R)
            khi, klo = c.sb("k_hi0", [P, KVH, T], F32R), c.sb("k_lo0", [P, KVH, T], F32R)
        with c.scope(AREA_W):
            wbuf = c.sb("w_raw", [P, KT, 256]), c.sb("w_hi", [P, KT, 256], F32R), c.sb("w_lo", [P, KT, 256], F32R)

        with c.scope(AREA_SQUARES):
            squares = c.sb("x1_squares", [P, 2, T]), c.sb("x1_squares_sum", [P, T])
        with c.scope(AREA_MID):
            wbuf2 = c.sb("w_raw2", [P, KT, 256]), c.sb("w_hi2", [P, KT, 256], F32R), c.sb("w_lo2", [P, KT, 256], F32R)

        qw, kw = QH * HD, KVH * HD
        ga, na, ga_out, na_out = io["ga_w_in"], io["na_w_in"], io["ga_w_out"], io["na_w_out"]

        def project_to(tag, w, col0, pairs, chunks, **more):
            return project(c, tag, w, col0, pairs, hi, lo, wbuf, chunks, **more)

        def start():
            prologue(c, io, consts, xt, hi, lo, mod, cols, FirstWeights(c, "q0", ga, 0, wbuf))

        v0, g0 = (ga, qw + kw), (ga, qw + 2 * kw)
        steps = [
            start,
            lambda: project_to("q0", ga, 0, (QH + KVH) // 2, ALL_CHUNKS, func=ACT.Copy, dest=qk, ahead=v0),
            lambda: project_values(c, "v0", *v0, 1, hi, lo, [wbuf], g0, split=(vhi, vlo)),
            lambda: project_to("g0", *g0, KT // 2, ALL_CHUNKS, func=ACT.Silu, dram=io["gd"]),
            lambda: norm_and_rotate(c, io, consts, mod, cols, qk, khi, klo),
            lambda: grouped_attention(c, io, consts, qk, khi, klo, vhi, vlo),
            lambda: project_to("o0", ga_out, 0, KT // 2, ALL_CHUNKS, residual=(mod[:, 0], io["xt"], xt),
                               raw_h=(qk, None), squares=squares, ahead=(na, 0)),
            lambda: project_to("q1", na, 0, KT // 2, LAT_CHUNKS, func=ACT.Copy, scale=ND ** -0.5,
                               dram=io["qd"], ahead=(na, D), norm=(1, xt, mod, squares[1], consts, io["xt"])),
            lambda: project_to("k1", na, D, KT // 2, ALL_CHUNKS, func=ACT.Copy, dram=io["kd"], ahead=(na, 2 * D)),
            lambda: project_values(c, "v1", na, 2 * D, D // 256, hi, lo, [wbuf, wbuf2], (na, 3 * D), dest=vraw),
            lambda: project_to("g1", na, 3 * D, KT // 2, LAT_CHUNKS, func=ACT.Silu, dram=io["gd"]),
            lambda: neighbourhood_attention(c, io, consts, vraw),
            lambda: project_to("o1", na_out, 0, KT // 2, LAT_CHUNKS, residual=(mod[:, 1], io["xt"], xt),
                               raw_h=(None, io["od"])),
            lambda: finish(c, io, consts, xt),
        ]
        for step in steps[:stop]:
            step()


_INS = ['x', 'c', 'ctx', 'c_ctx', 'mod_w', 'mod_b', 'norm_g', 'final_g', 'ga_w_in', 'ga_q_g', 'ga_k_g', 'ga_w_out',
        'na_w_in', 'na_w_out']


def kernel(**inputs):
    import numpy as _np
    import concourse.bacc as _bacc
    from concourse import mybir as _mybir
    from concourse.bass_utils import run_bass_kernel_spmd as _run

    nc = _bacc.Bacc("TRN2", target_bir_lowering=False, num_devices=1)
    cos, sin = rope_tables()
    mask_cols, mask_mid = window_masks()
    arrays = {n: _np.ascontiguousarray(inputs[n]) for n in _INS}
    wide = GRID_W - KW
    arrays["bias"] = _np.pad(_np.asarray(inputs["na_rpb"])[0], ((0, 0), (0, 0), (wide, wide)))
    arrays |= {"cos": cos, "sin": sin, "mask_cols": mask_cols, "mask_mid": mask_mid}
    io, in_map = {}, {}
    for name, a in arrays.items():
        if name.startswith(("ga_w", "na_w")):
            a = a[0]
        in_map[f"in_{name}"] = a
        io[name] = nc.dram_tensor(f"in_{name}", a.shape, _mybir.dt.from_np(a.dtype), kind="ExternalInput").ap()
    io["out"] = nc.dram_tensor("out", (1, NLAT, D), F32, kind="ExternalOutput").ap()
    backbone(nc, io)
    r = _run(nc, [in_map], core_ids=[0])
    return r.results[0]["out"]
```
